# Optimizing a Trainium2 kernel written in Bass

```python
import jax, jax.numpy as jnp
from jax import lax
import numpy as np

D_MODEL = 1024
BATCH = 1
SEQ = 1024
DEPTH = 1

CHUNK = 64
EPS = 1e-6
MLA_HEADS = 8
Q_RANK = 256
KV_RANK = 128
QK_NOPE = 64
QK_ROPE = 32
V_HEAD = 64
MLA_WIDTH = MLA_HEADS * V_HEAD
ROPE_THETA = 10000.0
Q_BLOCK = 128
SGU_GROUPS = 8
SGU_GROUP_DIM = 64
SGU_WIDTH = SGU_GROUPS * SGU_GROUP_DIM
SGU_LEN = 128
N_BRANCH = 2
N_GROUPS = 4
EXPERTS_PER_GROUP = 8
N_EXPERTS = N_GROUPS * EXPERTS_PER_GROUP
TOP_K = 2
D_EXPERT = 256
MOE_BLOCK = 128
SPLIT_POINTS = [Q_RANK, Q_RANK + KV_RANK, Q_RANK + KV_RANK + QK_ROPE,
                Q_RANK + KV_RANK + QK_ROPE + 2 * SGU_WIDTH]
IN_COLS = Q_RANK + KV_RANK + QK_ROPE + 2 * SGU_WIDTH + N_BRANCH * D_MODEL

kernel_name = "hybrid_mla_gmlp_hiermoe_block"

def _rmsnorm(x, g):
    xf = x.astype(jnp.float32)
    y = xf * lax.rsqrt(jnp.mean(xf * xf, axis=-1, keepdims=True) + EPS)
    return (y * g.astype(jnp.float32)).astype(x.dtype)

def _layernorm(x, g, b):
    xf = x.astype(jnp.float32)
    mu = jnp.mean(xf, axis=-1, keepdims=True)
    var = jnp.mean(jnp.square(xf - mu), axis=-1, keepdims=True)
    y = (xf - mu) * lax.rsqrt(var + EPS)
    return (y * g.astype(jnp.float32) + b.astype(jnp.float32)).astype(x.dtype)

def _rope(x, positions):
    r = x.shape[-1]
    freqs = ROPE_THETA ** (-jnp.arange(0, r, 2, dtype=jnp.float32) / r)
    ang = positions.astype(jnp.float32)[..., None] * freqs
    cos = jnp.cos(ang)[:, :, None, :]
    sin = jnp.sin(ang)[:, :, None, :]
    xf = x.astype(jnp.float32)
    x1, x2 = xf[..., : r // 2], xf[..., r // 2:]
    out = jnp.concatenate([x1 * cos - x2 * sin, x1 * sin + x2 * cos], axis=-1)
    return out.astype(x.dtype)

def _mla(c_q, c_kv, k_r, positions, g_cq, w_uq, g_ckv, w_uk, w_uv):
    b, s, _ = c_q.shape
    c_q = _rmsnorm(c_q, g_cq)
    q = (c_q @ w_uq).reshape(b, s, MLA_HEADS, QK_NOPE + QK_ROPE)
    q_nope = q[..., :QK_NOPE]
    q_rope = _rope(q[..., QK_NOPE:], positions)
    c_kv = _rmsnorm(c_kv, g_ckv)
    k_nope = (c_kv @ w_uk).reshape(b, s, MLA_HEADS, QK_NOPE)
    v = (c_kv @ w_uv).reshape(b, s, MLA_HEADS, V_HEAD)
    k_rope = _rope(k_r[:, :, None, :], positions)[:, :, 0, :]
    scale = (QK_NOPE + QK_ROPE) ** -0.5
    n_blk = s // Q_BLOCK
    qn_b = q_nope.reshape(b, n_blk, Q_BLOCK, MLA_HEADS, QK_NOPE).transpose(1, 0, 2, 3, 4)
    qr_b = q_rope.reshape(b, n_blk, Q_BLOCK, MLA_HEADS, QK_ROPE).transpose(1, 0, 2, 3, 4)
    key_chunk = jnp.arange(s) // CHUNK
    neg = jnp.finfo(jnp.float32).min

    def q_block(args):
        qn_i, qr_i, i = args
        sc = (jnp.einsum('bqhd,bkhd->bhqk', qn_i, k_nope)
              + jnp.einsum('bqhr,bkr->bhqk', qr_i, k_rope)).astype(jnp.float32) * scale
        q_chunk = (i * Q_BLOCK + jnp.arange(Q_BLOCK)) // CHUNK
        mask = key_chunk[None, :] <= q_chunk[:, None]
        sc = jnp.where(mask[None, None], sc, neg)
        p = jax.nn.softmax(sc, axis=-1).astype(v.dtype)
        return jnp.einsum('bhqk,bkhd->bqhd', p, v)

    o = lax.map(q_block, (qn_b, qr_b, jnp.arange(n_blk)))
    return o.transpose(1, 0, 2, 3, 4).reshape(b, s, MLA_WIDTH)

def _sgu(u, v, sgu_gain, sgu_bias, w_spatial, b_spatial):
    b, s, _ = v.shape
    v = _layernorm(v, sgu_gain, sgu_bias)
    v = v.reshape(b, s // SGU_LEN, SGU_LEN, SGU_GROUPS, SGU_GROUP_DIM)
    idx = jnp.arange(SGU_LEN) // CHUNK
    mask = idx[:, None] >= idx[None, :]
    w = jnp.where(mask[None], w_spatial, jnp.zeros_like(w_spatial))
    sv = jnp.einsum('gij,bnjgc->bnigc', w, v) + b_spatial.T[None, None, :, :, None]
    return u * sv.reshape(b, s, SGU_WIDTH)

def _hier_moe(h, w_rg, b_rg, w_re, b_re, w_eg, w_eu, w_ed):
    b, s, d = h.shape
    n = b * s
    xf = h.reshape(n, d)
    p_group = jax.nn.softmax((xf @ w_rg + b_rg).astype(jnp.float32), axis=-1)
    p_top, g_idx = lax.top_k(p_group, 1)
    le = (jnp.einsum('nd,gde->nge', xf, w_re) + b_re[None]).astype(jnp.float32)
    le_sel = jnp.take_along_axis(le, g_idx[:, :, None], axis=1)[:, 0, :]
    top_l, e_loc = lax.top_k(le_sel, TOP_K)
    gate = (jax.nn.softmax(top_l, axis=-1) * p_top).astype(h.dtype)
    e_glob = g_idx * EXPERTS_PER_GROUP + e_loc
    a = n * TOP_K
    e_flat = e_glob.reshape(a)
    tok_flat = jnp.repeat(jnp.arange(n, dtype=jnp.int32), TOP_K)
    w_flat = gate.reshape(a)
    order = jnp.argsort(e_flat)
    e_sorted = e_flat[order]
    tok_sorted = tok_flat[order]
    w_sorted = w_flat[order]
    counts = jnp.zeros((N_EXPERTS,), jnp.int32).at[e_flat].add(1)
    starts = jnp.cumsum(counts) - counts
    pcounts = (counts + MOE_BLOCK - 1) // MOE_BLOCK * MOE_BLOCK
    pends = jnp.cumsum(pcounts)
    pstarts = pends - pcounts
    rank = jnp.arange(a, dtype=jnp.int32) - starts[e_sorted]
    dest = pstarts[e_sorted] + rank
    p_rows = a + N_EXPERTS * MOE_BLOCK
    buf_tok = jnp.zeros((p_rows,), jnp.int32).at[dest].set(tok_sorted)
    buf_w = jnp.zeros((p_rows,), h.dtype).at[dest].set(w_sorted)
    n_blk = p_rows // MOE_BLOCK
    blk_e = jnp.clip(jnp.searchsorted(pends, jnp.arange(n_blk, dtype=jnp.int32) * MOE_BLOCK,
                                      side='right'), 0, N_EXPERTS - 1)
    xs = xf[buf_tok].reshape(n_blk, MOE_BLOCK, d)

    def expert_block(args):
        xb, e = args
        hid = jax.nn.silu(xb @ w_eg[e]) * (xb @ w_eu[e])
        return hid @ w_ed[e]

    ys = lax.map(expert_block, (xs, blk_e)).reshape(p_rows, d)
    out = jnp.zeros((n, d), h.dtype).at[buf_tok].add(ys * buf_w[:, None])
    return out.reshape(b, s, d)

def setup_inputs(seed: int = 0) -> dict:
    key = jax.random.key(seed)
    ks = jax.random.split(key, 26)
    f32 = jnp.float32

    def nrm(k, shape, fan_in):
        return jax.random.normal(k, shape, f32) * (fan_in ** -0.5)

    def gain(k, shape):
        return 1.0 + 0.02 * jax.random.normal(k, shape, f32)

    L = DEPTH
    x = jax.random.normal(ks[0], (BATCH, SEQ, D_MODEL), f32)
    offset = jax.random.randint(ks[1], (BATCH, 1), 0, 1024, dtype=jnp.int32)
    positions = offset + jnp.arange(SEQ, dtype=jnp.int32)[None, :]
    return {
        "x": x,
        "positions": positions,
        "g_attn_norm": gain(ks[2], (L, D_MODEL)),
        "w_in": nrm(ks[3], (L, D_MODEL, IN_COLS), D_MODEL),
        "g_cq": gain(ks[4], (L, Q_RANK)),
        "w_uq": nrm(ks[5], (L, Q_RANK, MLA_HEADS * (QK_NOPE + QK_ROPE)), Q_RANK),
        "g_ckv": gain(ks[6], (L, KV_RANK)),
        "w_uk": nrm(ks[7], (L, KV_RANK, MLA_HEADS * QK_NOPE), KV_RANK),
        "w_uv": nrm(ks[8], (L, KV_RANK, MLA_WIDTH), KV_RANK),
        "w_o_attn": nrm(ks[9], (L, MLA_WIDTH, D_MODEL), MLA_WIDTH),
        "sgu_gain": gain(ks[10], (L, SGU_WIDTH)),
        "sgu_bias": 0.02 * jax.random.normal(ks[11], (L, SGU_WIDTH), f32),
        "w_spatial": nrm(ks[12], (L, SGU_GROUPS, SGU_LEN, SGU_LEN), SGU_LEN),
        "b_spatial": gain(ks[13], (L, SGU_GROUPS, SGU_LEN)),
        "w_o_sgu": nrm(ks[14], (L, SGU_WIDTH, D_MODEL), SGU_WIDTH),
        "w_out": nrm(ks[15], (L, D_MODEL, D_MODEL), D_MODEL),
        "g_ffn_norm": gain(ks[16], (L, D_MODEL)),
        "w_router_group": nrm(ks[17], (L, D_MODEL, N_GROUPS), D_MODEL),
        "b_router_group": 0.01 * jax.random.normal(ks[18], (L, N_GROUPS), f32),
        "w_router_expert": nrm(ks[19], (L, N_GROUPS, D_MODEL, EXPERTS_PER_GROUP), D_MODEL),
        "b_router_expert": 0.01 * jax.random.normal(ks[20], (L, N_GROUPS, EXPERTS_PER_GROUP), f32),
        "w_exp_gate": nrm(ks[21], (L, N_EXPERTS, D_MODEL, D_EXPERT), D_MODEL),
        "w_exp_up": nrm(ks[22], (L, N_EXPERTS, D_MODEL, D_EXPERT), D_MODEL),
        "w_exp_down": nrm(ks[23], (L, N_EXPERTS, D_EXPERT, D_MODEL), D_EXPERT),
        "g_final": gain(ks[24], (D_MODEL,)),
    }

def reference(x, positions, g_attn_norm, w_in, g_cq, w_uq, g_ckv, w_uk, w_uv, w_o_attn,
              sgu_gain, sgu_bias, w_spatial, b_spatial, w_o_sgu, w_out, g_ffn_norm,
              w_router_group, b_router_group, w_router_expert, b_router_expert,
              w_exp_gate, w_exp_up, w_exp_down, g_final):
    for l in range(DEPTH):
        h = _rmsnorm(x, g_attn_norm[l])
        z = h @ w_in[l]
        c_q, c_kv, k_r, uv, gate_logits = jnp.split(z, SPLIT_POINTS, axis=-1)
        attn = _mla(c_q, c_kv, k_r, positions, g_cq[l], w_uq[l], g_ckv[l], w_uk[l], w_uv[l])
        attn = attn @ w_o_attn[l]
        uv = jax.nn.gelu(uv)
        u, v = uv[..., :SGU_WIDTH], uv[..., SGU_WIDTH:]
        sgu = _sgu(u, v, sgu_gain[l], sgu_bias[l], w_spatial[l], b_spatial[l]) @ w_o_sgu[l]
        gates = jax.nn.sigmoid(gate_logits.astype(jnp.float32)).astype(x.dtype)
        g_a, g_b = gates[..., :D_MODEL], gates[..., D_MODEL:]
        x = x + (g_a * attn + g_b * sgu) @ w_out[l]
        x = x + _hier_moe(_rmsnorm(x, g_ffn_norm[l]), w_router_group[l], b_router_group[l],
                          w_router_expert[l], b_router_expert[l],
                          w_exp_gate[l], w_exp_up[l], w_exp_down[l])
    return _rmsnorm(x, g_final)


_drawn_inputs = setup_inputs


def setup_inputs(seed=0):
    import zlib

    import numpy as np

    out = dict(_drawn_inputs(seed))
    spreads = {}
    factors = {'g_cq': 8.0,
     'g_ckv': 7.237,
     'sgu_gain': 30.464,
     'sgu_bias': 33.69,
     'b_spatial': 26.426,
     'b_router_group': 29.527,
     'b_router_expert': 27.876,
     'g_final': 8.115,
     'g_ffn_norm': 7.461}
    for name, (base, spread) in spreads.items():
        noise = np.random.default_rng([zlib.crc32(name.encode()), seed]).standard_normal(out[name].shape)
        drawn = base * np.exp(spread * noise) if base else spread * noise
        out[name] = __import__('jax').numpy.asarray(drawn.astype(out[name].dtype))
    for name, factor in factors.items():
        out[name] = (out[name] * factor).astype(out[name].dtype)
    return out
```

```python
from contextlib import ExitStack

import numpy as np

import concourse.bass as bass
from concourse import mybir

F32 = mybir.dt.float32
F32R = mybir.dt.float32r
BF16 = mybir.dt.bfloat16
I32 = mybir.dt.int32
U32 = mybir.dt.uint32
ALU = mybir.AluOpType
ACT = mybir.ActivationFunctionType
AX = mybir.AxisListType.X

P = 128
D = 1024
T = 1024
NT = T // P
KD = D // P
HALF = 512
EPS = 1e-6
HEADS, NOPE, ROPE, VH = 8, 64, 32, 64
QR, KVR = 256, 128
SCALE = (NOPE + ROPE) ** -0.5
THETA = 10000.0
SGU = 512
KS = SGU // P
CHUNK = 64
G, EPG = 4, 8
NE = G * EPG
DE = 256
NOVF = 15
NBLK = 48
NR = G + NE
C_UV, C_GATE = QR + KVR + ROPE, QR + KVR + ROPE + 2 * SGU
BIG = 1.0e30
FAR = 8192.0
PI_IN = 3.1415925
TWO_PI = 2 * np.pi
C1 = 6.28125
C2 = float(np.float32(np.floor((TWO_PI - C1) * 2 ** 21) / 2 ** 21))
C3 = float(TWO_PI - C1 - C2)
MAGIC = 1.5 * 2 ** 23
KB = 1024
NQ = 64


def rope_constants():
    f = (np.float32(THETA) ** (-np.arange(0, ROPE, 2, dtype=np.float32) / np.float32(ROPE))).astype(np.float32)
    turn = np.concatenate([-f, f])
    c = np.zeros((P, 8), np.float32)
    c[:64, 1], c[:64, 2] = 0.25, np.pi / 2
    c[64:96, 0], c[64:96, 1], c[64:96, 2] = np.concatenate([f, f]), 0.25, np.pi / 2
    c[96:, 0] = turn
    c[:64, 3] = np.concatenate([turn, turn])
    c[64:, 3], c[64:, 4], c[64:, 5] = np.concatenate([f] * 4), 0.25, np.pi / 2
    return c


def chunks_through(s):
    return sum((i % NT) // 4 + 1 for i in range(s + 1))


def build(nc, a, out, stop_after=None):
    base = 16512

    with ExitStack() as ctx:
        def at(name, kb, shape, dt):
            return nc.alloc_sbuf_tensor_at(name, shape, dt, offset=base + int(kb * KB))

        sems = {}

        def sem(name):
            if name not in sems:
                sems[name] = ctx.enter_context(nc.semaphore(name))
            return sems[name]

        ident = at("ident", 0, [P, P], F32)
        iota_row = at("iota_row", 0.5, [P, P], F32)
        ones = at("ones", 1, [P, P], F32)
        mask_l = at("mask_l", 1.5, [P, P], F32R)
        mask_r = at("mask_r", 2, [P, CHUNK], F32R)
        before = at("before", 2.25, [P, P], BF16)
        ones_b = at("ones_b", 2.5, [P, P], BF16)
        iota_col = at("iota_col", 2.75, [P, 1], F32)
        epst = at("epst", 2.78125, [P, 1], F32)
        cst = at("cst", 2.8125, [P, 8], F32)
        gcol = at("gcol", 2.875, [P, 3], F32)
        ssq = at("ssq", 3, [P, 3 * NT], F32)
        std = at("std", 3.125, [P, 3 * NT], F32)
        rstd = at("rstd", 3.25, [P, 3 * NT], F32)
        negm = at("negm", 3.5, [P, NQ], F32)
        lsum = at("lsum", 3.75, [P, NQ], F32)
        rl = at("rl", 4, [P, NQ], F32)
        bnst = at("bnst", 4.25, [P, NT, 6], F32)
        bnag = at("bnag", 4.5, [P, NT, 2], F32)
        gatew = at("gatew", 4.75, [P, 2, NT], F32)
        yidx = at("yidx", 5, [P, NBLK], U32)
        xidx = at("xidx", 5.25, [P, NBLK], U32)
        xcol = [at(f"xcol{i}", 5.75 + i / 32, [P, 1], U32) for i in range(2)]
        ycol = [at(f"ycol{i}", 5.8125 + i / 32, [P, 1], U32) for i in range(2)]
        ovf_e = at("ovf_e", 5.5, [1, 16], I32)
        ovf_n = at("ovf_n", 5.625, [1, 8], I32)

        raw = [at(f"raw{i}", 8 + 4 * i, [P, KD, P], F32) for i in range(3)]
        w_hi = [at(f"w_hi{i}", 20 + 8 * i, [P, KD, P], F32R) for i in range(3)]
        w_lo = [at(f"w_lo{i}", 24 + 8 * i, [P, KD, P], F32R) for i in range(3)]
        ht_hi = at("ht_hi", 44, [P, KD, T], F32R)
        ht_lo = at("ht_lo", 76, [P, KD, T], F32R)
        xin = [at(f"xin{i}", 108 + 4 * i, [P, D], F32) for i in range(4)]
        hrow = [at(f"hrow{i}", 124 + 4 * i, [P, D], F32) for i in range(2)]
        g_attn = at("g_attn", 176, [P, D], F32)
        junk = at("junk", 180, [P, D], F32)
        pos_i = at("pos_i", 200, [P, T], I32)
        ang = at("ang", 160, [P, T], F32)
        turns = at("turns", 164, [P, T], F32)
        tab_q = at("tab_q", 132, [P, T], F32)
        tab_k = at("tab_k", 168, [P, T], F32)
        c_raw = at("c_raw", 136, [P, 3, T], F32)
        c_sq = at("c_sq", 148, [P, 3, T], F32)
        c_rs = at("c_rs", 160, [P, 4, HALF], F32)
        kr1 = at("kr1", 192, [P, T], F32)
        kr2 = at("kr2", 196, [P, T], F32)
        c_hi = at("c_hi", 108, [P, 3, T], F32R)
        c_lo = at("c_lo", 120, [P, 3, T], F32R)
        h_raw = [at(f"h_raw{i}", 8 + 1.5 * i, [P, 384], F32) for i in range(2)]
        h_hi = [at(f"h_hi{i}", 11 + 3 * i, [P, 384], F32R) for i in range(2)]
        h_lo = [at(f"h_lo{i}", 12.5 + 3 * i, [P, 384], F32R) for i in range(2)]
        pt_hi = [at(f"pt_hi{i}", 17 + 4 * i, [P, 4, P], F32R) for i in range(4)]
        pt_lo = [at(f"pt_lo{i}", 19 + 4 * i, [P, 4, P], F32R) for i in range(4)]
        q_tmp = [at(f"q_tmp{i}", 33 + 2 * i, [P, HALF], F32) for i in range(2)]
        q_hi = [at(f"q_hi{i}", 136 + 8 * i, [P, T], F32R) for i in range(2)]
        q_lo = [at(f"q_lo{i}", 140 + 8 * i, [P, T], F32R) for i in range(2)]
        v_hi = [at(f"v_hi{i}", 152 + 4 * i, [P, NT, VH], F32R) for i in range(2)]
        v_lo = [at(f"v_lo{i}", 154 + 4 * i, [P, NT, VH], F32R) for i in range(2)]
        o_tok = at("o_tok", 160, [P, NT, HEADS * VH], F32)
        k_hi = [at(f"k_hi{i}", 176 + 8 * i, [P, T], F32R) for i in range(2)]
        k_lo = [at(f"k_lo{i}", 180 + 8 * i, [P, T], F32R) for i in range(2)]
        prob = [at(f"prob{i}", 192 + 4 * i, [P, T], F32) for i in range(2)]
        ot_hi = at("ot_hi", 108, [P, KS, T], F32R)
        ot_lo = at("ot_lo", 124, [P, KS, T], F32R)
        st_hi = at("st_hi", 140, [P, KS, T], F32R)
        st_lo = at("st_lo", 156, [P, KS, T], F32R)
        u_t = at("u_t", 172, [P, KS, T], F32)
        v_t = at("v_t", 188, [P, KS, T], F32)
        sp_hi = at("sp_hi", 8, [P, 8, P], F32R)
        sp_lo = at("sp_lo", 12, [P, 8, P], F32R)
        sp_raw = at("sp_raw", 16, [P, 8, P], F32)
        ln_g = at("ln_g", 20, [P, SGU], F32)
        ln_b = at("ln_b", 22, [P, SGU], F32)
        vn_hi = [at(f"vn_hi{i}", 24 + 4 * i, [P, SGU], F32R) for i in range(2)]
        vn_lo = [at(f"vn_lo{i}", 26 + 4 * i, [P, SGU], F32R) for i in range(2)]
        ln_t = [at(f"ln_t{i}", 32 + 2 * i, [P, SGU], F32) for i in range(2)]
        s_t = [at(f"s_t{i}", 36 + 2 * i, [P, KS, P], F32) for i in range(2)]
        sp_b = at("sp_b", 40, [P, KS, P], F32)
        mix = at("mix", 172, [P, KD, T], F32)
        sig_b = [at("sig_b0", 204, [P, HALF], F32), at("sig_b1", 6, [P, HALF], F32)]
        wo_hi = at("wo_hi", 44, [P, KD, D], F32R)
        wo_lo = at("wo_lo", 76, [P, KD, D], F32R)
        mt_hi = [at(f"mt_hi{i}", 108 + 8 * i, [P, KD, P], F32R) for i in range(2)]
        mt_lo = [at(f"mt_lo{i}", 112 + 8 * i, [P, KD, P], F32R) for i in range(2)]
        xre = [at(f"xre{i}", 124 + 4 * i, [P, D], F32) for i in range(2)]
        x2 = at("x2", 132, [P, NT, D], F32)
        h2 = [at(f"h2{i}", 164 + 4 * i, [P, D], F32) for i in range(2)]
        h2t = [at(f"h2t{i}", 20 + 4 * i, [P, KD, P], F32) for i in range(2)]
        g_ffn = at("g_ffn", 28, [P, D], F32)
        w_rt = at("w_rt", 32, [P, KD, NR], F32)
        b_rt = at("b_rt", 33.25, [P, NR], F32)
        junk2 = at("junk2", 34, [P, D], F32)
        r_at = [172.0]

        def scratch(name, shape, dt=F32):
            n = int(np.prod(shape[1:])) * (2 if dt is BF16 else 4)
            t = at(name, r_at[0], shape, dt)
            r_at[0] += -(-n // 32) * 32 / KB
            return t

        logit = at("logit", 38.5, [P, NT, NR], F32)
        iog = scratch("iog", [P, NT, EPG])
        mg = scratch("mg", [P, NT])
        cand = scratch("cand", [P, NT, EPG])
        sel = scratch("sel", [P, NT])
        og = scratch("og", [P, NT, G])
        ex = scratch("ex", [P, NT, G])
        ptop = scratch("ptop", [P, NT])
        lprod = scratch("lprod", [P, NT, G, EPG])
        le = scratch("le", [P, NT, EPG])
        m12 = scratch("m12", [P, 2, NT])
        oh = [scratch(f"oh{k}", [P, NT, EPG]) for k in range(2)]
        oe = [scratch(f"oe{k}", [P, NT, G, EPG]) for k in range(2)]
        oe_b = scratch("oe_b", [P, NT, NE], BF16)
        cum_b = scratch("cum_b", [P, NT + 1, NE], BF16)
        cum = scratch("cum", [P, NT, NE])
        rank_e = scratch("rank_e", [P, NT, NE])
        prod = scratch("prod", [P, NT, NE])
        cnt = scratch("cnt", [P, NE])
        cmp7 = scratch("cmp7", [P, NE])
        novf = scratch("novf", [P, NE])
        incl = scratch("incl", [P, NE])
        ostart = scratch("ostart", [P, NE])
        rk = scratch("rk", [P, 2, NT])
        eid = scratch("eid", [P, 2, NT])
        osk = scratch("osk", [P, 2, NT])
        ob = scratch("ob", [P, 2, NT])
        obc = scratch("obc", [P, 2, NT])
        blk_k = scratch("blk_k", [P, 2, NT])
        val = scratch("val", [P, 2, NT])
        sel_a = [scratch(f"sel_a{i}", [P, P], F32R) for i in range(2)]
        sel_b = [scratch(f"sel_b{i}", [P, NBLK], F32R) for i in range(2)]
        tabf = scratch("tabf", [P, NBLK])
        tab0 = scratch("tab0", [P, NBLK])
        ovc = scratch("ovc", [1, 16, NE])
        ovf = scratch("ovf", [1, 16])
        assert r_at[0] < 207
        w_gu = [at(f"w_gu{i}", 8 + 24 * i, [P, 2, KD, DE], F32) for i in range(4)]
        w_dn = [at(f"w_dn{i}", 24 + 24 * i, [P, 2, D], F32) for i in range(4)]
        xs = [at(f"xs{i}", 108 + 4 * i, [P, D], F32) for i in range(2)]
        xst = [at(f"xst{i}", 116 + 4 * i, [P, KD, P], F32) for i in range(2)]
        sg = [at(f"sg{i}", 124 + i, [P, DE], F32) for i in range(2)]
        hid = [at(f"hid{i}", 126 + i, [P, DE], F32) for i in range(2)]
        hidt = [at(f"hidt{i}", 128 + i, [P, 2, P], F32) for i in range(2)]
        y = [at(f"y{i}", 164 + 4 * i, [P, D], F32) for i in range(2)]
        yin = [at(f"yin{i}", 8 + 8 * i, [P, 2, D], F32) for i in range(2)]
        g_fin = at("g_fin", 104, [P, D], F32)
        acc = [at(f"acc{i}", 24 + 4 * i, [P, D], F32) for i in range(2)]
        res = [at(f"res{i}", 32 + 4 * i, [P, D], F32) for i in range(2)]
        junk3 = at("junk3", 40, [P, D], F32)

        ps = ctx.enter_context(nc.psum_tensor("ps", [P, 8, HALF], F32))

        h2_dram = nc.dram_tensor("h2_dram", [T, D], F32, kind="Internal").ap()
        y_dram = nc.dram_tensor("y_dram", [2 * T, D], F32, kind="Internal").ap()

        ctx.enter_context(nc.allow_non_contiguous_dma(reason="small columns and weight slices"))
        block = ctx.enter_context(nc.Block())

        w_in = a["w_in"][0].rearrange("(k p) n -> p k n", p=P)
        w_oa = a["w_o_attn"][0].rearrange("(k p) n -> p k n", p=P)
        w_os = a["w_o_sgu"][0].rearrange("(k p) n -> p k n", p=P)
        w_out = a["w_out"][0].rearrange("(k p) n -> p k n", p=P)
        w_uq = a["w_uq"][0].rearrange("(k p) n -> p k n", p=P)
        x_d = a["x"][0].rearrange("(t p) d -> t p d", p=P)
        out_d = out[0].rearrange("(t p) d -> t p d", p=P)
        wg_d = a["w_exp_gate"][0].rearrange("e (p k) f -> e p (k f)", p=P)
        wu_d = a["w_exp_up"][0].rearrange("e (p k) f -> e p (k f)", p=P)
        wd_d = a["w_exp_down"][0].rearrange("e (p j) d -> e p (j d)", p=P)

        NZ, NU, NM = 4, 8, 3 * KD

        def unit_loads(n):
            r = raw[n % 3]
            if n == 0:
                return [(r[:, :, :], w_in[:, :, QR:QR + KVR])]
            if n == 1:
                c = QR + KVR
                hr = ROPE // 2
                return ([(r[:, :, q * 32:q * 32 + hr], w_in[:, :, c + hr:c + ROPE]) for q in range(2)]
                        + [(r[:, :, q * 32 + hr:q * 32 + 32], w_in[:, :, c:c + hr]) for q in range(2)]
                        + [(r[:, :, q * 32:q * 32 + 32], w_in[:, :, c:c + ROPE]) for q in (2, 3)])
            if n < NZ:
                return [(r[:, :, :], w_in[:, :, (n - 2) * P:(n - 1) * P])]
            if n < NZ + NU:
                c = C_UV + (n - NZ) * P
                return [(r[:, :, :], w_in[:, :, c:c + P])]
            f, kind = divmod(n - NZ - NU, 3)
            if kind < 2:
                c = C_GATE + kind * D + f * P
                return [(r[:, :, :], w_in[:, :, c:c + P])]
            return [(r[:, 0:KS, :], w_oa[:, :, f * P:(f + 1) * P]),
                    (r[:, KS:, :], w_os[:, :, f * P:(f + 1) * P])]

        raw_count = [0, 0, 0]
        raw_value = {}
        for n in range(NZ + NU + NM):
            raw_count[n % 3] += 16 * len(unit_loads(n))
            raw_value[n] = raw_count[n % 3]

        def unit_used(eng, n):
            if n < NZ:
                eng.wait_ge(sem("z_done"), 2 * n + 2)
            elif n < NZ + NU:
                eng.wait_ge(sem("uv_done"), 2 * (n - NZ) + 2)
            else:
                eng.wait_ge(sem("unit_done"), n - NZ - NU + 1)

        def load_units(sp, lo, hi):
            for n in range(lo, hi):
                if n >= 3:
                    sp.wait_ge(sem("w_split"), n - 2)
                for dst, src in unit_loads(n):
                    sp.dma_start(dst, src).then_inc(sem(f"raw_full{n % 3}"), 16)

        def split_units(pool, lo, hi):
            for n in range(lo, hi):
                pool.wait_ge(sem(f"raw_full{n % 3}"), raw_value[n])
                if n >= 3:
                    unit_used(pool, n - 3)
                pool.tensor_copy(w_hi[n % 3][:, :, :], raw[n % 3][:, :, :]).then_inc(sem("w_hi_done"), 1)
                pool.wait_ge(sem("w_hi_done"), n + 1)
                pool.tensor_tensor(w_lo[n % 3][:, :, :], raw[n % 3][:, :, :],
                                   w_hi[n % 3][:, :, :].bitcast(F32), ALU.subtract).then_inc(sem("w_split"), 1)

        def mm3(pe, dst, st, mv, first, last):
            pe.matmul(dst, st[0], mv[0], start=first, stop=False)
            pe.matmul(dst, st[0], mv[1], start=False, stop=False)
            return pe.matmul(dst, st[1], mv[0], start=False, stop=last)

        stages = ["X", "Z", "A", "O", "U", "L", "M", "W", "R", "E", "C"]
        on = stages if stop_after is None else stages[:stages.index(stop_after) + 1]

        @block.sync
        def _(sp):
            sp.dma_start(cst[:, :], a["rope_constants"]).then_inc(sem("cst_full"), 16)
            sp.dma_start(pos_i[:, :], a["positions"].to_broadcast([P, T])).then_inc(sem("pos_full"), 16)
            sp.dma_start(g_attn[:, :], a["g_attn_norm"].to_broadcast([P, D])).then_inc(sem("g_full"), 16)
            for t in range(NT):
                if t >= 4:
                    sp.wait_ge(sem("hrow_ready"), t - 3)
                sp.dma_start(xin[t % 4][:, :], x_d[t]).then_inc(sem(f"x_full{t % 4}"), 16)
                if t == 3:
                    load_units(sp, 0, 3)
            sp.dma_start(gcol[:, 0:1], a["g_ckv"].rearrange("a p -> p a")).then_inc(sem("gcol_full"), 16)
            sp.dma_start(gcol[:, 1:3], a["g_cq"].rearrange("a (k p) -> p (a k)", p=P)).then_inc(sem("gcol_full"), 16)
            if "Z" in on:
                load_units(sp, 3, NZ)
            if "A" in on:
                sp.wait_ge(sem("w_split"), NZ)
                for h in range(HEADS):
                    if h >= 2:
                        sp.wait_ge(sem("hw_split"), h - 1)
                    r, f = h_raw[h % 2], sem(f"hraw_full{h % 2}")
                    q = r[:, 0:256].rearrange("p (k c) -> p k c", k=2)
                    c = h * (NOPE + ROPE)
                    sp.dma_start(q[:, :, 0:96], w_uq[:, :, c:c + 96]).then_inc(f, 16)
                    sp.dma_start(q[:, :, 96:112], w_uq[:, :, c + 80:c + 96]).then_inc(f, 16)
                    sp.dma_start(q[:, :, 112:128], w_uq[:, :, c + 64:c + 80]).then_inc(f, 16)
                    sp.dma_start(r[:, 256:320], a["w_uk"][0][:, h * 64:h * 64 + 64]).then_inc(f, 16)
                    sp.dma_start(r[:, 320:384], a["w_uv"][0][:, h * 64:h * 64 + 64]).then_inc(f, 16)
            if "U" in on:
                sp.wait_ge(sem("pv_done"), NQ)
                load_units(sp, NZ, NZ + NU)
            if "L" in on:
                sp.wait_ge(sem("uv_done"), 2 * NU)
                sp.dma_start(sp_raw[:, :, :], a["w_spatial"][0].rearrange("g i j -> i g j")).then_inc(sem("spraw_full"), 16)
                sp.dma_start(ln_g[:, :], a["sgu_gain"].to_broadcast([P, SGU])).then_inc(sem("ln_full"), 16)
                sp.dma_start(ln_b[:, :], a["sgu_bias"].to_broadcast([P, SGU])).then_inc(sem("ln_full"), 16)
                bs = a["b_spatial"].rearrange("a (q h) i -> a h q i", h=2)
                for hh in range(2):
                    sp.dma_start(sp_b[64 * hh:64 * hh + 64, :, :],
                                 bs[:, hh].to_broadcast([64, KS, P])).then_inc(sem("ln_full"), 16)
            if "M" in on:
                sp.wait_ge(sem("sp_done"), NT)
                sp.wait_ge(sem("s_lo_ready"), NT)
                load_units(sp, NZ + NU, NZ + NU + NM)
            if "W" in on:
                nu = NZ + NU + NM
                sp.wait_ge(sem("w_split"), nu)
                for k in range(KD):
                    if k >= 3:
                        sp.wait_ge(sem("wo_split"), k - 2)
                    sp.dma_start(raw[k % 3][:, :, :].rearrange("p a b -> p (a b)"),
                                 w_out[:, k, :]).then_inc(sem(f"wo_full{k % 3}"), 16)
                sp.wait_ge(sem("unit_done"), NM)
                sp.dma_start(g_ffn[:, :], a["g_ffn_norm"].to_broadcast([P, D])).then_inc(sem("rt_full"), 16)
                sp.dma_start(w_rt[:, :, 0:G], a["w_router_group"][0].rearrange("(k p) g -> p k g", p=P)).then_inc(sem("rt_full"), 16)
                for g in range(G):
                    sp.dma_start(w_rt[:, :, G + g * EPG:G + (g + 1) * EPG],
                                 a["w_router_expert"][0, g].rearrange("(k p) e -> p k e", p=P)).then_inc(sem("rt_full"), 16)
                sp.dma_start(b_rt[:, 0:G], a["b_router_group"].to_broadcast([P, G])).then_inc(sem("rt_full"), 16)
                sp.dma_start(b_rt[:, G:NR], a["b_router_expert"].rearrange("a g e -> a (g e)").to_broadcast([P, NE])).then_inc(sem("rt_full"), 16)
                for t in range(NT):
                    if t >= 2:
                        sp.wait_ge(sem("x2_ready"), t - 1)
                    sp.dma_start(xre[t % 2][:, :], x_d[t]).then_inc(sem(f"xre_full{t % 2}"), 16)
                    if t >= 1:
                        sp.wait_ge(sem("h2_ready"), t)
                        sp.dma_start(h2_dram[(t - 1) * P:t * P, :], h2[(t - 1) % 2][:, :]).then_inc(sem(f"h2_stored{(t - 1) % 2}"), 16)
                sp.wait_ge(sem("h2_ready"), NT)
                sp.dma_start(h2_dram[(NT - 1) * P:NT * P, :], h2[(NT - 1) % 2][:, :]).then_inc(sem(f"h2_stored{(NT - 1) % 2}"), 16)
            if "E" in on:
                sp.wait_ge(sem("out_done"), NT)
                sp.wait_ge(sem("rt_done"), NT)
                sp.wait_ge(sem("logit_ready"), NT)
                sp.wait_ge(sem("logit_read"), 1)
                with sp.Fori(0, NE // 4) as it:
                    for j in range(4):
                        e = it * 4 + j
                        sp.wait_ge(sem(f"we_used{j}"), it + 1)
                        f = sem(f"we_full{j}")
                        gu = w_gu[j][:, :, :, :].rearrange("p s k f -> p s (k f)")
                        sp.dma_start(gu[:, 0, :], wg_d[bass.ds(e, 1)].rearrange("e p n -> (e p) n")).then_inc(f, 16)
                        sp.dma_start(gu[:, 1, :], wu_d[bass.ds(e, 1)].rearrange("e p n -> (e p) n")).then_inc(f, 16)
                        sp.dma_start(w_dn[j][:, :, :].rearrange("p j d -> p (j d)"),
                                     wd_d[bass.ds(e, 1)].rearrange("e p n -> (e p) n")).then_inc(f, 16)
                sp.wait_ge(sem("tab_read"), 1)
                n_ovf = sp.value_load(ovf_n[0:1, 0:1], min_val=0, max_val=NOVF)
                with sp.If(n_ovf > 0):
                    with sp.Fori(0, n_ovf) as b:
                        sp.wait_ge(sem("we_used0"), b + NE // 4 + 1)
                        e = sp.value_load(ovf_e[0:1, bass.ds(b, 1)], min_val=0, max_val=NE - 1)
                        f = sem("we_full0")
                        gu = w_gu[0][:, :, :, :].rearrange("p s k f -> p s (k f)")
                        sp.dma_start(gu[:, 0, :], wg_d[bass.ds(e, 1)].rearrange("e p n -> (e p) n")).then_inc(f, 16)
                        sp.dma_start(gu[:, 1, :], wu_d[bass.ds(e, 1)].rearrange("e p n -> (e p) n")).then_inc(f, 16)
                        sp.dma_start(w_dn[0][:, :, :].rearrange("p j d -> p (j d)"),
                                     wd_d[bass.ds(e, 1)].rearrange("e p n -> (e p) n")).then_inc(f, 16)
            if "C" in on:
                sp.wait_ge(sem("y_stored_all"), 1)
                sp.dma_start(g_fin[:, :], a["g_final"].rearrange("(a d) -> a d", a=1).to_broadcast([P, D])).then_inc(sem("gfin_full"), 16)
                for t in range(NT):
                    if t >= 2:
                        sp.wait_ge(sem("acc_ready"), t - 1)
                    for k in range(2):
                        r0 = k * T + t * P
                        sp.dma_start(yin[t % 2][:, k, :], y_dram[r0:r0 + P, :]).then_inc(sem(f"yin_full{t % 2}"), 16)
                    if t >= 1:
                        sp.wait_ge(sem("res_ready"), t)
                        sp.dma_start(out_d[t - 1], res[(t - 1) % 2][:, :]).then_inc(sem(f"res_stored{(t - 1) % 2}"), 16)
                sp.wait_ge(sem("res_ready"), NT)
                sp.dma_start(out_d[NT - 1], res[(NT - 1) % 2][:, :]).then_inc(sem(f"res_stored{(NT - 1) % 2}"), 16)
                for i in range(2):
                    sp.wait_ge(sem(f"res_stored{i}"), 16 * NT // 2)

        @block.tensor
        def _(pe):
            for t in range(NT):
                pe.wait_ge(sem("hrow_ready"), t + 1)
                if t == 0:
                    pe.wait_ge(sem("const_ready"), 1)
                if t >= 2:
                    pe.wait_ge(sem("ht_lo_ready"), t - 1)
                b = 2 * (t % 2)
                for k in range(KD):
                    mm = pe.transpose(ps[:, b + k // 4, (k % 4) * P:(k % 4) * P + P],
                                      hrow[t % 2][:, k * P:(k + 1) * P], ident[:, :])
                mm.then_inc(sem("x_tr"), 1)
            if "Z" in on:
                for u in range(NZ):
                    pe.wait_ge(sem("w_split"), u + 1)
                    for c in range(2):
                        pe.wait_ge(sem("ht_lo_ready"), 4 * (c + 1) if u == 0 else NT)
                        dst = ps[:, (2 * u + c + 4) % 8, :]
                        for k in range(KD):
                            mm = mm3(pe, dst, (w_hi[u % 3][:, k, :], w_lo[u % 3][:, k, :]),
                                     (ht_hi[:, k, c * HALF:(c + 1) * HALF], ht_lo[:, k, c * HALF:(c + 1) * HALF]),
                                     k == 0, k == KD - 1)
                        mm.then_inc(sem("z_done"), 1)
                pe.wait_ge(sem("c_sq_ready"), 2)
                for c in range(2):
                    pe.matmul(ps[:, 4 + c, :], ones[:, :], c_sq[:, 0, c * HALF:(c + 1) * HALF],
                              start=True, stop=True).then_inc(sem("ms_done"), 1)
                pe.wait_ge(sem("c_sq_ready"), 6)
                pe.wait_ge(sem("kr_read"), 2)
                for c in range(2):
                    pe.matmul(ps[:, 6 + c, :], ones[:, :], c_sq[:, 1, c * HALF:(c + 1) * HALF], start=True, stop=False)
                    pe.matmul(ps[:, 6 + c, :], ones[:, :], c_sq[:, 2, c * HALF:(c + 1) * HALF],
                              start=False, stop=True).then_inc(sem("ms_done"), 1)
            if "A" in on:
                def job(h, j):
                    hh, hl = h_hi[h % 2], h_lo[h % 2]
                    if j == 0:
                        pe.wait_ge(sem("hw_split"), h + 1)
                    if j in (1, 2):
                        pe.wait_ge(sem("q_tmp_ready"), 2 * h + j)
                    elif h or j:
                        pe.wait_ge(sem("kv_lo_ready"), 3 * h + max(j - 2, 0))
                    if j < 2:
                        cs = slice(j * HALF, (j + 1) * HALF)
                        for k in range(2):
                            mm = mm3(pe, ps[:, 7, :], (hh[:, k * P:(k + 1) * P], hl[:, k * P:(k + 1) * P]),
                                     (c_hi[:, 1 + k, cs], c_lo[:, 1 + k, cs]), k == 0, k == 1)
                    elif j < 4:
                        cs = slice((j - 2) * HALF, (j - 1) * HALF)
                        mm = mm3(pe, ps[:, 7, :], (hh[:, 256:384], hl[:, 256:384]),
                                 (c_hi[:, 0, cs], c_lo[:, 0, cs]), True, True)
                    else:
                        for t in range(NT):
                            ts = slice(t * P, (t + 1) * P)
                            mm = mm3(pe, ps[:, 7, t * VH:(t + 1) * VH], (c_hi[:, 0, ts], c_lo[:, 0, ts]),
                                     (hh[:, 320:384], hl[:, 320:384]), True, True)
                    mm.then_inc(sem("job_done"), 1)

                def scores(s):
                    h, i = divmod(s, NT)
                    pe.wait_ge(sem("q_lo_ready"), 2 * h + 1 + i // 4)
                    pe.wait_ge(sem("kv_lo_ready"), 3 * h + 1 + i // 4)
                    if s >= 2:
                        pe.wait_ge(sem("exp_done"), s - 1)
                    qs = slice(i * P, (i + 1) * P)
                    n = (i + 1) * P
                    for c in range(i // 4 + 1):
                        m = min(n - c * HALF, HALF)
                        dst = ps[:, 2 * (s % 2) + c, :]
                        last = c == i // 4
                        mm = mm3(pe, dst[:, 0:m], (q_hi[h % 2][:, qs], q_lo[h % 2][:, qs]),
                                 (k_hi[h % 2][:, c * HALF:c * HALF + m], k_lo[h % 2][:, c * HALF:c * HALF + m]),
                                 True, not last)
                        if last:
                            mm = pe.matmul(dst[:, m - CHUNK:m], mask_l[:, :], mask_r[:, :], start=False, stop=True)
                    mm.then_inc(sem("s_done"), 1)

                def prob_transposes(s):
                    i = s % NT
                    c0 = chunks_through(s - 1) if s else 0
                    pe.wait_ge(sem("exp_done"), s + 1)
                    for c in range(i // 4 + 1):
                        if c0 + c >= 2:
                            pe.wait_ge(sem("pt_lo_ready"), c0 + c - 1)
                        for j in range(4 * c, min(4 * c + 4, i + 1)):
                            mm = pe.transpose(ps[:, 4 + (c0 + c) % 2, (j % 4) * P:(j % 4) * P + P],
                                              prob[s % 2][:, j * P:(j + 1) * P], ident[:, :])
                        mm.then_inc(sem("pt_done"), 1)

                def values(s):
                    h, i = divmod(s, NT)
                    c0 = chunks_through(s - 1) if s else 0
                    pe.wait_ge(sem("kv_lo_ready"), 3 * h + 3)
                    pe.wait_ge(sem("pt_lo_ready"), chunks_through(s))
                    if s:
                        pe.wait_ge(sem("o_ready"), s)
                    dst = ps[:, 6, i * VH:(i + 1) * VH]
                    for j in range(i + 1):
                        c = (c0 + j // 4) % 4
                        mm = mm3(pe, dst, (pt_hi[c][:, j % 4, :], pt_lo[c][:, j % 4, :]),
                                 (v_hi[h % 2][:, j, :], v_lo[h % 2][:, j, :]), j == 0, j == i)
                    mm.then_inc(sem("pv_done"), 1)

                pe.wait_ge(sem("c_lo_ready"), 6)
                pe.wait_ge(sem("c_std_ready"), 4)
                for j in range(5):
                    job(0, j)
                scores(0)
                scores(1)
                for s in range(NQ):
                    prob_transposes(s)
                    if s + 2 < NQ:
                        scores(s + 2)
                    h, i = divmod(s, NT)
                    if i < 5 and h + 1 < HEADS:
                        job(h + 1, i)
                    values(s)
            if "O" in on:
                for t in range(NT):
                    pe.wait_ge(sem("o_ready"), NQ)
                    if t >= 4:
                        pe.wait_ge(sem("ot_lo_ready"), t - 3)
                    for j in range(KS):
                        mm = pe.transpose(ps[:, t % 4, j * P:(j + 1) * P], o_tok[:, t, j * P:(j + 1) * P], ident[:, :])
                    mm.then_inc(sem("ot_tr"), 1)
            if "U" in on:
                for n in range(NZ, NZ + NU):
                    pe.wait_ge(sem("w_split"), n + 1)
                    for c in range(2):
                        jj = 2 * (n - NZ) + c
                        if jj >= 4:
                            pe.wait_ge(sem("gelu_ready"), jj - 3)
                        cs = slice(c * HALF, (c + 1) * HALF)
                        for k in range(KD):
                            mm = mm3(pe, ps[:, 4 + jj % 4, :], (w_hi[n % 3][:, k, :], w_lo[n % 3][:, k, :]),
                                     (ht_hi[:, k, cs], ht_lo[:, k, cs]), k == 0, k == KD - 1)
                        mm.then_inc(sem("uv_done"), 1)
            if "L" in on:
                pe.wait_ge(sem("gelu_ready"), 2 * NU)
                pe.wait_ge(sem("sp_masked"), 1)
                for g in range(8):
                    mm = pe.transpose(ps[:, 4 + g // 4, (g % 4) * P:(g % 4) * P + P], sp_raw[:, g, :], ident[:, :])
                mm.then_inc(sem("sp_tr"), 1)

                def v_rows(t):
                    if t >= 2:
                        pe.wait_ge(sem("ln_read"), t - 1)
                    else:
                        pe.wait_ge(sem("ot_lo_ready"), NT)
                    for j in range(KS):
                        mm = pe.transpose(ps[:, 6 + t % 2, j * P:(j + 1) * P], v_t[:, j, t * P:(t + 1) * P], ident[:, :])
                    mm.then_inc(sem("v_tr"), 1)

                v_rows(0)
                pe.wait_ge(sem("sp_lo_ready"), 1)
                for t in range(NT):
                    if t + 1 < NT:
                        v_rows(t + 1)
                    pe.wait_ge(sem("vn_lo_ready"), t + 1)
                    if t >= 2:
                        pe.wait_ge(sem("s_read"), 2 * (t - 1))
                    for pr in range(KS):
                        b = 2 * (t % 2) + pr // 2
                        cs = slice(pr * P, (pr + 1) * P)
                        gs = slice(2 * pr, 2 * pr + 2)
                        mm = mm3(pe, ps[:, b, (pr % 2) * 256:(pr % 2) * 256 + 256],
                                 (vn_hi[t % 2][:, cs], vn_lo[t % 2][:, cs]),
                                 (sp_hi[:, gs, :].rearrange("p a b -> p (a b)"), sp_lo[:, gs, :].rearrange("p a b -> p (a b)")),
                                 True, True)
                    mm.then_inc(sem("sp_done"), 1)
            if "M" in on:
                pe.wait_ge(sem("s_lo_ready"), NT)
                for f in range(KD):
                    for kind in range(3):
                        n = NZ + NU + 3 * f + kind
                        pe.wait_ge(sem("w_split"), n + 1)
                        if f:
                            pe.wait_ge(sem("sig_a_ready" if kind == 0 else "sig_b_ready" if kind == 1 else "mix_ready"), 2 * f)
                        wh, wl = w_hi[n % 3], w_lo[n % 3]
                        for c in range(2):
                            cs = slice(c * HALF, (c + 1) * HALF)
                            if kind < 2:
                                for k in range(KD):
                                    mm = mm3(pe, ps[:, 2 * kind + c, :], (wh[:, k, :], wl[:, k, :]),
                                             (ht_hi[:, k, cs], ht_lo[:, k, cs]), k == 0, k == KD - 1)
                            else:
                                for k in range(KS):
                                    mm3(pe, ps[:, 4 + c, :], (wh[:, k, :], wl[:, k, :]),
                                        (ot_hi[:, k, cs], ot_lo[:, k, cs]), k == 0, k == KS - 1)
                                for k in range(KS):
                                    mm = mm3(pe, ps[:, 6 + c, :], (wh[:, KS + k, :], wl[:, KS + k, :]),
                                             (st_hi[:, k, cs], st_lo[:, k, cs]), k == 0, k == KS - 1)
                        mm.then_inc(sem("unit_done"), 1)
            if "W" in on:
                pe.wait_ge(sem("mix_ready"), 2 * KD)

                def router(t):
                    pe.wait_ge(sem("h2_ready"), t + 1)
                    if t >= 1:
                        pe.wait_ge(sem("h2t_ready"), t)
                    for k in range(KD):
                        mm = pe.transpose(ps[:, 4 + k // 4, (k % 4) * P:(k % 4) * P + P],
                                          h2[t % 2][:, k * P:(k + 1) * P], ident[:, :])
                    mm.then_inc(sem("h2_tr"), 1)
                    pe.wait_ge(sem("h2t_ready"), t + 1)
                    pe.wait_ge(sem("rt_full"), 16 * 8)
                    if t >= 1:
                        pe.wait_ge(sem("logit_ready"), t)
                    for k in range(KD):
                        mm = pe.matmul(ps[:, 6, 0:NR], h2t[t % 2][:, k, :], w_rt[:, k, :], start=(k == 0), stop=(k == KD - 1))
                    mm.then_inc(sem("rt_done"), 1)

                for t in range(NT):
                    pe.wait_ge(sem("mt_lo_ready"), t + 1)
                    if t >= 2:
                        pe.wait_ge(sem("x2_ready"), t - 1)
                    for k in range(KD):
                        if t == 0:
                            pe.wait_ge(sem("wo_split"), k + 1)
                        for c in range(2):
                            cs = slice(c * HALF, (c + 1) * HALF)
                            mm = mm3(pe, ps[:, 2 * (t % 2) + c, :], (mt_hi[t % 2][:, k, :], mt_lo[t % 2][:, k, :]),
                                     (wo_hi[:, k, cs], wo_lo[:, k, cs]), k == 0, k == KD - 1)
                    mm.then_inc(sem("out_done"), 1)
                    if t >= 1:
                        router(t - 1)
                router(NT - 1)
            if "R" in on:
                pe.wait_ge(sem("oe_ready"), 1)
                pe.matmul(ps[:, 0, 0:NT * NE], before[:, :], oe_b[:, :, :].rearrange("p t e -> p (t e)"), start=True, stop=False)
                pe.matmul(ps[:, 0, 0:NT * NE], ones_b[:, :], cum_b[:, 0:NT, :].rearrange("p t e -> p (t e)"),
                          start=False, stop=True)
                pe.matmul(ps[:, 1, 0:NE], ones_b[:, :], cum_b[:, NT, :], start=True, stop=True).then_inc(sem("rank_done"), 1)
                for i in range(2 * NT):
                    pe.wait_ge(sem("sel_ready"), i + 1)
                    pe.matmul(ps[:, 2, 0:NBLK], sel_a[i % 2][:, :], sel_b[i % 2][:, :], start=(i == 0),
                              stop=(i == 2 * NT - 1)).then_inc(sem("sel_used"), 1)
            if "E" in on:
                def rows_in(n, j):
                    pe.wait_ge(sem(f"xs_full{j}"), (n + 1) * 16)
                    pe.wait_ge(sem("xst_ready"), 2 * n + j)
                    v = xs[j][:, :].rearrange("s (p k) -> s k p", k=KD)
                    for k in range(KD):
                        mm = pe.transpose(ps[:, k // 4, (k % 4) * P:(k % 4) * P + P], v[:, k, :], ident[:, :])
                    mm.then_inc(sem("xs_tr"), 1)

                def gate_up(n, j, slot, full):
                    pe.wait_ge(sem("xst_ready"), 2 * n + j + 1)
                    pe.wait_ge(sem(f"we_full{slot}"), full)
                    pe.wait_ge(sem("hid_ready"), 2 * n + j + 1)
                    for half in range(2):
                        for k in range(KD):
                            mm = pe.matmul(ps[:, 2, half * DE:(half + 1) * DE], xst[j][:, k, :],
                                           w_gu[slot][:, half, k, :], start=(k == 0), stop=(k == KD - 1))
                    mm.then_inc(sem("gu_done"), 1)

                def down(n, j, slot):
                    pe.wait_ge(sem("hid_ready"), 2 * n + j + 1 + 1)
                    pe.wait_ge(sem("hidt_ready"), 2 * n + j + 1)
                    v = hid[j][:, :].rearrange("s (p q) -> s q p", q=2)
                    for q in range(2):
                        mm = pe.transpose(ps[:, 3, q * P:(q + 1) * P], v[:, q, :], ident[:, :])
                    mm.then_inc(sem("hid_tr"), 1)
                    pe.wait_ge(sem("hidt_ready"), 2 * n + j + 1 + 1)
                    pe.wait_ge(sem(f"y_ready{j}"), 2 * n + 2)
                    for c in range(2):
                        for q in range(2):
                            mm = pe.matmul(ps[:, 4 + 2 * j + c, :], hidt[j][:, q, :], w_dn[slot][:, q, c * HALF:(c + 1) * HALF],
                                           start=(q == 0), stop=(q == 1))
                    mm.then_inc(sem(f"we_used{slot}"), 1)

                pe.sem_inc(sem("hid_tr"), 1)
                pe.sem_inc(sem("xs_tr"), 1)
                for i in range(4):
                    pe.sem_inc(sem(f"we_used{i}"), 1)
                pe.wait_ge(sem("tab_read"), 1)
                rows_in(0, 0)
                with pe.Fori(0, NE // 4) as it:
                    for j in range(4):
                        gate_up(it * 2 + j // 2, j % 2, j, it * 48 + 48)
                        rows_in(it * 2 + (j + 1) // 2, (j + 1) % 2)
                        down(it * 2 + j // 2, j % 2, j)
                n_ovf = pe.value_load(ovf_n[0:1, 0:1], min_val=0, max_val=NOVF)
                with pe.If(n_ovf > 0):
                    with pe.Fori(0, n_ovf) as b:
                        pe.wait_ge(sem("xst_ready"), b + NE + 1)
                        pe.wait_ge(sem("we_full0"), b * 48 + 48 * (NE // 4 + 1))
                        pe.wait_ge(sem("hid_ready"), b + NE + 1)
                        for half in range(2):
                            for k in range(KD):
                                mm = pe.matmul(ps[:, 2, half * DE:(half + 1) * DE], xst[0][:, k, :],
                                               w_gu[0][:, half, k, :], start=(k == 0), stop=(k == KD - 1))
                        mm.then_inc(sem("gu_done"), 1)
                        pe.wait_ge(sem("hid_ready"), b + NE + 1 + 1)
                        v = hid[0][:, :].rearrange("s (p q) -> s q p", q=2)
                        for q in range(2):
                            mm = pe.transpose(ps[:, 3, q * P:(q + 1) * P], v[:, q, :], ident[:, :])
                        mm.then_inc(sem("hid_tr"), 1)
                        pe.wait_ge(sem("hidt_ready"), b + NE + 1 + 1)
                        pe.wait_ge(sem("y_ready0"), b * 2 + NE + 2)
                        for c in range(2):
                            for q in range(2):
                                mm = pe.matmul(ps[:, 4 + c, :], hidt[0][:, q, :], w_dn[0][:, q, c * HALF:(c + 1) * HALF],
                                               start=(q == 0), stop=(q == 1))
                        mm.then_inc(sem("we_used0"), 1)
                        pe.wait_ge(sem("xs_full0"), b * 16 + 16 * (NE // 2 + 2))
                        vx = xs[0][:, :].rearrange("s (p k) -> s k p", k=KD)
                        for k in range(KD):
                            mm = pe.transpose(ps[:, k // 4, (k % 4) * P:(k % 4) * P + P], vx[:, k, :], ident[:, :])
                        mm.then_inc(sem("xs_tr"), 1)

        @block.scalar
        def _(act):
            act.wait_ge(sem("const_ready"), 1)

            def ht_high(t):
                act.wait_ge(sem("x_tr"), t + 1)
                b = 2 * (t % 2)
                act.activation(ht_hi[:, :, t * P:(t + 1) * P],
                               ps[:, b:b + 2, :].rearrange("p b (k c) -> p (b k) c", c=P), ACT.Copy).then_inc(sem("ht_hi_ready"), 1)

            for t in range(NT):
                act.wait_ge(sem(f"x_full{t % 4}"), 16 * (t // 4 + 1))
                if t:
                    act.wait_ge(sem("ssq_ready"), t)
                act.activation(junk[:, :], xin[t % 4][:, :], ACT.Square, accum_out=ssq[:, t:t + 1]).then_inc(sem("ssq_ready"), 1)
                act.wait_ge(sem("ssq_ready"), t + 1)
                act.activation(std[:, t:t + 1], ssq[:, t:t + 1], ACT.Sqrt, scale=1.0 / D, bias=epst[:, :]).then_inc(sem("std_ready"), 1)
                if t:
                    ht_high(t - 1)
            ht_high(NT - 1)
            if "Z" in on:
                for j in range(2):
                    act.wait_ge(sem("ang_ready"), j + 1)
                    act.activation((tab_q if j == 0 else tab_k)[:, :], ang[:, :], ACT.Sin).then_inc(sem("sin_ready"), 1)
                for i, u in enumerate((0, 2, 3)):
                    for c in range(2):
                        cs = slice(c * HALF, (c + 1) * HALF)
                        act.wait_ge(sem("z_done"), 2 * u + c + 1)
                        src = ps[:, (2 * u + c + 4) % 8, :]
                        act.activation(c_raw[:, i, cs], src, ACT.Copy).then_inc(sem("c_raw_ready"), 1)
                        act.activation(c_sq[:, i, cs], src, ACT.Square).then_inc(sem("c_sq_ready"), 1)
                for i in range(4):
                    act.wait_ge(sem("ms_done"), i + 1)
                    act.activation(c_rs[:, i, :], ps[:, 4 + i, :], ACT.Sqrt, scale=1.0 / (KVR if i < 2 else QR),
                                   bias=epst[:, :]).then_inc(sem("c_std_ready"), 1)
                for i in range(6):
                    cs = slice((i % 2) * HALF, (i % 2 + 1) * HALF)
                    act.wait_ge(sem("cn_ready"), i + 1)
                    act.activation(c_hi[:, i // 2, cs], c_raw[:, i // 2, cs], ACT.Copy).then_inc(sem("c_hi_ready"), 1)
            if "A" in on:
                def job_high(h, j):
                    act.wait_ge(sem("job_done"), 5 * h + j + 1)
                    if j < 2:
                        act.wait_ge(sem("q_tmp_ready"), 2 * h + j + 1)
                        act.activation(q_hi[h % 2][:, j * HALF:(j + 1) * HALF], q_tmp[j][:, :], ACT.Copy).then_inc(sem("q_hi_ready"), 1)
                    elif j < 4:
                        act.activation(k_hi[h % 2][0:64, (j - 2) * HALF:(j - 1) * HALF], ps[0:64, 7, :], ACT.Copy).then_inc(sem("kv_hi_ready"), 1)
                    else:
                        act.activation(v_hi[h % 2][:, :, :].rearrange("p t c -> p (t c)"), ps[:, 7, :], ACT.Copy).then_inc(sem("kv_hi_ready"), 1)

                def exponent(s):
                    n = (s % NT + 1) * P
                    act.wait_ge(sem("max_ready"), s + 1)
                    if s >= 2:
                        act.wait_ge(sem("pt_done"), chunks_through(s - 2))
                    b = 2 * (s % 2)
                    act.activation(prob[s % 2][:, 0:n], ps[:, b:b + 2, :].rearrange("p b c -> p (b c)")[:, 0:n], ACT.Exp,
                                   bias=negm[:, s:s + 1], accum_out=lsum[:, s:s + 1]).then_inc(sem("exp_done"), 1)

                for j in range(5):
                    job_high(0, j)
                exponent(0)
                for s in range(NQ):
                    h, i = divmod(s, NT)
                    c0 = chunks_through(s - 1) if s else 0
                    for c in range(i // 4 + 1):
                        w = min(4, i + 1 - 4 * c)
                        cc = c0 + c
                        act.wait_ge(sem("pt_done"), cc + 1)
                        if cc >= 4:
                            used = next(x for x in range(s + 1) if chunks_through(x) > cc - 4)
                            act.wait_ge(sem("pv_done"), used + 1)
                        act.activation(pt_hi[cc % 4][:, 0:w, :].rearrange("p a b -> p (a b)"), ps[:, 4 + cc % 2, 0:w * P],
                                       ACT.Copy).then_inc(sem("pt_hi_ready"), 1)
                    if s + 1 < NQ:
                        exponent(s + 1)
                    if i < 5 and h + 1 < HEADS:
                        job_high(h + 1, i)
            if "O" in on:
                for t in range(NT):
                    act.wait_ge(sem("ot_tr"), t + 1)
                    act.activation(ot_hi[:, :, t * P:(t + 1) * P], ps[:, t % 4, :].rearrange("p (k c) -> p k c", c=P),
                                   ACT.Copy).then_inc(sem("ot_hi_ready"), 1)
            if "U" in on:
                act.wait_ge(sem("ot_tr"), NT)
                for jj in range(2 * NU):
                    f, c = divmod(jj, 2)
                    act.wait_ge(sem("uv_done"), jj + 1)
                    dst = (u_t if f < KS else v_t)[:, f % KS, c * HALF:(c + 1) * HALF]
                    act.activation(dst, ps[:, 4 + jj % 4, :], ACT.Gelu_apprx_tanh).then_inc(sem("gelu_ready"), 1)
            if "L" in on:
                act.wait_ge(sem("sp_tr"), 1)
                act.activation(sp_hi[:, :, :], ps[:, 4:6, :].rearrange("p b (g c) -> p (b g) c", c=P), ACT.Copy).then_inc(sem("sp_hi_ready"), 1)

                def ln_std(t):
                    act.wait_ge(sem("bn_ready"), t + 1)
                    act.activation(std[:, NT + t:NT + t + 1], bnag[:, t, 1:2], ACT.Sqrt, bias=epst[:, :]).then_inc(sem("ln_std_ready"), 1)

                def vn_high(t):
                    act.wait_ge(sem("ln_ready"), t + 1)
                    if t >= 2:
                        act.wait_ge(sem("sp_done"), t - 1)
                    act.activation(vn_hi[t % 2][:, :], ln_t[t % 2][:, :], ACT.Copy).then_inc(sem("vn_hi_ready"), 1)

                def s_high(t):
                    act.wait_ge(sem("s_ready"), t + 1)
                    act.activation(st_hi[:, :, t * P:(t + 1) * P], s_t[t % 2][:, :, :], ACT.Copy).then_inc(sem("s_hi_ready"), 1)

                for t in range(NT):
                    ln_std(t)
                    vn_high(t)
                    if t:
                        s_high(t - 1)
                s_high(NT - 1)
            if "M" in on:
                for f in range(KD):
                    for kind in range(2):
                        act.wait_ge(sem("unit_done"), 3 * f + kind + 1)
                        for c in range(2):
                            cs = slice(c * HALF, (c + 1) * HALF)
                            if kind == 1 and f:
                                act.wait_ge(sem("mix_ready"), 2 * f + c - 1)
                            dst = mix[:, f, cs] if kind == 0 else sig_b[c][:, :]
                            act.activation(dst, ps[:, 2 * kind + c, :],
                                           ACT.Sigmoid).then_inc(sem("sig_a_ready" if kind == 0 else "sig_b_ready"), 1)
            if "W" in on:
                for k in range(KD):
                    act.wait_ge(sem(f"wo_full{k % 3}"), 16 * (k // 3 + 1))
                    if k == 0:
                        act.wait_ge(sem("unit_done"), NM)
                    act.activation(wo_hi[:, k, :], raw[k % 3][:, :, :].rearrange("p a b -> p (a b)"), ACT.Copy).then_inc(sem("wo_hi_ready"), 1)
                    if k < 2:
                        act.wait_ge(sem("mix_ready"), 2 * KD)
                        act.activation(mt_hi[k][:, :, :], mix[:, :, k * P:(k + 1) * P], ACT.Copy).then_inc(sem("mt_hi_ready"), 1)

                def logits_in(t):
                    act.wait_ge(sem("h2_tr"), t + 1)
                    if t >= 2:
                        act.wait_ge(sem("rt_done"), t - 1)
                    act.activation(h2t[t % 2][:, :, :], ps[:, 4:6, :].rearrange("p b (k c) -> p (b k) c", c=P), ACT.Copy).then_inc(sem("h2t_ready"), 1)

                for t in range(NT):
                    act.wait_ge(sem("x2_ready"), t + 1)
                    if t:
                        act.wait_ge(sem("ssq2_ready"), t)
                    act.activation(junk2[:, :], x2[:, t, :], ACT.Square, accum_out=ssq[:, 8 + t:9 + t]).then_inc(sem("ssq2_ready"), 1)
                    act.wait_ge(sem("ssq2_ready"), t + 1)
                    act.activation(std[:, 8 + t:9 + t], ssq[:, 8 + t:9 + t], ACT.Sqrt, scale=1.0 / D, bias=epst[:, :]).then_inc(sem("std2_ready"), 1)
                    if t + 2 < NT:
                        act.wait_ge(sem("out_done"), t + 1)
                        act.activation(mt_hi[t % 2][:, :, :], mix[:, :, (t + 2) * P:(t + 3) * P], ACT.Copy).then_inc(sem("mt_hi_ready"), 1)
                    logits_in(t)
            if "R" in on:
                act.wait_ge(sem("gmax_ready"), 1)
                act.activation(ex[:, :, :], ex[:, :, :], ACT.Exp).then_inc(sem("gexp_ready"), 1)
                act.wait_ge(sem("ediff_ready"), 1)
                act.activation(gatew[:, 1, :], gatew[:, 1, :], ACT.Exp).then_inc(sem("gexp_ready"), 1)
            if "E" in on:
                def rows_copy(n, j):
                    act.wait_ge(sem("xs_tr"), 2 * n + j + 1 + 1)
                    act.activation(xst[j][:, :, :], ps[:, 0:2, :].rearrange("p b (k c) -> p (b k) c", c=P), ACT.Copy).then_inc(sem("xst_ready"), 1)

                act.sem_inc(sem("hidt_ready"), 1)
                rows_copy(0, 0)
                with act.Fori(0, NE // 4) as it:
                    for j in range(4):
                        n, q = it * 2 + j // 2, j % 2
                        act.wait_ge(sem("gu_done"), n * 2 + q + 1)
                        act.activation(sg[q][:, :], ps[:, 2, 0:DE], ACT.Silu).then_inc(sem("sg_ready"), 1)
                        rows_copy(it * 2 + (j + 1) // 2, (j + 1) % 2)
                        act.wait_ge(sem("hid_tr"), n * 2 + q + 1 + 1)
                        act.activation(hidt[q][:, :, :].rearrange("p a b -> p (a b)"), ps[:, 3, 0:2 * P], ACT.Copy).then_inc(sem("hidt_ready"), 1)
                        act.wait_ge(sem(f"we_used{j}"), it + 1 + 1)
                        act.wait_ge(sem(f"y_sent{q}"), n * 16 + 16)
                        act.activation(y[q][:, 0:HALF], ps[:, 4 + 2 * q, :], ACT.Copy).then_inc(sem(f"y_ready{q}"), 1)
                act.wait_ge(sem("tab_read"), 1)
                n_ovf = act.value_load(ovf_n[0:1, 0:1], min_val=0, max_val=NOVF)
                with act.If(n_ovf > 0):
                    with act.Fori(0, n_ovf) as b:
                        act.wait_ge(sem("gu_done"), b + NE + 1)
                        act.activation(sg[0][:, :], ps[:, 2, 0:DE], ACT.Silu).then_inc(sem("sg_ready"), 1)
                        act.wait_ge(sem("hid_tr"), b + NE + 1 + 1)
                        act.activation(hidt[0][:, :, :].rearrange("p a b -> p (a b)"), ps[:, 3, 0:2 * P], ACT.Copy).then_inc(sem("hidt_ready"), 1)
                        act.wait_ge(sem("we_used0"), b + NE // 4 + 1 + 1)
                        act.wait_ge(sem("y_sent0"), b * 16 + 16 * (NE // 2) + 16)
                        act.activation(y[0][:, 0:HALF], ps[:, 4, :], ACT.Copy).then_inc(sem("y_ready0"), 1)
                        act.wait_ge(sem("xs_tr"), b + NE + 2 + 1)
                        act.activation(xst[0][:, :, :], ps[:, 0:2, :].rearrange("p b (k c) -> p (b k) c", c=P), ACT.Copy).then_inc(sem("xst_ready"), 1)
            if "C" in on:
                for t in range(NT):
                    act.wait_ge(sem("acc_ready"), t + 1)
                    if t:
                        act.wait_ge(sem("ssq3_ready"), t)
                    act.activation(junk3[:, :], acc[t % 2][:, :], ACT.Square, accum_out=ssq[:, 16 + t:17 + t]).then_inc(sem("ssq3_ready"), 1)
                    act.wait_ge(sem("ssq3_ready"), t + 1)
                    act.activation(std[:, 16 + t:17 + t], ssq[:, 16 + t:17 + t], ACT.Sqrt, scale=1.0 / D, bias=epst[:, :]).then_inc(sem("std3_ready"), 1)

        @block.vector
        def _(dve):
            steps = [0]

            def link(ins):
                steps[0] += 1
                ins.then_inc(sem("dve_step"), 1)
                dve.wait_ge(sem("dve_step"), steps[0])

            dve.wait_ge(sem("iota_ready"), 2)
            link(dve.tensor_scalar(ident[:, :], iota_row[:, :], iota_col[:, :], None, ALU.is_equal))
            link(dve.tensor_scalar(before[:, :], iota_row[:, :], iota_col[:, :], None, ALU.is_gt))
            link(dve.memset(ones[:, :], 1.0))
            link(dve.memset(ones_b[:, :], 1.0))
            link(dve.memset(epst[:, :], EPS))
            link(dve.memset(mask_l[:, :].bitcast(F32), 0.0))
            link(dve.memset(mask_l[0:1, 0:CHUNK].bitcast(F32), -BIG))
            dve.memset(mask_r[:, :].bitcast(F32), 1.0).then_inc(sem("const_ready"), 1)

            def rope_angles(j):
                fr, ph = cst[:, 3 * j:3 * j + 1], cst[:, 3 * j + 2:3 * j + 3]
                if j:
                    dve.wait_ge(sem("sin_ready"), j)
                link(dve.tensor_copy(turns[:, :], pos_i[:, :]))
                link(dve.tensor_scalar(ang[:, :], turns[:, :], fr, None, ALU.mult))
                link(dve.tensor_scalar(turns[:, :], ang[:, :], 1.0 / TWO_PI, cst[:, 3 * j + 1:3 * j + 2], ALU.mult, ALU.add))
                link(dve.tensor_scalar(turns[:, :], turns[:, :], MAGIC, MAGIC, ALU.add, ALU.subtract))
                for c in (C1, C2, C3):
                    link(dve.scalar_tensor_tensor(ang[:, :], turns[:, :], -c, ang[:, :], ALU.mult, ALU.add))
                link(dve.tensor_scalar(ang[:, :], ang[:, :], ph, PI_IN, ALU.add, ALU.min))
                dve.tensor_scalar(ang[:, :], ang[:, :], -PI_IN, None, ALU.max).then_inc(sem("ang_ready"), 1)

            def ht_low(t):
                dve.wait_ge(sem("ht_hi_ready"), t + 1)
                b = 2 * (t % 2)
                ts = slice(t * P, (t + 1) * P)
                dve.tensor_tensor(ht_lo[:, :, ts], ps[:, b:b + 2, :].rearrange("p b (k c) -> p (b k) c", c=P),
                                  ht_hi[:, :, ts].bitcast(F32), ALU.subtract).then_inc(sem("ht_lo_ready"), 1)

            dve.wait_ge(sem("g_full"), 16)
            for t in range(NT):
                dve.wait_ge(sem("std_ready"), t + 1)
                link(dve.reciprocal(rstd[:, t:t + 1], std[:, t:t + 1]))
                if t >= 2:
                    dve.wait_ge(sem("x_tr"), t - 1)
                dve.scalar_tensor_tensor(hrow[t % 2][:, :], xin[t % 4][:, :], rstd[:, t:t + 1], g_attn[:, :],
                                         ALU.mult, ALU.mult).then_inc(sem("hrow_ready"), 1)
                if t:
                    ht_low(t - 1)
            ht_low(NT - 1)
            if "Z" in on:
                dve.wait_ge(sem("cst_full"), 16)
                dve.wait_ge(sem("pos_full"), 16)
                rope_angles(0)
                rope_angles(1)
                dve.wait_ge(sem("sin_ready"), 2)
                link(dve.tensor_scalar(tab_q[:, :], tab_q[:, :], SCALE, None, ALU.mult))
                for c in range(2):
                    cs = slice(c * HALF, (c + 1) * HALF)
                    dve.wait_ge(sem("z_done"), 3 + c)
                    dve.tensor_tensor(kr1[64:128, cs], ps[64:128, 6 + c, :], tab_k[64:128, cs], ALU.mult).then_inc(sem("kr_half"), 1)
                    dve.tensor_tensor(kr2[64:128, cs], ps[0:64, 6 + c, :], tab_k[0:64, cs], ALU.mult).then_inc(sem("kr_read"), 1)
                dve.wait_ge(sem("kr_half"), 2)
                dve.wait_ge(sem("kr_read"), 2)
                link(dve.tensor_tensor(kr1[64:128, :], kr1[64:128, :], kr2[64:128, :], ALU.add))
                for i in range(2):
                    link(dve.tensor_copy(k_hi[i][64:128, :], kr1[64:128, :]))
                    link(dve.tensor_tensor(k_lo[i][64:128, :], kr1[64:128, :], k_hi[i][64:128, :].bitcast(F32), ALU.subtract))
                dve.wait_ge(sem("gcol_full"), 32)
                dve.wait_ge(sem("c_raw_ready"), 6)
                for i in range(4):
                    dve.wait_ge(sem("c_std_ready"), i + 1)
                    link(dve.reciprocal(c_rs[:, i, :], c_rs[:, i, :]))
                for i in range(6):
                    cs = slice((i % 2) * HALF, (i % 2 + 1) * HALF)
                    u = i // 2
                    dve.scalar_tensor_tensor(c_raw[:, u, cs], c_raw[:, u, cs], gcol[:, u:u + 1],
                                             c_rs[:, (0 if u == 0 else 2) + i % 2, :], ALU.mult, ALU.mult).then_inc(sem("cn_ready"), 1)
                for i in range(6):
                    cs = slice((i % 2) * HALF, (i % 2 + 1) * HALF)
                    u = i // 2
                    dve.wait_ge(sem("c_hi_ready"), i + 1)
                    dve.tensor_tensor(c_lo[:, u, cs], c_raw[:, u, cs], c_hi[:, u, cs].bitcast(F32), ALU.subtract).then_inc(sem("c_lo_ready"), 1)
            if "A" in on:
                def job_read(h, j):
                    dve.wait_ge(sem("job_done"), 5 * h + j + 1)
                    if j < 2:
                        if h:
                            dve.wait_ge(sem("q_lo_ready"), 2 * h + j - 1)
                        dve.tensor_tensor(q_tmp[j][:, :], ps[:, 7, :], tab_q[:, j * HALF:(j + 1) * HALF], ALU.mult).then_inc(sem("q_tmp_ready"), 1)
                    elif j < 4:
                        cs = slice((j - 2) * HALF, (j - 1) * HALF)
                        dve.wait_ge(sem("kv_hi_ready"), 3 * h + j - 1)
                        dve.tensor_tensor(k_lo[h % 2][0:64, cs], ps[0:64, 7, :], k_hi[h % 2][0:64, cs].bitcast(F32), ALU.subtract).then_inc(sem("kv_lo_ready"), 1)
                    else:
                        dve.wait_ge(sem("kv_hi_ready"), 3 * h + 3)
                        dve.tensor_tensor(v_lo[h % 2][:, :, :].rearrange("p t c -> p (t c)"), ps[:, 7, :],
                                          v_hi[h % 2][:, :, :].rearrange("p t c -> p (t c)").bitcast(F32), ALU.subtract).then_inc(sem("kv_lo_ready"), 1)

                def row_max(s):
                    n = (s % NT + 1) * P
                    dve.wait_ge(sem("s_done"), s + 1)
                    b = 2 * (s % 2)
                    dve.tensor_reduce(negm[:, s:s + 1], ps[:, b:b + 2, :].rearrange("p b c -> p (b c)")[:, 0:n], AX, ALU.max,
                                      negate=True).then_inc(sem("max_ready"), 1)

                def o_rows(s):
                    h, i = divmod(s, NT)
                    dve.wait_ge(sem("exp_done"), s + 1)
                    dve.reciprocal(rl[:, s:s + 1], lsum[:, s:s + 1]).then_inc(sem("rl_ready"), 1)
                    dve.wait_ge(sem("rl_ready"), s + 1)
                    dve.wait_ge(sem("pv_done"), s + 1)
                    dve.tensor_scalar(o_tok[:, i, h * VH:(h + 1) * VH], ps[:, 6, i * VH:(i + 1) * VH], rl[:, s:s + 1], None,
                                      ALU.mult).then_inc(sem("o_ready"), 1)

                for j in range(5):
                    job_read(0, j)
                row_max(0)
                for s in range(NQ):
                    h, i = divmod(s, NT)
                    if s + 1 < NQ:
                        row_max(s + 1)
                    if s:
                        o_rows(s - 1)
                    c0 = chunks_through(s - 1) if s else 0
                    for c in range(i // 4 + 1):
                        w = min(4, i + 1 - 4 * c)
                        cc = c0 + c
                        dve.wait_ge(sem("pt_hi_ready"), cc + 1)
                        dve.tensor_tensor(pt_lo[cc % 4][:, 0:w, :].rearrange("p a b -> p (a b)"), ps[:, 4 + cc % 2, 0:w * P],
                                          pt_hi[cc % 4][:, 0:w, :].rearrange("p a b -> p (a b)").bitcast(F32), ALU.subtract).then_inc(sem("pt_lo_ready"), 1)
                    if i < 5 and h + 1 < HEADS:
                        job_read(h + 1, i)
                o_rows(NQ - 1)
            if "O" in on:
                for t in range(NT):
                    ts = slice(t * P, (t + 1) * P)
                    dve.wait_ge(sem("ot_hi_ready"), t + 1)
                    dve.tensor_tensor(ot_lo[:, :, ts], ps[:, t % 4, :].rearrange("p (k c) -> p k c", c=P),
                                      ot_hi[:, :, ts].bitcast(F32), ALU.subtract).then_inc(sem("ot_lo_ready"), 1)
            if "L" in on:
                dve.wait_ge(sem("spraw_full"), 16)
                dve.memset(sp_raw[0:CHUNK, :, CHUNK:P], 0.0).then_inc(sem("sp_masked"), 1)
                dve.wait_ge(sem("sp_hi_ready"), 1)
                dve.tensor_tensor(sp_lo[:, :, :], ps[:, 4:6, :].rearrange("p b (g c) -> p (b g) c", c=P),
                                  sp_hi[:, :, :].bitcast(F32), ALU.subtract).then_inc(sem("sp_lo_ready"), 1)
                dve.wait_ge(sem("ln_full"), 64)

                def norm_v(t):
                    bank = ps[:, 6 + t % 2, :]
                    dve.wait_ge(sem("v_tr"), t + 1)
                    link(dve.bn_stats(bnst[:, t, :], bank))
                    dve.bn_aggr(bnag[:, t, :], bnst[:, t, :]).then_inc(sem("bn_ready"), 1)
                    dve.wait_ge(sem("ln_std_ready"), t + 1)
                    link(dve.reciprocal(rstd[:, NT + t:NT + t + 1], std[:, NT + t:NT + t + 1]))
                    if t >= 2:
                        dve.wait_ge(sem("vn_lo_ready"), t - 1)
                    ins = dve.tensor_scalar(ln_t[t % 2][:, :], bank, bnag[:, t, 0:1], rstd[:, NT + t:NT + t + 1],
                                            ALU.subtract, ALU.mult)
                    ins.then_inc(sem("ln_read"), 1)
                    dve.wait_ge(sem("ln_read"), t + 1)
                    link(dve.tensor_tensor(ln_t[t % 2][:, :], ln_t[t % 2][:, :], ln_g[:, :], ALU.mult))
                    dve.tensor_tensor(ln_t[t % 2][:, :], ln_t[t % 2][:, :], ln_b[:, :], ALU.add).then_inc(sem("ln_ready"), 1)
                    dve.wait_ge(sem("vn_hi_ready"), t + 1)
                    dve.tensor_tensor(vn_lo[t % 2][:, :], ln_t[t % 2][:, :], vn_hi[t % 2][:, :].bitcast(F32), ALU.subtract).then_inc(sem("vn_lo_ready"), 1)

                def gate_u(t):
                    ts = slice(t * P, (t + 1) * P)
                    dve.wait_ge(sem("sp_done"), t + 1)
                    if t >= 2:
                        dve.wait_ge(sem("s_lo_ready"), t - 1)
                    src = ps[:, 2 * (t % 2):2 * (t % 2) + 2, :].rearrange("p b (q h i) -> p (b q) h i", q=2, h=2)
                    for hh in range(2):
                        r = slice(64 * hh, 64 * hh + 64)
                        dve.tensor_tensor(s_t[t % 2][r, :, :], src[r, :, hh, :], sp_b[r, :, :], ALU.add).then_inc(sem("s_read"), 1)
                    dve.wait_ge(sem("s_read"), 2 * t + 2)
                    dve.tensor_tensor(s_t[t % 2][:, :, :], s_t[t % 2][:, :, :], u_t[:, :, ts], ALU.mult).then_inc(sem("s_ready"), 1)

                def gate_low(t):
                    ts = slice(t * P, (t + 1) * P)
                    dve.wait_ge(sem("s_hi_ready"), t + 1)
                    dve.tensor_tensor(st_lo[:, :, ts], s_t[t % 2][:, :, :], st_hi[:, :, ts].bitcast(F32), ALU.subtract).then_inc(sem("s_lo_ready"), 1)

                norm_v(0)
                for t in range(NT):
                    if t + 1 < NT:
                        norm_v(t + 1)
                    gate_u(t)
                    gate_low(t)
            if "M" in on:
                for f in range(KD):
                    for c in range(2):
                        n = 2 * f + c
                        cs = slice(c * HALF, (c + 1) * HALF)
                        dve.wait_ge(sem("unit_done"), 3 * f + 3)
                        dve.wait_ge(sem("sig_a_ready"), n + 1)
                        dve.tensor_tensor(mix[:, f, cs], ps[:, 4 + c, :], mix[:, f, cs], ALU.mult).then_inc(sem("mix_a_ready"), 1)
                        dve.wait_ge(sem("sig_b_ready"), n + 1)
                        link(dve.tensor_tensor(sig_b[c][:, :], ps[:, 6 + c, :], sig_b[c][:, :], ALU.mult))
                        dve.wait_ge(sem("mix_a_ready"), n + 1)
                        dve.tensor_tensor(mix[:, f, cs], mix[:, f, cs], sig_b[c][:, :], ALU.add).then_inc(sem("mix_ready"), 1)
            if "W" in on:
                def mt_low(t):
                    dve.wait_ge(sem("mt_hi_ready"), t + 1)
                    dve.tensor_tensor(mt_lo[t % 2][:, :, :], mix[:, :, t * P:(t + 1) * P], mt_hi[t % 2][:, :, :].bitcast(F32),
                                      ALU.subtract).then_inc(sem("mt_lo_ready"), 1)

                for k in range(KD):
                    dve.wait_ge(sem("wo_hi_ready"), k + 1)
                    dve.tensor_tensor(wo_lo[:, k, :], raw[k % 3][:, :, :].rearrange("p a b -> p (a b)"),
                                      wo_hi[:, k, :].bitcast(F32), ALU.subtract).then_inc(sem("wo_split"), 1)
                    if k < 2:
                        mt_low(k)
                dve.wait_ge(sem("rt_full"), 128)

                def logits(t):
                    dve.wait_ge(sem("rt_done"), t + 1)
                    dve.tensor_tensor(logit[:, t, :], ps[:, 6, 0:NR], b_rt[:, :], ALU.add).then_inc(sem("logit_ready"), 1)

                for t in range(NT):
                    dve.wait_ge(sem("out_done"), t + 1)
                    dve.wait_ge(sem(f"xre_full{t % 2}"), 16 * (t // 2 + 1))
                    dve.tensor_tensor(x2[:, t, :], ps[:, 2 * (t % 2):2 * (t % 2) + 2, :].rearrange("p b c -> p (b c)"),
                                      xre[t % 2][:, :], ALU.add).then_inc(sem("x2_ready"), 1)
                    dve.wait_ge(sem("std2_ready"), t + 1)
                    link(dve.reciprocal(rstd[:, 8 + t:9 + t], std[:, 8 + t:9 + t]))
                    if t >= 2:
                        dve.wait_ge(sem("h2_tr"), t - 1)
                        dve.wait_ge(sem(f"h2_stored{t % 2}"), 16 * (t // 2))
                    dve.scalar_tensor_tensor(h2[t % 2][:, :], x2[:, t, :], rstd[:, 8 + t:9 + t], g_ffn[:, :],
                                             ALU.mult, ALU.mult).then_inc(sem("h2_ready"), 1)
                    if t + 2 < NT:
                        mt_low(t + 2)
                    if t:
                        logits(t - 1)
                logits(NT - 1)
            if "R" in on:
                lg = logit[:, :, 0:G]
                lx = logit[:, :, G:NR].rearrange("p t (g e) -> p t g e", g=G)
                dve.wait_ge(sem("logit_ready"), NT)

                def wide(ap, n):
                    return ap.unsqueeze(2).to_broadcast([P, NT, n])

                link(dve.tensor_copy(iog[:, :, :], iota_row[:, 0:EPG].unsqueeze(1).to_broadcast([P, NT, EPG])))

                def first_max(src, m, n, onehot):
                    link(dve.tensor_reduce(m, src, AX, ALU.max))
                    link(dve.tensor_tensor(cand[:, :, 0:n], src, wide(m, n), ALU.is_lt))
                    link(dve.scalar_tensor_tensor(cand[:, :, 0:n], cand[:, :, 0:n], 64.0, iog[:, :, 0:n], ALU.mult, ALU.add))
                    link(dve.tensor_reduce(sel[:, :], cand[:, :, 0:n], AX, ALU.min))
                    link(dve.tensor_tensor(onehot, cand[:, :, 0:n], wide(sel[:, :], n), ALU.is_equal))

                first_max(lg, mg[:, :], G, og[:, :, :])
                dve.tensor_tensor(ex[:, :, :], lg, wide(mg[:, :], G), ALU.subtract).then_inc(sem("gmax_ready"), 1)
                dve.wait_ge(sem("gexp_ready"), 1)
                link(dve.tensor_reduce(ptop[:, :], ex[:, :, :], AX, ALU.add))
                link(dve.reciprocal(ptop[:, :], ptop[:, :]))
                og4 = og[:, :, :].unsqueeze(3).to_broadcast([P, NT, G, EPG])
                for t in range(NT):
                    dve.tensor_tensor(lprod[:, t], lx[:, t], og4[:, t], ALU.mult).then_inc(sem("lprod_ready"), 1)
                dve.wait_ge(sem("lprod_ready"), NT)
                link(dve.tensor_tensor(le[:, :, :], lprod[:, :, 0, :], lprod[:, :, 1, :], ALU.add))
                link(dve.tensor_tensor(le[:, :, :], le[:, :, :], lprod[:, :, 2, :], ALU.add))
                dve.tensor_tensor(le[:, :, :], le[:, :, :], lprod[:, :, 3, :], ALU.add).then_inc(sem("logit_read"), 1)
                dve.wait_ge(sem("logit_read"), 1)
                first_max(le[:, :, :], m12[:, 0, :], EPG, oh[0][:, :, :])
                link(dve.scalar_tensor_tensor(le[:, :, :], oh[0][:, :, :], -BIG, le[:, :, :], ALU.mult, ALU.add))
                first_max(le[:, :, :], m12[:, 1, :], EPG, oh[1][:, :, :])
                dve.tensor_tensor(gatew[:, 1, :], m12[:, 1, :], m12[:, 0, :], ALU.subtract).then_inc(sem("ediff_ready"), 1)
                for k in range(2):
                    for t in range(NT):
                        ins = dve.tensor_tensor(oe[k][:, t], oh[k][:, t].unsqueeze(1).to_broadcast([P, G, EPG]), og4[:, t], ALU.mult)
                        ins.then_inc(sem("oeh_ready"), 1)
                dve.wait_ge(sem("oeh_ready"), 2 * NT)
                oef = [oe[k][:, :, :, :].rearrange("p t g e -> p t (g e)") for k in range(2)]
                link(dve.tensor_tensor(oe_b[:, :, :], oef[0], oef[1], ALU.add))
                link(dve.memset(cum_b[:, 0, :], 0.0))
                for t in range(NT):
                    link(dve.tensor_tensor(cum_b[:, t + 1, :], cum_b[:, t, :], oe_b[:, t, :], ALU.add))
                dve.memset(cmp7[:, :], 0.0).then_inc(sem("oe_ready"), 1)
                dve.wait_ge(sem("gexp_ready"), 2)
                link(dve.tensor_scalar(gatew[:, 0, :], gatew[:, 1, :], 1.0, None, ALU.add))
                link(dve.reciprocal(gatew[:, 0, :], gatew[:, 0, :]))
                link(dve.tensor_tensor(gatew[:, 0, :], gatew[:, 0, :], ptop[:, :], ALU.mult))
                link(dve.tensor_tensor(gatew[:, 1, :], gatew[:, 1, :], gatew[:, 0, :], ALU.mult))
                dve.wait_ge(sem("rank_done"), 1)
                link(dve.tensor_copy(rank_e[:, :, :].rearrange("p t e -> p (t e)"), ps[:, 0, 0:NT * NE]))
                link(dve.tensor_copy(cnt[:, :], ps[:, 1, 0:NE]))
                link(dve.tensor_scalar(novf[:, :], cnt[:, :], float(P), None, ALU.is_gt))
                for j in range(2, 8):
                    link(dve.scalar_tensor_tensor(novf[:, :], cnt[:, :], float(P * j), novf[:, :], ALU.is_gt, ALU.add))
                link(dve.tensor_tensor_scan(incl[:, :], ones[:, 0:NE], novf[:, :], 0.0, ALU.mult, ALU.add))
                link(dve.tensor_tensor(ostart[:, :], incl[:, :], novf[:, :], ALU.subtract))
                for k in range(2):
                    for dst, src in ((rk, rank_e[:, :, :]),
                                     (osk, ostart[:, :].unsqueeze(1).to_broadcast([P, NT, NE])),
                                     (eid, iota_row[:, 0:NE].unsqueeze(1).to_broadcast([P, NT, NE]))):
                        link(dve.tensor_tensor(prod[:, :, :], oef[k], src, ALU.mult))
                        link(dve.tensor_reduce(dst[:, k, :], prod[:, :, :], AX, ALU.add))
                link(dve.tensor_scalar(ob[:, :, :], rk[:, :, :], float(P), None, ALU.is_ge))
                link(dve.tensor_copy(obc[:, :, :], ob[:, :, :]))
                for j in range(2, 8):
                    link(dve.scalar_tensor_tensor(ob[:, :, :], rk[:, :, :], float(P * j), ob[:, :, :], ALU.is_ge, ALU.add))
                link(dve.scalar_tensor_tensor(rk[:, :, :], ob[:, :, :], -float(P), rk[:, :, :], ALU.mult, ALU.add))
                link(dve.scalar_tensor_tensor(blk_k[:, :, :], ob[:, :, :], float(NE - 1), osk[:, :, :], ALU.add, ALU.add))
                link(dve.tensor_tensor(blk_k[:, :, :], blk_k[:, :, :], eid[:, :, :], ALU.subtract))
                link(dve.tensor_tensor(blk_k[:, :, :], blk_k[:, :, :], obc[:, :, :], ALU.mult))
                link(dve.tensor_tensor(blk_k[:, :, :], blk_k[:, :, :], eid[:, :, :], ALU.add))
                for k in range(2):
                    link(dve.tensor_scalar(val[:, k, :], iota_row[:, 0:NT], float(P), float(k * T + 1), ALU.mult, ALU.add))
                link(dve.tensor_scalar(val[:, :, :], val[:, :, :], iota_col[:, :], None, ALU.add))
                for i in range(2 * NT):
                    k, t = divmod(i, NT)
                    if i >= 2:
                        dve.wait_ge(sem("sel_used"), i - 1)
                    link(dve.tensor_scalar(sel_a[i % 2][:, :], iota_row[:, :], rk[:, k, t:t + 1], None, ALU.is_equal))
                    dve.tensor_scalar(sel_b[i % 2][:, :], iota_row[:, 0:NBLK], blk_k[:, k, t:t + 1], val[:, k, t:t + 1],
                                      ALU.is_equal, ALU.mult).then_inc(sem("sel_ready"), 1)
                dve.wait_ge(sem("sel_used"), 2 * NT)
                link(dve.tensor_scalar(tab0[:, :], ps[:, 2, 0:NBLK], 0.0, FAR, ALU.is_equal, ALU.mult))
                link(dve.scalar_tensor_tensor(tabf[:, :], ps[:, 2, 0:NBLK], -1.0, tab0[:, :], ALU.add, ALU.add))
                link(dve.tensor_copy(yidx[:, :], tabf[:, :]))
                link(dve.tensor_scalar(tab0[:, :], tabf[:, :], float(T), -float(T), ALU.is_ge, ALU.mult))
                link(dve.tensor_tensor(tabf[:, :], tabf[:, :], tab0[:, :], ALU.add))
                link(dve.tensor_copy(xidx[:, :], tabf[:, :]))
                link(dve.tensor_copy(ovf_n[0:1, 0:1], incl[0:1, NE - 1:NE]))
                link(dve.tensor_tensor(ovc[0:1, :, :], incl[0:1, :].unsqueeze(1).to_broadcast([1, 16, NE]),
                                       iota_row[0:1, 0:16].unsqueeze(2).to_broadcast([1, 16, NE]), ALU.is_le))
                link(dve.tensor_reduce(ovf[0:1, :], ovc[0:1, :, :], AX, ALU.add))
                link(dve.tensor_scalar(ovf[0:1, :], ovf[0:1, :], float(NE - 1), None, ALU.min))
                dve.tensor_copy(ovf_e[0:1, :], ovf[0:1, :]).then_inc(sem("tab_read"), 1)
            if "E" in on:
                dve.sem_inc(sem("hid_ready"), 1)
                dve.sem_inc(sem("y_ready0"), 2)
                dve.sem_inc(sem("y_ready1"), 2)
                with dve.Fori(0, NE // 4) as it:
                    for j in range(4):
                        n, q = it * 2 + j // 2, j % 2
                        dve.wait_ge(sem("sg_ready"), n * 2 + q + 1)
                        dve.wait_ge(sem("hid_tr"), n * 2 + q + 1)
                        dve.tensor_tensor(hid[q][:, :], ps[:, 2, DE:2 * DE], sg[q][:, :], ALU.mult).then_inc(sem("hid_ready"), 1)
                        dve.wait_ge(sem(f"we_used{j}"), it + 1 + 1)
                        dve.wait_ge(sem(f"y_sent{q}"), n * 16 + 16)
                        dve.tensor_copy(y[q][:, HALF:D], ps[:, 5 + 2 * q, :]).then_inc(sem(f"y_ready{q}"), 1)
                n_ovf = dve.value_load(ovf_n[0:1, 0:1], min_val=0, max_val=NOVF)
                with dve.If(n_ovf > 0):
                    with dve.Fori(0, n_ovf) as b:
                        dve.wait_ge(sem("sg_ready"), b + NE + 1)
                        dve.wait_ge(sem("hid_tr"), b + NE + 1)
                        dve.tensor_tensor(hid[0][:, :], ps[:, 2, DE:2 * DE], sg[0][:, :], ALU.mult).then_inc(sem("hid_ready"), 1)
                        dve.wait_ge(sem("we_used0"), b + NE // 4 + 1 + 1)
                        dve.wait_ge(sem("y_sent0"), b * 16 + 16 * (NE // 2) + 16)
                        dve.tensor_copy(y[0][:, HALF:D], ps[:, 5, :]).then_inc(sem("y_ready0"), 1)
            if "C" in on:
                dve.wait_ge(sem("gfin_full"), 16)
                for t in range(NT):
                    dve.wait_ge(sem(f"yin_full{t % 2}"), 32 * (t // 2 + 1))
                    if t >= 2:
                        dve.wait_ge(sem("res_ready"), t - 1)
                    link(dve.scalar_tensor_tensor(acc[t % 2][:, :], yin[t % 2][:, 0, :], gatew[:, 0, t:t + 1], x2[:, t, :], ALU.mult, ALU.add))
                    dve.scalar_tensor_tensor(acc[t % 2][:, :], yin[t % 2][:, 1, :], gatew[:, 1, t:t + 1], acc[t % 2][:, :],
                                             ALU.mult, ALU.add).then_inc(sem("acc_ready"), 1)
                    dve.wait_ge(sem("std3_ready"), t + 1)
                    link(dve.reciprocal(rstd[:, 16 + t:17 + t], std[:, 16 + t:17 + t]))
                    if t >= 2:
                        dve.wait_ge(sem(f"res_stored{t % 2}"), 16 * (t // 2))
                    dve.scalar_tensor_tensor(res[t % 2][:, :], acc[t % 2][:, :], rstd[:, 16 + t:17 + t], g_fin[:, :],
                                             ALU.mult, ALU.mult).then_inc(sem("res_ready"), 1)

        @block.gpsimd
        def _(pool):
            pool.iota(iota_row[:, :], [[1, P]], base=0, channel_multiplier=0,
                      allow_small_or_imprecise_dtypes=True).then_inc(sem("iota_ready"), 1)
            pool.iota(iota_col[:, :], [[0, 1]], base=0, channel_multiplier=1,
                      allow_small_or_imprecise_dtypes=True).then_inc(sem("iota_ready"), 1)
            if "Z" in on:
                split_units(pool, 0, NZ)
            if "A" in on:
                def head_split(h):
                    pool.wait_ge(sem(f"hraw_full{h % 2}"), 80 * (h // 2 + 1))
                    if h >= 2:
                        pool.wait_ge(sem("job_done"), 5 * (h - 1))
                    pool.tensor_copy(h_hi[h % 2][:, :], h_raw[h % 2][:, :]).then_inc(sem("hw_hi"), 1)
                    pool.wait_ge(sem("hw_hi"), h + 1)
                    pool.tensor_tensor(h_lo[h % 2][:, :], h_raw[h % 2][:, :], h_hi[h % 2][:, :].bitcast(F32),
                                       ALU.subtract).then_inc(sem("hw_split"), 1)

                head_split(0)
                for h in range(HEADS):
                    for j in range(2):
                        pool.wait_ge(sem("q_hi_ready"), 2 * h + j + 1)
                        pool.tensor_tensor(q_lo[h % 2][:, j * HALF:(j + 1) * HALF], q_tmp[j][:, :],
                                           q_hi[h % 2][:, j * HALF:(j + 1) * HALF].bitcast(F32), ALU.subtract).then_inc(sem("q_lo_ready"), 1)
                    if h + 1 < HEADS:
                        head_split(h + 1)
            if "U" in on:
                split_units(pool, NZ, NZ + NU)
            if "M" in on:
                split_units(pool, NZ + NU, NZ + NU + NM)
            if "E" in on:
                x_copies, y_copies = pool.alloc_register("x_copies"), pool.alloc_register("y_copies")
                pool.reg_mov(x_copies, 0)
                pool.reg_mov(y_copies, 0)
                last_token, last_row = pool.to_reg(T - 1), pool.to_reg(2 * T - 1)

                def gather(blk, j):
                    pool.tensor_copy(xcol[j][:, :], xidx[:, blk]).then_inc(sem("xcol_ready"), 1)
                    pool.reg_add(x_copies, x_copies, 1)
                    pool.wait_ge(sem("tab_read"), 1)
                    pool.wait_ge(sem("xcol_ready"), x_copies)
                    pool.indirect_dma_start(xs[j][:, :], None, h2_dram, bass.IndirectOffsetOnAxis(xcol[j][:, :], 0),
                                            bounds_check=last_token, oob_is_err=False).then_inc(sem(f"xs_full{j}"), 16)

                def scatter(blk, j, sent):
                    pool.wait_ge(sem(f"y_sent{j}"), sent * 16 + 16)
                    pool.tensor_copy(ycol[j][:, :], yidx[:, blk]).then_inc(sem("ycol_ready"), 1)
                    pool.reg_add(y_copies, y_copies, 1)
                    pool.wait_ge(sem("tab_read"), 1)
                    pool.wait_ge(sem("ycol_ready"), y_copies)
                    pool.indirect_dma_start(y_dram, bass.IndirectOffsetOnAxis(ycol[j][:, :], 0), y[j][:, :], None,
                                            bounds_check=last_row, oob_is_err=False).then_inc(sem(f"y_sent{j}"), 16)

                pool.wait_ge(sem("out_done"), NT)
                for j in range(2):
                    pool.memset(xs[j][:, :], 0.0).then_inc(sem("xs_clear"), 1)
                pool.wait_ge(sem("xs_clear"), 2)
                for i in range(2):
                    pool.wait_ge(sem(f"h2_stored{i}"), 16 * NT // 2)
                pool.wait_ge(sem("tab_read"), 1)
                gather(slice(0, 1), 0)
                for j in range(2):
                    pool.dma_start(ycol[j][:, :], yidx[:, j:j + 1]).then_inc(sem(f"y_sent{j}"), 16)
                with pool.Fori(0, NE // 4) as it:
                    for j in range(4):
                        q, e = j % 2, it * 4 + j
                        pool.wait_ge(sem("xs_tr"), e + 1)
                        gather(bass.ds(e + 1, 1), 1 - q)
                        pool.wait_ge(sem(f"y_ready{q}"), (it * 2 + j // 2) * 2 + 2 + 2)
                        scatter(bass.ds(e, 1), q, it * 2 + j // 2)
                n_ovf = pool.value_load(ovf_n[0:1, 0:1], min_val=0, max_val=NOVF)
                with pool.If(n_ovf > 0):
                    with pool.Fori(0, n_ovf) as b:
                        pool.wait_ge(sem("xs_tr"), b + NE + 1 + 1)
                        gather(bass.ds(b + NE + 1, 1), 0)
                        pool.wait_ge(sem("y_ready0"), b * 2 + NE + 2 + 2)
                        scatter(bass.ds(b + NE, 1), 0, b + NE // 2)
                    pool.wait_ge(sem("y_sent0"), n_ovf * 16 + 16 * (NE // 2) + 16)
                pool.wait_ge(sem("y_sent0"), 16 * (NE // 2) + 16)
                pool.wait_ge(sem("y_sent1"), 16 * (NE // 2) + 16)
                pool.memset(junk3[:, 0:1], 0.0).then_inc(sem("y_stored_all"), 1)


_INS = ["x", "positions", "g_attn_norm", "w_in", "g_cq", "w_uq", "g_ckv", "w_uk", "w_uv", "w_o_attn", "sgu_gain",
        "sgu_bias", "w_spatial", "b_spatial", "w_o_sgu", "w_out", "g_ffn_norm", "w_router_group", "b_router_group",
        "w_router_expert", "b_router_expert", "w_exp_gate", "w_exp_up", "w_exp_down", "g_final"]


def kernel(**inputs):
    import numpy as _np
    import concourse.bacc as _bacc
    from concourse import mybir as _mybir
    from concourse.bass_utils import run_bass_kernel_spmd as _run

    nc = _bacc.Bacc("TRN2", target_bir_lowering=False, num_devices=1)
    arrays, args = {}, {}
    for name in _INS:
        arr = _np.ascontiguousarray(inputs[name])
        arrays[f"in_{name}_dram"] = arr
        args[name] = nc.dram_tensor(f"in_{name}_dram", arr.shape, _mybir.dt.from_np(arr.dtype), kind="ExternalInput").ap()
    c = rope_constants()
    arrays["rope_constants_dram"] = c
    args["rope_constants"] = nc.dram_tensor("rope_constants_dram", c.shape, _mybir.dt.float32, kind="ExternalInput").ap()
    out = nc.dram_tensor("out_0_dram", (1, T, D), _mybir.dt.float32, kind="ExternalOutput").ap()
    build(nc, args, out)
    r = _run(nc, [arrays], core_ids=[0])
    return r.results[0]["out_0_dram"]
```

```python
from contextlib import ExitStack

import numpy as np

import concourse.bass as bass
from concourse import mybir

F32 = mybir.dt.float32
F32R = mybir.dt.float32r
BF16 = mybir.dt.bfloat16
I32 = mybir.dt.int32
U32 = mybir.dt.uint32
ALU = mybir.AluOpType
ACT = mybir.ActivationFunctionType
AX = mybir.AxisListType.X

P = 128
D = 1024
T = 1024
NT = T // P
KD = D // P
HALF = 512
EPS = 1e-6
HEADS, NOPE, ROPE, VH = 8, 64, 32, 64
QR, KVR = 256, 128
SCALE = (NOPE + ROPE) ** -0.5
THETA = 10000.0
SGU = 512
KS = SGU // P
CHUNK = 64
G, EPG = 4, 8
NE = G * EPG
DE = 256
NOVF = 15
NBLK = 48
NR = G + NE
C_UV, C_GATE = QR + KVR + ROPE, QR + KVR + ROPE + 2 * SGU
BIG = 1.0e30
FAR = 8192.0
PI_IN = 3.1415925
TWO_PI = 2 * np.pi
C1 = 6.28125
C2 = float(np.float32(np.floor((TWO_PI - C1) * 2 ** 21) / 2 ** 21))
C3 = float(TWO_PI - C1 - C2)
MAGIC = 1.5 * 2 ** 23
KB = 1024
NQ = 64


def rope_constants():
    f = (np.float32(THETA) ** (-np.arange(0, ROPE, 2, dtype=np.float32) / np.float32(ROPE))).astype(np.float32)
    turn = np.concatenate([-f, f])
    c = np.zeros((P, 8), np.float32)
    c[:64, 1], c[:64, 2] = 0.25, np.pi / 2
    c[64:96, 0], c[64:96, 1], c[64:96, 2] = np.concatenate([f, f]), 0.25, np.pi / 2
    c[96:, 0] = turn
    c[:64, 3] = np.concatenate([turn, turn])
    c[64:, 3], c[64:, 4], c[64:, 5] = np.concatenate([f] * 4), 0.25, np.pi / 2
    return c


def chunks_through(s):
    return sum((i % NT) // 4 + 1 for i in range(s + 1))


def build(nc, a, out, stop_after=None):
    base = 16512

    with ExitStack() as ctx:
        def at(name, kb, shape, dt):
            return nc.alloc_sbuf_tensor_at(name, shape, dt, offset=base + int(kb * KB))

        sems = {}

        def sem(name):
            if name not in sems:
                sems[name] = ctx.enter_context(nc.semaphore(name))
            return sems[name]

        ident = at("ident", 0, [P, P], F32)
        iota_row = at("iota_row", 0.5, [P, P], F32)
        ones = at("ones", 1, [P, P], F32)
        mask_l = at("mask_l", 1.5, [P, P], F32R)
        mask_r = at("mask_r", 2, [P, CHUNK], F32R)
        before = at("before", 2.25, [P, P], BF16)
        ones_b = at("ones_b", 2.5, [P, P], BF16)
        iota_col = at("iota_col", 2.75, [P, 1], F32)
        epst = at("epst", 2.78125, [P, 1], F32)
        cst = at("cst", 2.8125, [P, 8], F32)
        gcol = at("gcol", 2.875, [P, 3], F32)
        ssq = at("ssq", 3, [P, 3 * NT], F32)
        std = at("std", 3.125, [P, 3 * NT], F32)
        rstd = at("rstd", 3.25, [P, 3 * NT], F32)
        negm = at("negm", 3.5, [P, NQ], F32)
        lsum = at("lsum", 3.75, [P, NQ], F32)
        rl = at("rl", 4, [P, NQ], F32)
        bnst = at("bnst", 4.25, [P, NT, 6], F32)
        bnag = at("bnag", 4.5, [P, NT, 2], F32)
        gatew = at("gatew", 4.75, [P, 2, NT], F32)
        yidx = at("yidx", 5, [P, NBLK], U32)
        xidx = at("xidx", 5.25, [P, NBLK], U32)
        xcol = [at(f"xcol{i}", 5.75 + i / 32, [P, 1], U32) for i in range(4)]
        ycol = [at(f"ycol{i}", 5.875 + i / 32, [P, 1], U32) for i in range(2)]
        ovf_e = at("ovf_e", 5.5, [1, 16], I32)
        ovf_n = at("ovf_n", 5.625, [1, 8], I32)

        raw = [at(f"raw{i}", 8 + 4 * i, [P, KD, P], F32) for i in range(3)]
        w_hi = [at(f"w_hi{i}", 20 + 8 * i, [P, KD, P], F32R) for i in range(3)]
        w_lo = [at(f"w_lo{i}", 24 + 8 * i, [P, KD, P], F32R) for i in range(3)]
        ht_hi = at("ht_hi", 44, [P, KD, T], F32R)
        ht_lo = at("ht_lo", 76, [P, KD, T], F32R)
        xin = [at(f"xin{i}", 108 + 4 * i, [P, D], F32) for i in range(4)]
        hrow = [at(f"hrow{i}", 124 + 4 * i, [P, D], F32) for i in range(2)]
        g_attn = at("g_attn", 176, [P, D], F32)
        junk = at("junk", 180, [P, D], F32)
        pos_i = at("pos_i", 200, [P, T], I32)
        ang = at("ang", 160, [P, T], F32)
        turns = at("turns", 164, [P, T], F32)
        tab_q = at("tab_q", 132, [P, T], F32)
        tab_k = at("tab_k", 168, [P, T], F32)
        c_raw = at("c_raw", 136, [P, 3, T], F32)
        c_sq = at("c_sq", 148, [P, 3, T], F32)
        c_rs = at("c_rs", 160, [P, 4, HALF], F32)
        kr1 = at("kr1", 192, [P, T], F32)
        kr2 = at("kr2", 196, [P, T], F32)
        c_hi = at("c_hi", 108, [P, 3, T], F32R)
        c_lo = at("c_lo", 120, [P, 3, T], F32R)
        h_raw = [at(f"h_raw{i}", 8 + 1.5 * i, [P, 384], F32) for i in range(2)]
        h_hi = [at(f"h_hi{i}", 11 + 3 * i, [P, 384], F32R) for i in range(2)]
        h_lo = [at(f"h_lo{i}", 12.5 + 3 * i, [P, 384], F32R) for i in range(2)]
        pt_hi = [at(f"pt_hi{i}", 17 + 4 * i, [P, 4, P], F32R) for i in range(4)]
        pt_lo = [at(f"pt_lo{i}", 19 + 4 * i, [P, 4, P], F32R) for i in range(4)]
        q_tmp = [at(f"q_tmp{i}", 33 + 2 * i, [P, HALF], F32) for i in range(2)]
        q_hi = [at(f"q_hi{i}", 136 + 8 * i, [P, T], F32R) for i in range(2)]
        q_lo = [at(f"q_lo{i}", 140 + 8 * i, [P, T], F32R) for i in range(2)]
        v_hi = [at(f"v_hi{i}", 152 + 4 * i, [P, NT, VH], F32R) for i in range(2)]
        v_lo = [at(f"v_lo{i}", 154 + 4 * i, [P, NT, VH], F32R) for i in range(2)]
        o_tok = at("o_tok", 160, [P, NT, HEADS * VH], F32)
        k_hi = [at(f"k_hi{i}", 176 + 8 * i, [P, T], F32R) for i in range(2)]
        k_lo = [at(f"k_lo{i}", 180 + 8 * i, [P, T], F32R) for i in range(2)]
        prob = [at(f"prob{i}", 192 + 4 * i, [P, T], F32) for i in range(2)]
        ot_hi = at("ot_hi", 108, [P, KS, T], F32R)
        ot_lo = at("ot_lo", 124, [P, KS, T], F32R)
        st_hi = at("st_hi", 140, [P, KS, T], F32R)
        st_lo = at("st_lo", 156, [P, KS, T], F32R)
        u_t = at("u_t", 172, [P, KS, T], F32)
        v_t = at("v_t", 188, [P, KS, T], F32)
        sp_hi = at("sp_hi", 8, [P, 8, P], F32R)
        sp_lo = at("sp_lo", 12, [P, 8, P], F32R)
        sp_raw = at("sp_raw", 16, [P, 8, P], F32)
        ln_g = at("ln_g", 20, [P, SGU], F32)
        ln_b = at("ln_b", 22, [P, SGU], F32)
        vn_hi = [at(f"vn_hi{i}", 24 + 4 * i, [P, SGU], F32R) for i in range(2)]
        vn_lo = [at(f"vn_lo{i}", 26 + 4 * i, [P, SGU], F32R) for i in range(2)]
        ln_t = [at(f"ln_t{i}", 32 + 2 * i, [P, SGU], F32) for i in range(2)]
        s_t = [at(f"s_t{i}", 36 + 2 * i, [P, KS, P], F32) for i in range(2)]
        sp_b = at("sp_b", 40, [P, KS, P], F32)
        mix = at("mix", 172, [P, KD, T], F32)
        sig_b = [at("sig_b0", 204, [P, HALF], F32), at("sig_b1", 6, [P, HALF], F32)]
        wo_hi = at("wo_hi", 44, [P, KD, D], F32R)
        wo_lo = at("wo_lo", 76, [P, KD, D], F32R)
        mt_hi = [at(f"mt_hi{i}", 108 + 8 * i, [P, KD, P], F32R) for i in range(2)]
        mt_lo = [at(f"mt_lo{i}", 112 + 8 * i, [P, KD, P], F32R) for i in range(2)]
        xre = [at(f"xre{i}", 124 + 4 * i, [P, D], F32) for i in range(2)]
        x2 = at("x2", 132, [P, NT, D], F32)
        h2 = [at(f"h2{i}", 164 + 4 * i, [P, D], F32) for i in range(2)]
        h2t = [at(f"h2t{i}", 20 + 4 * i, [P, KD, P], F32) for i in range(2)]
        g_ffn = at("g_ffn", 28, [P, D], F32)
        w_rt = at("w_rt", 32, [P, KD, NR], F32)
        b_rt = at("b_rt", 33.25, [P, NR], F32)
        junk2 = at("junk2", 34, [P, D], F32)
        r_at = [172.0]

        def scratch(name, shape, dt=F32):
            n = int(np.prod(shape[1:])) * (2 if dt is BF16 else 4)
            t = at(name, r_at[0], shape, dt)
            r_at[0] += -(-n // 32) * 32 / KB
            return t

        logit = at("logit", 38.5, [P, NT, NR], F32)
        iog = scratch("iog", [P, NT, EPG])
        mg = scratch("mg", [P, NT])
        cand = scratch("cand", [P, NT, EPG])
        sel = scratch("sel", [P, NT])
        og = scratch("og", [P, NT, G])
        ex = scratch("ex", [P, NT, G])
        ptop = scratch("ptop", [P, NT])
        lprod = scratch("lprod", [P, NT, G, EPG])
        le = scratch("le", [P, NT, EPG])
        m12 = scratch("m12", [P, 2, NT])
        oh = [scratch(f"oh{k}", [P, NT, EPG]) for k in range(2)]
        oe = [scratch(f"oe{k}", [P, NT, G, EPG]) for k in range(2)]
        oe_b = scratch("oe_b", [P, NT, NE], BF16)
        cum_b = scratch("cum_b", [P, NT + 1, NE], BF16)
        cum = scratch("cum", [P, NT, NE])
        rank_e = scratch("rank_e", [P, NT, NE])
        prod = scratch("prod", [P, NT, NE])
        cnt = scratch("cnt", [P, NE])
        cmp7 = scratch("cmp7", [P, NE])
        novf = scratch("novf", [P, NE])
        incl = scratch("incl", [P, NE])
        ostart = scratch("ostart", [P, NE])
        rk = scratch("rk", [P, 2, NT])
        eid = scratch("eid", [P, 2, NT])
        osk = scratch("osk", [P, 2, NT])
        ob = scratch("ob", [P, 2, NT])
        obc = scratch("obc", [P, 2, NT])
        blk_k = scratch("blk_k", [P, 2, NT])
        val = scratch("val", [P, 2, NT])
        sel_a = [scratch(f"sel_a{i}", [P, P], F32R) for i in range(2)]
        sel_b = [scratch(f"sel_b{i}", [P, NBLK], F32R) for i in range(2)]
        tabf = scratch("tabf", [P, NBLK])
        tab0 = scratch("tab0", [P, NBLK])
        ovc = scratch("ovc", [1, 16, NE])
        ovf = scratch("ovf", [1, 16])
        assert r_at[0] < 188, r_at
        raw_e = [[at(f"raw_e{g}{q}", 8 + 8 * (3 * q + g), [P, 2048], F32) for q in range(2)] for g in range(3)]
        we_hi = [at(f"we_hi{i}", 56 + 16 * i, [P, 2048], F32R) for i in range(4)]
        we_lo = [at(f"we_lo{i}", 64 + 16 * i, [P, 2048], F32R) for i in range(4)]
        xs = [at(f"xs{i}", (128, 188, 192, 196)[i], [P, D], F32) for i in range(4)]
        xst_hi = [at(f"xst_hi{i}", (120, 180)[i], [P, KD, P], F32R) for i in range(2)]
        xst_lo = [at(f"xst_lo{i}", (124, 184)[i], [P, KD, P], F32R) for i in range(2)]
        sg = at("sg", 200, [P, DE], F32)
        hid = at("hid", 201, [P, DE], F32)
        hidt_hi = at("hidt_hi", 202, [P, 2, P], F32R)
        hidt_lo = at("hidt_lo", 203, [P, 2, P], F32R)
        y = [at(f"y{i}", 164 + 4 * i, [P, D], F32) for i in range(2)]
        yin = [at(f"yin{i}", 8 + 8 * i, [P, 2, D], F32) for i in range(2)]
        g_fin = at("g_fin", 104, [P, D], F32)
        acc = [at(f"acc{i}", 24 + 4 * i, [P, D], F32) for i in range(2)]
        res = [at(f"res{i}", 32 + 4 * i, [P, D], F32) for i in range(2)]
        junk3 = at("junk3", 40, [P, D], F32)

        ps = ctx.enter_context(nc.psum_tensor("ps", [P, 8, HALF], F32))

        h2_dram = nc.dram_tensor("h2_dram", [T, D], F32, kind="Internal").ap()
        y_dram = nc.dram_tensor("y_dram", [2 * T, D], F32, kind="Internal").ap()

        ctx.enter_context(nc.allow_non_contiguous_dma(reason="small columns and weight slices"))
        block = ctx.enter_context(nc.Block())

        w_in = a["w_in"][0].rearrange("(k p) n -> p k n", p=P)
        w_oa = a["w_o_attn"][0].rearrange("(k p) n -> p k n", p=P)
        w_os = a["w_o_sgu"][0].rearrange("(k p) n -> p k n", p=P)
        w_out = a["w_out"][0].rearrange("(k p) n -> p k n", p=P)
        w_uq = a["w_uq"][0].rearrange("(k p) n -> p k n", p=P)
        x_d = a["x"][0].rearrange("(t p) d -> t p d", p=P)
        out_d = out[0].rearrange("(t p) d -> t p d", p=P)
        wg_d = a["w_exp_gate"][0].rearrange("e (p k) f -> e p (k f)", p=P)
        wu_d = a["w_exp_up"][0].rearrange("e (p k) f -> e p (k f)", p=P)
        wd_d = a["w_exp_down"][0].rearrange("e (p j) d -> e p (j d)", p=P)

        NZ, NU, NM = 4, 8, 3 * KD

        def unit_loads(n):
            r = raw[n % 3]
            if n == 0:
                return [(r[:, :, :], w_in[:, :, QR:QR + KVR])]
            if n == 1:
                c = QR + KVR
                hr = ROPE // 2
                return ([(r[:, :, q * 32:q * 32 + hr], w_in[:, :, c + hr:c + ROPE]) for q in range(2)]
                        + [(r[:, :, q * 32 + hr:q * 32 + 32], w_in[:, :, c:c + hr]) for q in range(2)]
                        + [(r[:, :, q * 32:q * 32 + 32], w_in[:, :, c:c + ROPE]) for q in (2, 3)])
            if n < NZ:
                return [(r[:, :, :], w_in[:, :, (n - 2) * P:(n - 1) * P])]
            if n < NZ + NU:
                c = C_UV + (n - NZ) * P
                return [(r[:, :, :], w_in[:, :, c:c + P])]
            f, kind = divmod(n - NZ - NU, 3)
            if kind < 2:
                c = C_GATE + kind * D + f * P
                return [(r[:, :, :], w_in[:, :, c:c + P])]
            return [(r[:, 0:KS, :], w_oa[:, :, f * P:(f + 1) * P]),
                    (r[:, KS:, :], w_os[:, :, f * P:(f + 1) * P])]

        raw_count = [0, 0, 0]
        raw_value = {}
        for n in range(NZ + NU + NM):
            raw_count[n % 3] += 16 * len(unit_loads(n))
            raw_value[n] = raw_count[n % 3]

        def unit_used(eng, n):
            if n < NZ:
                eng.wait_ge(sem("z_done"), 2 * n + 2)
            elif n < NZ + NU:
                eng.wait_ge(sem("uv_done"), 2 * (n - NZ) + 2)
            else:
                eng.wait_ge(sem("unit_done"), n - NZ - NU + 1)

        def load_units(sp, lo, hi):
            for n in range(lo, hi):
                if n >= 3:
                    sp.wait_ge(sem("w_split"), n - 2)
                for dst, src in unit_loads(n):
                    sp.dma_start(dst, src).then_inc(sem(f"raw_full{n % 3}"), 16)

        def split_units(pool, lo, hi):
            for n in range(lo, hi):
                pool.wait_ge(sem(f"raw_full{n % 3}"), raw_value[n])
                if n >= 3:
                    unit_used(pool, n - 3)
                pool.tensor_copy(w_hi[n % 3][:, :, :], raw[n % 3][:, :, :]).then_inc(sem("w_hi_done"), 1)
                pool.wait_ge(sem("w_hi_done"), n + 1)
                pool.tensor_tensor(w_lo[n % 3][:, :, :], raw[n % 3][:, :, :],
                                   w_hi[n % 3][:, :, :].bitcast(F32), ALU.subtract).then_inc(sem("w_split"), 1)

        def mm3(pe, dst, st, mv, first, last):
            pe.matmul(dst, st[0], mv[0], start=first, stop=False)
            pe.matmul(dst, st[0], mv[1], start=False, stop=False)
            return pe.matmul(dst, st[1], mv[0], start=False, stop=last)

        def place(g, e):
            return (3 * e - 1, 3 * e + 1, 3 * e + 3)[g] if not (isinstance(e, int) and e == 0 and g == 0) else 0

        def wait(eng, name, value):
            if not (isinstance(value, int) and value <= 0):
                eng.wait_ge(sem(name), value)

        def experts(eng, body):
            for j in range(4):
                body(j, j, lambda n: True)
            with eng.Fori(1, NE // 4 - 1) as it:
                for j in range(4):
                    body(it * 4 + j, j, lambda n: True)
            for j in range(4):
                e = NE - 4 + j
                body(e, j, lambda n, e=e: e + n < NE)

        def fourth(e, j):
            return e // 4 if isinstance(e, int) else (e - j) // 4

        stages = ["X", "Z", "A", "O", "U", "L", "M", "W", "R", "E", "C"]
        on = stages if stop_after is None else stages[:stages.index(stop_after) + 1]

        @block.sync
        def _(sp):
            sp.dma_start(cst[:, :], a["rope_constants"]).then_inc(sem("cst_full"), 16)
            sp.dma_start(pos_i[:, :], a["positions"].to_broadcast([P, T])).then_inc(sem("pos_full"), 16)
            sp.dma_start(g_attn[:, :], a["g_attn_norm"].to_broadcast([P, D])).then_inc(sem("g_full"), 16)
            for t in range(NT):
                if t >= 4:
                    sp.wait_ge(sem("hrow_ready"), t - 3)
                sp.dma_start(xin[t % 4][:, :], x_d[t]).then_inc(sem(f"x_full{t % 4}"), 16)
                if t == 3:
                    load_units(sp, 0, 3)
            sp.dma_start(gcol[:, 0:1], a["g_ckv"].rearrange("a p -> p a")).then_inc(sem("gcol_full"), 16)
            sp.dma_start(gcol[:, 1:3], a["g_cq"].rearrange("a (k p) -> p (a k)", p=P)).then_inc(sem("gcol_full"), 16)
            if "Z" in on:
                load_units(sp, 3, NZ)
            if "A" in on:
                sp.wait_ge(sem("w_split"), NZ)
                for h in range(HEADS):
                    if h >= 2:
                        sp.wait_ge(sem("hw_split"), h - 1)
                    r, f = h_raw[h % 2], sem(f"hraw_full{h % 2}")
                    q = r[:, 0:256].rearrange("p (k c) -> p k c", k=2)
                    c = h * (NOPE + ROPE)
                    sp.dma_start(q[:, :, 0:96], w_uq[:, :, c:c + 96]).then_inc(f, 16)
                    sp.dma_start(q[:, :, 96:112], w_uq[:, :, c + 80:c + 96]).then_inc(f, 16)
                    sp.dma_start(q[:, :, 112:128], w_uq[:, :, c + 64:c + 80]).then_inc(f, 16)
                    sp.dma_start(r[:, 256:320], a["w_uk"][0][:, h * 64:h * 64 + 64]).then_inc(f, 16)
                    sp.dma_start(r[:, 320:384], a["w_uv"][0][:, h * 64:h * 64 + 64]).then_inc(f, 16)
            if "U" in on:
                sp.wait_ge(sem("pv_done"), NQ)
                load_units(sp, NZ, NZ + NU)
            if "L" in on:
                sp.wait_ge(sem("uv_done"), 2 * NU)
                sp.dma_start(sp_raw[:, :, :], a["w_spatial"][0].rearrange("g i j -> i g j")).then_inc(sem("spraw_full"), 16)
                sp.dma_start(ln_g[:, :], a["sgu_gain"].to_broadcast([P, SGU])).then_inc(sem("ln_full"), 16)
                sp.dma_start(ln_b[:, :], a["sgu_bias"].to_broadcast([P, SGU])).then_inc(sem("ln_full"), 16)
                bs = a["b_spatial"].rearrange("a (q h) i -> a h q i", h=2)
                for hh in range(2):
                    sp.dma_start(sp_b[64 * hh:64 * hh + 64, :, :],
                                 bs[:, hh].to_broadcast([64, KS, P])).then_inc(sem("ln_full"), 16)
            if "M" in on:
                sp.wait_ge(sem("sp_done"), NT)
                sp.wait_ge(sem("s_lo_ready"), NT)
                load_units(sp, NZ + NU, NZ + NU + NM)
            if "W" in on:
                nu = NZ + NU + NM
                sp.wait_ge(sem("w_split"), nu)
                for k in range(KD):
                    if k >= 3:
                        sp.wait_ge(sem("wo_split"), k - 2)
                    sp.dma_start(raw[k % 3][:, :, :].rearrange("p a b -> p (a b)"),
                                 w_out[:, k, :]).then_inc(sem(f"wo_full{k % 3}"), 16)
                sp.wait_ge(sem("unit_done"), NM)
                sp.dma_start(g_ffn[:, :], a["g_ffn_norm"].to_broadcast([P, D])).then_inc(sem("rt_full"), 16)
                sp.dma_start(w_rt[:, :, 0:G], a["w_router_group"][0].rearrange("(k p) g -> p k g", p=P)).then_inc(sem("rt_full"), 16)
                for g in range(G):
                    sp.dma_start(w_rt[:, :, G + g * EPG:G + (g + 1) * EPG],
                                 a["w_router_expert"][0, g].rearrange("(k p) e -> p k e", p=P)).then_inc(sem("rt_full"), 16)
                sp.dma_start(b_rt[:, 0:G], a["b_router_group"].to_broadcast([P, G])).then_inc(sem("rt_full"), 16)
                sp.dma_start(b_rt[:, G:NR], a["b_router_expert"].rearrange("a g e -> a (g e)").to_broadcast([P, NE])).then_inc(sem("rt_full"), 16)
                for t in range(NT):
                    if t >= 2:
                        sp.wait_ge(sem("x2_ready"), t - 1)
                    sp.dma_start(xre[t % 2][:, :], x_d[t]).then_inc(sem(f"xre_full{t % 2}"), 16)
                    if t >= 1:
                        sp.wait_ge(sem("h2_ready"), t)
                        sp.dma_start(h2_dram[(t - 1) * P:t * P, :], h2[(t - 1) % 2][:, :]).then_inc(sem(f"h2_stored{(t - 1) % 2}"), 16)
                sp.wait_ge(sem("h2_ready"), NT)
                sp.dma_start(h2_dram[(NT - 1) * P:NT * P, :], h2[(NT - 1) % 2][:, :]).then_inc(sem(f"h2_stored{(NT - 1) % 2}"), 16)
            if "E" in on:
                sp.wait_ge(sem("out_done"), NT)
                sp.wait_ge(sem("rt_done"), NT)
                sp.wait_ge(sem("logit_ready"), NT)
                sp.wait_ge(sem("logit_read"), 1)

                def load_expert(e, q, free_gu, free_dn, src):
                    for g, w_d in enumerate((wg_d, wu_d, wd_d)):
                        if g < 2:
                            wait(sp, "lo_gu", free_gu + g)
                        else:
                            wait(sp, "lo_dn", free_dn)
                        sp.dma_start(raw_e[g][q][:, :], w_d[bass.ds(src, 1)].rearrange("e p n -> (e p) n")).then_inc(
                            sem(f"raw_e_full{g}{q}"), 16)

                experts(sp, lambda e, j, left: load_expert(e, j % 2, 2 * e - 3, e - 1, e))
                sp.wait_ge(sem("tab_read"), 1)
                n_ovf = sp.value_load(ovf_n[0:1, 0:1], min_val=0, max_val=NOVF)
                with sp.If(n_ovf > 0):
                    with sp.Fori(0, n_ovf) as b:
                        e = sp.value_load(ovf_e[0:1, bass.ds(b, 1)], min_val=0, max_val=NE - 1)
                        load_expert(b + NE, 0, 2 * b + 2 * NE - 1, b + NE, e)
            if "C" in on:
                sp.wait_ge(sem("y_stored_all"), 1)
                sp.dma_start(g_fin[:, :], a["g_final"].rearrange("(a d) -> a d", a=1).to_broadcast([P, D])).then_inc(sem("gfin_full"), 16)
                for t in range(NT):
                    if t >= 2:
                        sp.wait_ge(sem("acc_ready"), t - 1)
                    for k in range(2):
                        r0 = k * T + t * P
                        sp.dma_start(yin[t % 2][:, k, :], y_dram[r0:r0 + P, :]).then_inc(sem(f"yin_full{t % 2}"), 16)
                    if t >= 1:
                        sp.wait_ge(sem("res_ready"), t)
                        sp.dma_start(out_d[t - 1], res[(t - 1) % 2][:, :]).then_inc(sem(f"res_stored{(t - 1) % 2}"), 16)
                sp.wait_ge(sem("res_ready"), NT)
                sp.dma_start(out_d[NT - 1], res[(NT - 1) % 2][:, :]).then_inc(sem(f"res_stored{(NT - 1) % 2}"), 16)
                for i in range(2):
                    sp.wait_ge(sem(f"res_stored{i}"), 16 * NT // 2)

        @block.tensor
        def _(pe):
            for t in range(NT):
                pe.wait_ge(sem("hrow_ready"), t + 1)
                if t == 0:
                    pe.wait_ge(sem("const_ready"), 1)
                if t >= 2:
                    pe.wait_ge(sem("ht_lo_ready"), t - 1)
                b = 2 * (t % 2)
                for k in range(KD):
                    mm = pe.transpose(ps[:, b + k // 4, (k % 4) * P:(k % 4) * P + P],
                                      hrow[t % 2][:, k * P:(k + 1) * P], ident[:, :])
                mm.then_inc(sem("x_tr"), 1)
            if "Z" in on:
                for u in range(NZ):
                    pe.wait_ge(sem("w_split"), u + 1)
                    for c in range(2):
                        pe.wait_ge(sem("ht_lo_ready"), 4 * (c + 1) if u == 0 else NT)
                        dst = ps[:, (2 * u + c + 4) % 8, :]
                        for k in range(KD):
                            mm = mm3(pe, dst, (w_hi[u % 3][:, k, :], w_lo[u % 3][:, k, :]),
                                     (ht_hi[:, k, c * HALF:(c + 1) * HALF], ht_lo[:, k, c * HALF:(c + 1) * HALF]),
                                     k == 0, k == KD - 1)
                        mm.then_inc(sem("z_done"), 1)
                pe.wait_ge(sem("c_sq_ready"), 2)
                for c in range(2):
                    pe.matmul(ps[:, 4 + c, :], ones[:, :], c_sq[:, 0, c * HALF:(c + 1) * HALF],
                              start=True, stop=True).then_inc(sem("ms_done"), 1)
                pe.wait_ge(sem("c_sq_ready"), 6)
                pe.wait_ge(sem("kr_read"), 2)
                for c in range(2):
                    pe.matmul(ps[:, 6 + c, :], ones[:, :], c_sq[:, 1, c * HALF:(c + 1) * HALF], start=True, stop=False)
                    pe.matmul(ps[:, 6 + c, :], ones[:, :], c_sq[:, 2, c * HALF:(c + 1) * HALF],
                              start=False, stop=True).then_inc(sem("ms_done"), 1)
            if "A" in on:
                def job(h, j):
                    hh, hl = h_hi[h % 2], h_lo[h % 2]
                    if j == 0:
                        pe.wait_ge(sem("hw_split"), h + 1)
                    if j in (1, 2):
                        pe.wait_ge(sem("q_tmp_ready"), 2 * h + j)
                    elif h or j:
                        pe.wait_ge(sem("kv_lo_ready"), 3 * h + max(j - 2, 0))
                    if j < 2:
                        cs = slice(j * HALF, (j + 1) * HALF)
                        for k in range(2):
                            mm = mm3(pe, ps[:, 7, :], (hh[:, k * P:(k + 1) * P], hl[:, k * P:(k + 1) * P]),
                                     (c_hi[:, 1 + k, cs], c_lo[:, 1 + k, cs]), k == 0, k == 1)
                    elif j < 4:
                        cs = slice((j - 2) * HALF, (j - 1) * HALF)
                        mm = mm3(pe, ps[:, 7, :], (hh[:, 256:384], hl[:, 256:384]),
                                 (c_hi[:, 0, cs], c_lo[:, 0, cs]), True, True)
                    else:
                        for t in range(NT):
                            ts = slice(t * P, (t + 1) * P)
                            mm = mm3(pe, ps[:, 7, t * VH:(t + 1) * VH], (c_hi[:, 0, ts], c_lo[:, 0, ts]),
                                     (hh[:, 320:384], hl[:, 320:384]), True, True)
                    mm.then_inc(sem("job_done"), 1)

                def scores(s):
                    h, i = divmod(s, NT)
                    pe.wait_ge(sem("q_lo_ready"), 2 * h + 1 + i // 4)
                    pe.wait_ge(sem("kv_lo_ready"), 3 * h + 1 + i // 4)
                    if s >= 2:
                        pe.wait_ge(sem("exp_done"), s - 1)
                    qs = slice(i * P, (i + 1) * P)
                    n = (i + 1) * P
                    for c in range(i // 4 + 1):
                        m = min(n - c * HALF, HALF)
                        dst = ps[:, 2 * (s % 2) + c, :]
                        last = c == i // 4
                        mm = mm3(pe, dst[:, 0:m], (q_hi[h % 2][:, qs], q_lo[h % 2][:, qs]),
                                 (k_hi[h % 2][:, c * HALF:c * HALF + m], k_lo[h % 2][:, c * HALF:c * HALF + m]),
                                 True, not last)
                        if last:
                            mm = pe.matmul(dst[:, m - CHUNK:m], mask_l[:, :], mask_r[:, :], start=False, stop=True)
                    mm.then_inc(sem("s_done"), 1)

                def prob_transposes(s):
                    i = s % NT
                    c0 = chunks_through(s - 1) if s else 0
                    pe.wait_ge(sem("exp_done"), s + 1)
                    for c in range(i // 4 + 1):
                        if c0 + c >= 2:
                            pe.wait_ge(sem("pt_lo_ready"), c0 + c - 1)
                        for j in range(4 * c, min(4 * c + 4, i + 1)):
                            mm = pe.transpose(ps[:, 4 + (c0 + c) % 2, (j % 4) * P:(j % 4) * P + P],
                                              prob[s % 2][:, j * P:(j + 1) * P], ident[:, :])
                        mm.then_inc(sem("pt_done"), 1)

                def values(s):
                    h, i = divmod(s, NT)
                    c0 = chunks_through(s - 1) if s else 0
                    pe.wait_ge(sem("kv_lo_ready"), 3 * h + 3)
                    pe.wait_ge(sem("pt_lo_ready"), chunks_through(s))
                    if s:
                        pe.wait_ge(sem("o_ready"), s)
                    dst = ps[:, 6, i * VH:(i + 1) * VH]
                    for j in range(i + 1):
                        c = (c0 + j // 4) % 4
                        mm = mm3(pe, dst, (pt_hi[c][:, j % 4, :], pt_lo[c][:, j % 4, :]),
                                 (v_hi[h % 2][:, j, :], v_lo[h % 2][:, j, :]), j == 0, j == i)
                    mm.then_inc(sem("pv_done"), 1)

                pe.wait_ge(sem("c_lo_ready"), 6)
                pe.wait_ge(sem("c_std_ready"), 4)
                for j in range(5):
                    job(0, j)
                scores(0)
                scores(1)
                for s in range(NQ):
                    prob_transposes(s)
                    if s + 2 < NQ:
                        scores(s + 2)
                    h, i = divmod(s, NT)
                    if i < 5 and h + 1 < HEADS:
                        job(h + 1, i)
                    values(s)
            if "O" in on:
                for t in range(NT):
                    pe.wait_ge(sem("o_ready"), NQ)
                    if t >= 4:
                        pe.wait_ge(sem("ot_lo_ready"), t - 3)
                    for j in range(KS):
                        mm = pe.transpose(ps[:, t % 4, j * P:(j + 1) * P], o_tok[:, t, j * P:(j + 1) * P], ident[:, :])
                    mm.then_inc(sem("ot_tr"), 1)
            if "U" in on:
                for n in range(NZ, NZ + NU):
                    pe.wait_ge(sem("w_split"), n + 1)
                    for c in range(2):
                        jj = 2 * (n - NZ) + c
                        if jj >= 4:
                            pe.wait_ge(sem("gelu_ready"), jj - 3)
                        cs = slice(c * HALF, (c + 1) * HALF)
                        for k in range(KD):
                            mm = mm3(pe, ps[:, 4 + jj % 4, :], (w_hi[n % 3][:, k, :], w_lo[n % 3][:, k, :]),
                                     (ht_hi[:, k, cs], ht_lo[:, k, cs]), k == 0, k == KD - 1)
                        mm.then_inc(sem("uv_done"), 1)
            if "L" in on:
                pe.wait_ge(sem("gelu_ready"), 2 * NU)
                pe.wait_ge(sem("sp_masked"), 1)
                for g in range(8):
                    mm = pe.transpose(ps[:, 4 + g // 4, (g % 4) * P:(g % 4) * P + P], sp_raw[:, g, :], ident[:, :])
                mm.then_inc(sem("sp_tr"), 1)

                def v_rows(t):
                    if t >= 2:
                        pe.wait_ge(sem("ln_read"), t - 1)
                    else:
                        pe.wait_ge(sem("ot_lo_ready"), NT)
                    for j in range(KS):
                        mm = pe.transpose(ps[:, 6 + t % 2, j * P:(j + 1) * P], v_t[:, j, t * P:(t + 1) * P], ident[:, :])
                    mm.then_inc(sem("v_tr"), 1)

                v_rows(0)
                pe.wait_ge(sem("sp_lo_ready"), 1)
                for t in range(NT):
                    if t + 1 < NT:
                        v_rows(t + 1)
                    pe.wait_ge(sem("vn_lo_ready"), t + 1)
                    if t >= 2:
                        pe.wait_ge(sem("s_read"), 2 * (t - 1))
                    for pr in range(KS):
                        b = 2 * (t % 2) + pr // 2
                        cs = slice(pr * P, (pr + 1) * P)
                        gs = slice(2 * pr, 2 * pr + 2)
                        mm = mm3(pe, ps[:, b, (pr % 2) * 256:(pr % 2) * 256 + 256],
                                 (vn_hi[t % 2][:, cs], vn_lo[t % 2][:, cs]),
                                 (sp_hi[:, gs, :].rearrange("p a b -> p (a b)"), sp_lo[:, gs, :].rearrange("p a b -> p (a b)")),
                                 True, True)
                    mm.then_inc(sem("sp_done"), 1)
            if "M" in on:
                pe.wait_ge(sem("s_lo_ready"), NT)
                for f in range(KD):
                    for kind in range(3):
                        n = NZ + NU + 3 * f + kind
                        pe.wait_ge(sem("w_split"), n + 1)
                        if f:
                            pe.wait_ge(sem("sig_a_ready" if kind == 0 else "sig_b_ready" if kind == 1 else "mix_ready"), 2 * f)
                        wh, wl = w_hi[n % 3], w_lo[n % 3]
                        for c in range(2):
                            cs = slice(c * HALF, (c + 1) * HALF)
                            if kind < 2:
                                for k in range(KD):
                                    mm = mm3(pe, ps[:, 2 * kind + c, :], (wh[:, k, :], wl[:, k, :]),
                                             (ht_hi[:, k, cs], ht_lo[:, k, cs]), k == 0, k == KD - 1)
                            else:
                                for k in range(KS):
                                    mm3(pe, ps[:, 4 + c, :], (wh[:, k, :], wl[:, k, :]),
                                        (ot_hi[:, k, cs], ot_lo[:, k, cs]), k == 0, k == KS - 1)
                                for k in range(KS):
                                    mm = mm3(pe, ps[:, 6 + c, :], (wh[:, KS + k, :], wl[:, KS + k, :]),
                                             (st_hi[:, k, cs], st_lo[:, k, cs]), k == 0, k == KS - 1)
                        mm.then_inc(sem("unit_done"), 1)
            if "W" in on:
                pe.wait_ge(sem("mix_ready"), 2 * KD)

                def router(t):
                    pe.wait_ge(sem("h2_ready"), t + 1)
                    if t >= 1:
                        pe.wait_ge(sem("h2t_ready"), t)
                    for k in range(KD):
                        mm = pe.transpose(ps[:, 4 + k // 4, (k % 4) * P:(k % 4) * P + P],
                                          h2[t % 2][:, k * P:(k + 1) * P], ident[:, :])
                    mm.then_inc(sem("h2_tr"), 1)
                    pe.wait_ge(sem("h2t_ready"), t + 1)
                    pe.wait_ge(sem("rt_full"), 16 * 8)
                    if t >= 1:
                        pe.wait_ge(sem("logit_ready"), t)
                    for k in range(KD):
                        mm = pe.matmul(ps[:, 6, 0:NR], h2t[t % 2][:, k, :], w_rt[:, k, :], start=(k == 0), stop=(k == KD - 1))
                    mm.then_inc(sem("rt_done"), 1)

                for t in range(NT):
                    pe.wait_ge(sem("mt_lo_ready"), t + 1)
                    if t >= 2:
                        pe.wait_ge(sem("x2_ready"), t - 1)
                    for k in range(KD):
                        if t == 0:
                            pe.wait_ge(sem("wo_split"), k + 1)
                        for c in range(2):
                            cs = slice(c * HALF, (c + 1) * HALF)
                            mm = mm3(pe, ps[:, 2 * (t % 2) + c, :], (mt_hi[t % 2][:, k, :], mt_lo[t % 2][:, k, :]),
                                     (wo_hi[:, k, cs], wo_lo[:, k, cs]), k == 0, k == KD - 1)
                    mm.then_inc(sem("out_done"), 1)
                    if t >= 1:
                        router(t - 1)
                router(NT - 1)
            if "R" in on:
                pe.wait_ge(sem("oe_ready"), 1)
                pe.matmul(ps[:, 0, 0:NT * NE], before[:, :], oe_b[:, :, :].rearrange("p t e -> p (t e)"), start=True, stop=False)
                pe.matmul(ps[:, 0, 0:NT * NE], ones_b[:, :], cum_b[:, 0:NT, :].rearrange("p t e -> p (t e)"),
                          start=False, stop=True)
                pe.matmul(ps[:, 1, 0:NE], ones_b[:, :], cum_b[:, NT, :], start=True, stop=True).then_inc(sem("rank_done"), 1)
                for i in range(2 * NT):
                    pe.wait_ge(sem("sel_ready"), i + 1)
                    pe.matmul(ps[:, 2, 0:NBLK], sel_a[i % 2][:, :], sel_b[i % 2][:, :], start=(i == 0),
                              stop=(i == 2 * NT - 1)).then_inc(sem("sel_used"), 1)
            if "E" in on:
                def rows_in(e, j, full=None):
                    pe.wait_ge(sem(f"xs_full{j % 4}"), 16 * (fourth(e, j) + 1) if full is None else full)
                    wait(pe, "xst_ready", e)
                    v = xs[j % 4][:, :].rearrange("s (p k) -> s k p", k=KD)
                    for k in range(KD):
                        mm = pe.transpose(ps[:, k // 4, (k % 4) * P:(k % 4) * P + P], v[:, k, :], ident[:, :])
                    mm.then_inc(sem("xs_tr"), 1)

                def columns(e, j, g, slot):
                    pe.wait_ge(sem("xst_ready"), e + 1)
                    pe.wait_ge(sem("lo_gu"), 2 * e + g + 1)
                    q = j % 2
                    for k in range(KD):
                        ws = slice(k * DE, (k + 1) * DE)
                        mm = mm3(pe, ps[:, 2 + g, 0:DE], (xst_hi[q][:, k, :], xst_lo[q][:, k, :]),
                                 (we_hi[slot][:, ws], we_lo[slot][:, ws]), k == 0, k == KD - 1)
                    mm.then_inc(sem("group_used"), 1)

                def hidden_in(e):
                    pe.wait_ge(sem("hid_ready"), e + 1)
                    v = hid[:, :].rearrange("s (p q) -> s q p", q=2)
                    for q in range(2):
                        mm = pe.transpose(ps[:, 4, q * P:(q + 1) * P], v[:, q, :], ident[:, :])
                    mm.then_inc(sem("hid_tr"), 1)

                def down(e, slot):
                    pe.wait_ge(sem("hidt_ready"), e + 1)
                    pe.wait_ge(sem("lo_dn"), e + 1)
                    wait(pe, "y_left", e)
                    wait(pe, "y_right", e)
                    for c in range(2):
                        for q in range(2):
                            ws = slice(q * D + c * HALF, q * D + (c + 1) * HALF)
                            mm = mm3(pe, ps[:, 5 + c, :], (hidt_hi[:, q, :], hidt_lo[:, q, :]),
                                     (we_hi[slot][:, ws], we_lo[slot][:, ws]), q == 0, q == 1)
                    mm.then_inc(sem("group_used"), 1)

                def expert(e, j, left):
                    columns(e, j, 1, place(1, j) % 4)
                    if left(2):
                        rows_in(e + 2, j + 2, None if isinstance(e, int) else 16 * ((e - j) // 4 + (j + 2) // 4 + 1))
                    hidden_in(e)
                    if left(1):
                        columns(e + 1, j + 1, 0, place(0, j + 1) % 4)
                    down(e, place(2, j) % 4)

                pe.wait_ge(sem("tab_read"), 1)
                rows_in(0, 0)
                rows_in(1, 1)
                columns(0, 0, 0, 0)
                experts(pe, expert)
                n_ovf = pe.value_load(ovf_n[0:1, 0:1], min_val=0, max_val=NOVF)
                with pe.If(n_ovf > 0):
                    with pe.Fori(0, n_ovf) as b:
                        rows_in(b + NE, 0, 16 * (b + NE // 4 + 1))
                        for g in range(2):
                            columns(b + NE, 0, g, g)
                        hidden_in(b + NE)
                        down(b + NE, 2)

        @block.scalar
        def _(act):
            act.wait_ge(sem("const_ready"), 1)

            def ht_high(t):
                act.wait_ge(sem("x_tr"), t + 1)
                b = 2 * (t % 2)
                act.activation(ht_hi[:, :, t * P:(t + 1) * P],
                               ps[:, b:b + 2, :].rearrange("p b (k c) -> p (b k) c", c=P), ACT.Copy).then_inc(sem("ht_hi_ready"), 1)

            for t in range(NT):
                act.wait_ge(sem(f"x_full{t % 4}"), 16 * (t // 4 + 1))
                if t:
                    act.wait_ge(sem("ssq_ready"), t)
                act.activation(junk[:, :], xin[t % 4][:, :], ACT.Square, accum_out=ssq[:, t:t + 1]).then_inc(sem("ssq_ready"), 1)
                act.wait_ge(sem("ssq_ready"), t + 1)
                act.activation(std[:, t:t + 1], ssq[:, t:t + 1], ACT.Sqrt, scale=1.0 / D, bias=epst[:, :]).then_inc(sem("std_ready"), 1)
                if t:
                    ht_high(t - 1)
            ht_high(NT - 1)
            if "Z" in on:
                for j in range(2):
                    act.wait_ge(sem("ang_ready"), j + 1)
                    act.activation((tab_q if j == 0 else tab_k)[:, :], ang[:, :], ACT.Sin).then_inc(sem("sin_ready"), 1)
                for i, u in enumerate((0, 2, 3)):
                    for c in range(2):
                        cs = slice(c * HALF, (c + 1) * HALF)
                        act.wait_ge(sem("z_done"), 2 * u + c + 1)
                        src = ps[:, (2 * u + c + 4) % 8, :]
                        act.activation(c_raw[:, i, cs], src, ACT.Copy).then_inc(sem("c_raw_ready"), 1)
                        act.activation(c_sq[:, i, cs], src, ACT.Square).then_inc(sem("c_sq_ready"), 1)
                for i in range(4):
                    act.wait_ge(sem("ms_done"), i + 1)
                    act.activation(c_rs[:, i, :], ps[:, 4 + i, :], ACT.Sqrt, scale=1.0 / (KVR if i < 2 else QR),
                                   bias=epst[:, :]).then_inc(sem("c_std_ready"), 1)
                for i in range(6):
                    cs = slice((i % 2) * HALF, (i % 2 + 1) * HALF)
                    act.wait_ge(sem("cn_ready"), i + 1)
                    act.activation(c_hi[:, i // 2, cs], c_raw[:, i // 2, cs], ACT.Copy).then_inc(sem("c_hi_ready"), 1)
            if "A" in on:
                def job_high(h, j):
                    act.wait_ge(sem("job_done"), 5 * h + j + 1)
                    if j < 2:
                        act.wait_ge(sem("q_tmp_ready"), 2 * h + j + 1)
                        act.activation(q_hi[h % 2][:, j * HALF:(j + 1) * HALF], q_tmp[j][:, :], ACT.Copy).then_inc(sem("q_hi_ready"), 1)
                    elif j < 4:
                        act.activation(k_hi[h % 2][0:64, (j - 2) * HALF:(j - 1) * HALF], ps[0:64, 7, :], ACT.Copy).then_inc(sem("kv_hi_ready"), 1)
                    else:
                        act.activation(v_hi[h % 2][:, :, :].rearrange("p t c -> p (t c)"), ps[:, 7, :], ACT.Copy).then_inc(sem("kv_hi_ready"), 1)

                def exponent(s):
                    n = (s % NT + 1) * P
                    act.wait_ge(sem("max_ready"), s + 1)
                    if s >= 2:
                        act.wait_ge(sem("pt_done"), chunks_through(s - 2))
                    b = 2 * (s % 2)
                    act.activation(prob[s % 2][:, 0:n], ps[:, b:b + 2, :].rearrange("p b c -> p (b c)")[:, 0:n], ACT.Exp,
                                   bias=negm[:, s:s + 1], accum_out=lsum[:, s:s + 1]).then_inc(sem("exp_done"), 1)

                for j in range(5):
                    job_high(0, j)
                exponent(0)
                for s in range(NQ):
                    h, i = divmod(s, NT)
                    c0 = chunks_through(s - 1) if s else 0
                    for c in range(i // 4 + 1):
                        w = min(4, i + 1 - 4 * c)
                        cc = c0 + c
                        act.wait_ge(sem("pt_done"), cc + 1)
                        if cc >= 4:
                            used = next(x for x in range(s + 1) if chunks_through(x) > cc - 4)
                            act.wait_ge(sem("pv_done"), used + 1)
                        act.activation(pt_hi[cc % 4][:, 0:w, :].rearrange("p a b -> p (a b)"), ps[:, 4 + cc % 2, 0:w * P],
                                       ACT.Copy).then_inc(sem("pt_hi_ready"), 1)
                    if s + 1 < NQ:
                        exponent(s + 1)
                    if i < 5 and h + 1 < HEADS:
                        job_high(h + 1, i)
            if "O" in on:
                for t in range(NT):
                    act.wait_ge(sem("ot_tr"), t + 1)
                    act.activation(ot_hi[:, :, t * P:(t + 1) * P], ps[:, t % 4, :].rearrange("p (k c) -> p k c", c=P),
                                   ACT.Copy).then_inc(sem("ot_hi_ready"), 1)
            if "U" in on:
                act.wait_ge(sem("ot_tr"), NT)
                for jj in range(2 * NU):
                    f, c = divmod(jj, 2)
                    act.wait_ge(sem("uv_done"), jj + 1)
                    dst = (u_t if f < KS else v_t)[:, f % KS, c * HALF:(c + 1) * HALF]
                    act.activation(dst, ps[:, 4 + jj % 4, :], ACT.Gelu_apprx_tanh).then_inc(sem("gelu_ready"), 1)
            if "L" in on:
                act.wait_ge(sem("sp_tr"), 1)
                act.activation(sp_hi[:, :, :], ps[:, 4:6, :].rearrange("p b (g c) -> p (b g) c", c=P), ACT.Copy).then_inc(sem("sp_hi_ready"), 1)

                def ln_std(t):
                    act.wait_ge(sem("bn_ready"), t + 1)
                    act.activation(std[:, NT + t:NT + t + 1], bnag[:, t, 1:2], ACT.Sqrt, bias=epst[:, :]).then_inc(sem("ln_std_ready"), 1)

                def vn_high(t):
                    act.wait_ge(sem("ln_ready"), t + 1)
                    if t >= 2:
                        act.wait_ge(sem("sp_done"), t - 1)
                    act.activation(vn_hi[t % 2][:, :], ln_t[t % 2][:, :], ACT.Copy).then_inc(sem("vn_hi_ready"), 1)

                def s_high(t):
                    act.wait_ge(sem("s_ready"), t + 1)
                    act.activation(st_hi[:, :, t * P:(t + 1) * P], s_t[t % 2][:, :, :], ACT.Copy).then_inc(sem("s_hi_ready"), 1)

                for t in range(NT):
                    ln_std(t)
                    vn_high(t)
                    if t:
                        s_high(t - 1)
                s_high(NT - 1)
            if "M" in on:
                for f in range(KD):
                    for kind in range(2):
                        act.wait_ge(sem("unit_done"), 3 * f + kind + 1)
                        for c in range(2):
                            cs = slice(c * HALF, (c + 1) * HALF)
                            if kind == 1 and f:
                                act.wait_ge(sem("mix_ready"), 2 * f + c - 1)
                            dst = mix[:, f, cs] if kind == 0 else sig_b[c][:, :]
                            act.activation(dst, ps[:, 2 * kind + c, :],
                                           ACT.Sigmoid).then_inc(sem("sig_a_ready" if kind == 0 else "sig_b_ready"), 1)
            if "W" in on:
                for k in range(KD):
                    act.wait_ge(sem(f"wo_full{k % 3}"), 16 * (k // 3 + 1))
                    if k == 0:
                        act.wait_ge(sem("unit_done"), NM)
                    act.activation(wo_hi[:, k, :], raw[k % 3][:, :, :].rearrange("p a b -> p (a b)"), ACT.Copy).then_inc(sem("wo_hi_ready"), 1)
                    if k < 2:
                        act.wait_ge(sem("mix_ready"), 2 * KD)
                        act.activation(mt_hi[k][:, :, :], mix[:, :, k * P:(k + 1) * P], ACT.Copy).then_inc(sem("mt_hi_ready"), 1)

                def logits_in(t):
                    act.wait_ge(sem("h2_tr"), t + 1)
                    if t >= 2:
                        act.wait_ge(sem("rt_done"), t - 1)
                    act.activation(h2t[t % 2][:, :, :], ps[:, 4:6, :].rearrange("p b (k c) -> p (b k) c", c=P), ACT.Copy).then_inc(sem("h2t_ready"), 1)

                for t in range(NT):
                    act.wait_ge(sem("x2_ready"), t + 1)
                    if t:
                        act.wait_ge(sem("ssq2_ready"), t)
                    act.activation(junk2[:, :], x2[:, t, :], ACT.Square, accum_out=ssq[:, 8 + t:9 + t]).then_inc(sem("ssq2_ready"), 1)
                    act.wait_ge(sem("ssq2_ready"), t + 1)
                    act.activation(std[:, 8 + t:9 + t], ssq[:, 8 + t:9 + t], ACT.Sqrt, scale=1.0 / D, bias=epst[:, :]).then_inc(sem("std2_ready"), 1)
                    if t + 2 < NT:
                        act.wait_ge(sem("out_done"), t + 1)
                        act.activation(mt_hi[t % 2][:, :, :], mix[:, :, (t + 2) * P:(t + 3) * P], ACT.Copy).then_inc(sem("mt_hi_ready"), 1)
                    logits_in(t)
            if "R" in on:
                act.wait_ge(sem("gmax_ready"), 1)
                act.activation(ex[:, :, :], ex[:, :, :], ACT.Exp).then_inc(sem("gexp_ready"), 1)
                act.wait_ge(sem("ediff_ready"), 1)
                act.activation(gatew[:, 1, :], gatew[:, 1, :], ACT.Exp).then_inc(sem("gexp_ready"), 1)
            if "E" in on:
                def high(g, e, q, full, used, slot):
                    act.wait_ge(sem(f"raw_e_full{g}{q}"), full)
                    wait(act, "group_used", used)
                    act.activation(we_hi[slot][:, :], raw_e[g][q][:, :], ACT.Copy).then_inc(sem("hi_gu" if g < 2 else "hi_dn"), 1)

                def split(g, e, j):
                    full = 16 * (e // 2 + 1) if isinstance(e, int) else 8 * (e - j % 2) + 16
                    high(g, e, j % 2, full, place(g, e) - 3, place(g, j) % 4)

                def rows_high(e, q):
                    act.wait_ge(sem("xs_tr"), e + 1)
                    act.activation(xst_hi[q][:, :, :], ps[:, 0:2, :].rearrange("p b (k c) -> p (b k) c", c=P), ACT.Copy).then_inc(sem("xst_hi_ready"), 1)

                def silu(e, used):
                    act.wait_ge(sem("group_used"), used)
                    wait(act, "hid_ready", e)
                    act.activation(sg[:, :], ps[:, 2, 0:DE], ACT.Silu).then_inc(sem("sg_ready"), 1)

                def hidden_high(e):
                    act.wait_ge(sem("hid_tr"), e + 1)
                    act.activation(hidt_hi[:, :, :].rearrange("p a b -> p (a b)"), ps[:, 4, 0:2 * P], ACT.Copy).then_inc(sem("hidt_hi_ready"), 1)

                def left_half(e, q, used, sent):
                    act.wait_ge(sem("group_used"), used)
                    wait(act, f"y_sent{q}", sent)
                    act.activation(y[q][:, 0:HALF], ps[:, 5, :], ACT.Copy).then_inc(sem("y_left"), 1)

                def expert(e, j, left):
                    silu(e, 3 * e + 2)
                    if left(2):
                        rows_high(e + 2, j % 2)
                    hidden_high(e)
                    if left(2):
                        split(0, e + 2, j + 2)
                    if left(1):
                        split(2, e + 1, j + 1)
                    left_half(e, j % 2, 3 * e + 4 if not (isinstance(e, int) and e == NE - 1) else 3 * NE, 8 * (e - j % 2))
                    if left(2):
                        split(1, e + 2, j + 2)

                act.wait_ge(sem("out_done"), NT)
                act.wait_ge(sem("rt_done"), NT)
                split(0, 0, 0)
                split(1, 0, 0)
                split(0, 1, 1)
                split(2, 0, 0)
                act.wait_ge(sem("tab_read"), 1)
                rows_high(0, 0)
                rows_high(1, 1)
                split(1, 1, 1)
                experts(act, expert)
                n_ovf = act.value_load(ovf_n[0:1, 0:1], min_val=0, max_val=NOVF)
                with act.If(n_ovf > 0):
                    with act.Fori(0, n_ovf) as b:
                        for g in range(3):
                            high(g, b + NE, 0, b * 16 + 16 * (NE // 2 + 1), b * 3 + 3 * NE, g)
                        rows_high(b + NE, 0)
                        silu(b + NE, b * 3 + 3 * NE + 2)
                        hidden_high(b + NE)
                        left_half(b + NE, 0, b * 3 + 3 * NE + 3, b * 16 + 16 * (NE // 2))
            if "C" in on:
                for t in range(NT):
                    act.wait_ge(sem("acc_ready"), t + 1)
                    if t:
                        act.wait_ge(sem("ssq3_ready"), t)
                    act.activation(junk3[:, :], acc[t % 2][:, :], ACT.Square, accum_out=ssq[:, 16 + t:17 + t]).then_inc(sem("ssq3_ready"), 1)
                    act.wait_ge(sem("ssq3_ready"), t + 1)
                    act.activation(std[:, 16 + t:17 + t], ssq[:, 16 + t:17 + t], ACT.Sqrt, scale=1.0 / D, bias=epst[:, :]).then_inc(sem("std3_ready"), 1)

        @block.vector
        def _(dve):
            steps = [0]

            def link(ins):
                steps[0] += 1
                ins.then_inc(sem("dve_step"), 1)
                dve.wait_ge(sem("dve_step"), steps[0])

            dve.wait_ge(sem("iota_ready"), 2)
            link(dve.tensor_scalar(ident[:, :], iota_row[:, :], iota_col[:, :], None, ALU.is_equal))
            link(dve.tensor_scalar(before[:, :], iota_row[:, :], iota_col[:, :], None, ALU.is_gt))
            link(dve.memset(ones[:, :], 1.0))
            link(dve.memset(ones_b[:, :], 1.0))
            link(dve.memset(epst[:, :], EPS))
            link(dve.memset(mask_l[:, :].bitcast(F32), 0.0))
            link(dve.memset(mask_l[0:1, 0:CHUNK].bitcast(F32), -BIG))
            dve.memset(mask_r[:, :].bitcast(F32), 1.0).then_inc(sem("const_ready"), 1)

            def rope_angles(j):
                fr, ph = cst[:, 3 * j:3 * j + 1], cst[:, 3 * j + 2:3 * j + 3]
                if j:
                    dve.wait_ge(sem("sin_ready"), j)
                link(dve.tensor_copy(turns[:, :], pos_i[:, :]))
                link(dve.tensor_scalar(ang[:, :], turns[:, :], fr, None, ALU.mult))
                link(dve.tensor_scalar(turns[:, :], ang[:, :], 1.0 / TWO_PI, cst[:, 3 * j + 1:3 * j + 2], ALU.mult, ALU.add))
                link(dve.tensor_scalar(turns[:, :], turns[:, :], MAGIC, MAGIC, ALU.add, ALU.subtract))
                for c in (C1, C2, C3):
                    link(dve.scalar_tensor_tensor(ang[:, :], turns[:, :], -c, ang[:, :], ALU.mult, ALU.add))
                link(dve.tensor_scalar(ang[:, :], ang[:, :], ph, PI_IN, ALU.add, ALU.min))
                dve.tensor_scalar(ang[:, :], ang[:, :], -PI_IN, None, ALU.max).then_inc(sem("ang_ready"), 1)

            def ht_low(t):
                dve.wait_ge(sem("ht_hi_ready"), t + 1)
                b = 2 * (t % 2)
                ts = slice(t * P, (t + 1) * P)
                dve.tensor_tensor(ht_lo[:, :, ts], ps[:, b:b + 2, :].rearrange("p b (k c) -> p (b k) c", c=P),
                                  ht_hi[:, :, ts].bitcast(F32), ALU.subtract).then_inc(sem("ht_lo_ready"), 1)

            dve.wait_ge(sem("g_full"), 16)
            for t in range(NT):
                dve.wait_ge(sem("std_ready"), t + 1)
                link(dve.reciprocal(rstd[:, t:t + 1], std[:, t:t + 1]))
                if t >= 2:
                    dve.wait_ge(sem("x_tr"), t - 1)
                dve.scalar_tensor_tensor(hrow[t % 2][:, :], xin[t % 4][:, :], rstd[:, t:t + 1], g_attn[:, :],
                                         ALU.mult, ALU.mult).then_inc(sem("hrow_ready"), 1)
                if t:
                    ht_low(t - 1)
            ht_low(NT - 1)
            if "Z" in on:
                dve.wait_ge(sem("cst_full"), 16)
                dve.wait_ge(sem("pos_full"), 16)
                rope_angles(0)
                rope_angles(1)
                dve.wait_ge(sem("sin_ready"), 2)
                link(dve.tensor_scalar(tab_q[:, :], tab_q[:, :], SCALE, None, ALU.mult))
                for c in range(2):
                    cs = slice(c * HALF, (c + 1) * HALF)
                    dve.wait_ge(sem("z_done"), 3 + c)
                    dve.tensor_tensor(kr1[64:128, cs], ps[64:128, 6 + c, :], tab_k[64:128, cs], ALU.mult).then_inc(sem("kr_half"), 1)
                    dve.tensor_tensor(kr2[64:128, cs], ps[0:64, 6 + c, :], tab_k[0:64, cs], ALU.mult).then_inc(sem("kr_read"), 1)
                dve.wait_ge(sem("kr_half"), 2)
                dve.wait_ge(sem("kr_read"), 2)
                link(dve.tensor_tensor(kr1[64:128, :], kr1[64:128, :], kr2[64:128, :], ALU.add))
                for i in range(2):
                    link(dve.tensor_copy(k_hi[i][64:128, :], kr1[64:128, :]))
                    link(dve.tensor_tensor(k_lo[i][64:128, :], kr1[64:128, :], k_hi[i][64:128, :].bitcast(F32), ALU.subtract))
                dve.wait_ge(sem("gcol_full"), 32)
                dve.wait_ge(sem("c_raw_ready"), 6)
                for i in range(4):
                    dve.wait_ge(sem("c_std_ready"), i + 1)
                    link(dve.reciprocal(c_rs[:, i, :], c_rs[:, i, :]))
                for i in range(6):
                    cs = slice((i % 2) * HALF, (i % 2 + 1) * HALF)
                    u = i // 2
                    dve.scalar_tensor_tensor(c_raw[:, u, cs], c_raw[:, u, cs], gcol[:, u:u + 1],
                                             c_rs[:, (0 if u == 0 else 2) + i % 2, :], ALU.mult, ALU.mult).then_inc(sem("cn_ready"), 1)
                for i in range(6):
                    cs = slice((i % 2) * HALF, (i % 2 + 1) * HALF)
                    u = i // 2
                    dve.wait_ge(sem("c_hi_ready"), i + 1)
                    dve.tensor_tensor(c_lo[:, u, cs], c_raw[:, u, cs], c_hi[:, u, cs].bitcast(F32), ALU.subtract).then_inc(sem("c_lo_ready"), 1)
            if "A" in on:
                def job_read(h, j):
                    dve.wait_ge(sem("job_done"), 5 * h + j + 1)
                    if j < 2:
                        if h:
                            dve.wait_ge(sem("q_lo_ready"), 2 * h + j - 1)
                        dve.tensor_tensor(q_tmp[j][:, :], ps[:, 7, :], tab_q[:, j * HALF:(j + 1) * HALF], ALU.mult).then_inc(sem("q_tmp_ready"), 1)
                    elif j < 4:
                        cs = slice((j - 2) * HALF, (j - 1) * HALF)
                        dve.wait_ge(sem("kv_hi_ready"), 3 * h + j - 1)
                        dve.tensor_tensor(k_lo[h % 2][0:64, cs], ps[0:64, 7, :], k_hi[h % 2][0:64, cs].bitcast(F32), ALU.subtract).then_inc(sem("kv_lo_ready"), 1)
                    else:
                        dve.wait_ge(sem("kv_hi_ready"), 3 * h + 3)
                        dve.tensor_tensor(v_lo[h % 2][:, :, :].rearrange("p t c -> p (t c)"), ps[:, 7, :],
                                          v_hi[h % 2][:, :, :].rearrange("p t c -> p (t c)").bitcast(F32), ALU.subtract).then_inc(sem("kv_lo_ready"), 1)

                def row_max(s):
                    n = (s % NT + 1) * P
                    dve.wait_ge(sem("s_done"), s + 1)
                    b = 2 * (s % 2)
                    dve.tensor_reduce(negm[:, s:s + 1], ps[:, b:b + 2, :].rearrange("p b c -> p (b c)")[:, 0:n], AX, ALU.max,
                                      negate=True).then_inc(sem("max_ready"), 1)

                def o_rows(s):
                    h, i = divmod(s, NT)
                    dve.wait_ge(sem("exp_done"), s + 1)
                    dve.reciprocal(rl[:, s:s + 1], lsum[:, s:s + 1]).then_inc(sem("rl_ready"), 1)
                    dve.wait_ge(sem("rl_ready"), s + 1)
                    dve.wait_ge(sem("pv_done"), s + 1)
                    dve.tensor_scalar(o_tok[:, i, h * VH:(h + 1) * VH], ps[:, 6, i * VH:(i + 1) * VH], rl[:, s:s + 1], None,
                                      ALU.mult).then_inc(sem("o_ready"), 1)

                for j in range(5):
                    job_read(0, j)
                row_max(0)
                for s in range(NQ):
                    h, i = divmod(s, NT)
                    if s + 1 < NQ:
                        row_max(s + 1)
                    if s:
                        o_rows(s - 1)
                    c0 = chunks_through(s - 1) if s else 0
                    for c in range(i // 4 + 1):
                        w = min(4, i + 1 - 4 * c)
                        cc = c0 + c
                        dve.wait_ge(sem("pt_hi_ready"), cc + 1)
                        dve.tensor_tensor(pt_lo[cc % 4][:, 0:w, :].rearrange("p a b -> p (a b)"), ps[:, 4 + cc % 2, 0:w * P],
                                          pt_hi[cc % 4][:, 0:w, :].rearrange("p a b -> p (a b)").bitcast(F32), ALU.subtract).then_inc(sem("pt_lo_ready"), 1)
                    if i < 5 and h + 1 < HEADS:
                        job_read(h + 1, i)
                o_rows(NQ - 1)
            if "O" in on:
                for t in range(NT):
                    ts = slice(t * P, (t + 1) * P)
                    dve.wait_ge(sem("ot_hi_ready"), t + 1)
                    dve.tensor_tensor(ot_lo[:, :, ts], ps[:, t % 4, :].rearrange("p (k c) -> p k c", c=P),
                                      ot_hi[:, :, ts].bitcast(F32), ALU.subtract).then_inc(sem("ot_lo_ready"), 1)
            if "L" in on:
                dve.wait_ge(sem("spraw_full"), 16)
                dve.memset(sp_raw[0:CHUNK, :, CHUNK:P], 0.0).then_inc(sem("sp_masked"), 1)
                dve.wait_ge(sem("sp_hi_ready"), 1)
                dve.tensor_tensor(sp_lo[:, :, :], ps[:, 4:6, :].rearrange("p b (g c) -> p (b g) c", c=P),
                                  sp_hi[:, :, :].bitcast(F32), ALU.subtract).then_inc(sem("sp_lo_ready"), 1)
                dve.wait_ge(sem("ln_full"), 64)

                def norm_v(t):
                    bank = ps[:, 6 + t % 2, :]
                    dve.wait_ge(sem("v_tr"), t + 1)
                    link(dve.bn_stats(bnst[:, t, :], bank))
                    dve.bn_aggr(bnag[:, t, :], bnst[:, t, :]).then_inc(sem("bn_ready"), 1)
                    dve.wait_ge(sem("ln_std_ready"), t + 1)
                    link(dve.reciprocal(rstd[:, NT + t:NT + t + 1], std[:, NT + t:NT + t + 1]))
                    if t >= 2:
                        dve.wait_ge(sem("vn_lo_ready"), t - 1)
                    ins = dve.tensor_scalar(ln_t[t % 2][:, :], bank, bnag[:, t, 0:1], rstd[:, NT + t:NT + t + 1],
                                            ALU.subtract, ALU.mult)
                    ins.then_inc(sem("ln_read"), 1)
                    dve.wait_ge(sem("ln_read"), t + 1)
                    link(dve.tensor_tensor(ln_t[t % 2][:, :], ln_t[t % 2][:, :], ln_g[:, :], ALU.mult))
                    dve.tensor_tensor(ln_t[t % 2][:, :], ln_t[t % 2][:, :], ln_b[:, :], ALU.add).then_inc(sem("ln_ready"), 1)
                    dve.wait_ge(sem("vn_hi_ready"), t + 1)
                    dve.tensor_tensor(vn_lo[t % 2][:, :], ln_t[t % 2][:, :], vn_hi[t % 2][:, :].bitcast(F32), ALU.subtract).then_inc(sem("vn_lo_ready"), 1)

                def gate_u(t):
                    ts = slice(t * P, (t + 1) * P)
                    dve.wait_ge(sem("sp_done"), t + 1)
                    if t >= 2:
                        dve.wait_ge(sem("s_lo_ready"), t - 1)
                    src = ps[:, 2 * (t % 2):2 * (t % 2) + 2, :].rearrange("p b (q h i) -> p (b q) h i", q=2, h=2)
                    for hh in range(2):
                        r = slice(64 * hh, 64 * hh + 64)
                        dve.tensor_tensor(s_t[t % 2][r, :, :], src[r, :, hh, :], sp_b[r, :, :], ALU.add).then_inc(sem("s_read"), 1)
                    dve.wait_ge(sem("s_read"), 2 * t + 2)
                    dve.tensor_tensor(s_t[t % 2][:, :, :], s_t[t % 2][:, :, :], u_t[:, :, ts], ALU.mult).then_inc(sem("s_ready"), 1)

                def gate_low(t):
                    ts = slice(t * P, (t + 1) * P)
                    dve.wait_ge(sem("s_hi_ready"), t + 1)
                    dve.tensor_tensor(st_lo[:, :, ts], s_t[t % 2][:, :, :], st_hi[:, :, ts].bitcast(F32), ALU.subtract).then_inc(sem("s_lo_ready"), 1)

                norm_v(0)
                for t in range(NT):
                    if t + 1 < NT:
                        norm_v(t + 1)
                    gate_u(t)
                    gate_low(t)
            if "M" in on:
                for f in range(KD):
                    for c in range(2):
                        n = 2 * f + c
                        cs = slice(c * HALF, (c + 1) * HALF)
                        dve.wait_ge(sem("unit_done"), 3 * f + 3)
                        dve.wait_ge(sem("sig_a_ready"), n + 1)
                        dve.tensor_tensor(mix[:, f, cs], ps[:, 4 + c, :], mix[:, f, cs], ALU.mult).then_inc(sem("mix_a_ready"), 1)
                        dve.wait_ge(sem("sig_b_ready"), n + 1)
                        link(dve.tensor_tensor(sig_b[c][:, :], ps[:, 6 + c, :], sig_b[c][:, :], ALU.mult))
                        dve.wait_ge(sem("mix_a_ready"), n + 1)
                        dve.tensor_tensor(mix[:, f, cs], mix[:, f, cs], sig_b[c][:, :], ALU.add).then_inc(sem("mix_ready"), 1)
            if "W" in on:
                def mt_low(t):
                    dve.wait_ge(sem("mt_hi_ready"), t + 1)
                    dve.tensor_tensor(mt_lo[t % 2][:, :, :], mix[:, :, t * P:(t + 1) * P], mt_hi[t % 2][:, :, :].bitcast(F32),
                                      ALU.subtract).then_inc(sem("mt_lo_ready"), 1)

                for k in range(KD):
                    dve.wait_ge(sem("wo_hi_ready"), k + 1)
                    dve.tensor_tensor(wo_lo[:, k, :], raw[k % 3][:, :, :].rearrange("p a b -> p (a b)"),
                                      wo_hi[:, k, :].bitcast(F32), ALU.subtract).then_inc(sem("wo_split"), 1)
                    if k < 2:
                        mt_low(k)
                dve.wait_ge(sem("rt_full"), 128)

                def logits(t):
                    dve.wait_ge(sem("rt_done"), t + 1)
                    dve.tensor_tensor(logit[:, t, :], ps[:, 6, 0:NR], b_rt[:, :], ALU.add).then_inc(sem("logit_ready"), 1)

                for t in range(NT):
                    dve.wait_ge(sem("out_done"), t + 1)
                    dve.wait_ge(sem(f"xre_full{t % 2}"), 16 * (t // 2 + 1))
                    dve.tensor_tensor(x2[:, t, :], ps[:, 2 * (t % 2):2 * (t % 2) + 2, :].rearrange("p b c -> p (b c)"),
                                      xre[t % 2][:, :], ALU.add).then_inc(sem("x2_ready"), 1)
                    dve.wait_ge(sem("std2_ready"), t + 1)
                    link(dve.reciprocal(rstd[:, 8 + t:9 + t], std[:, 8 + t:9 + t]))
                    if t >= 2:
                        dve.wait_ge(sem("h2_tr"), t - 1)
                        dve.wait_ge(sem(f"h2_stored{t % 2}"), 16 * (t // 2))
                    dve.scalar_tensor_tensor(h2[t % 2][:, :], x2[:, t, :], rstd[:, 8 + t:9 + t], g_ffn[:, :],
                                             ALU.mult, ALU.mult).then_inc(sem("h2_ready"), 1)
                    if t + 2 < NT:
                        mt_low(t + 2)
                    if t:
                        logits(t - 1)
                logits(NT - 1)
            if "R" in on:
                lg = logit[:, :, 0:G]
                lx = logit[:, :, G:NR].rearrange("p t (g e) -> p t g e", g=G)
                dve.wait_ge(sem("logit_ready"), NT)

                def wide(ap, n):
                    return ap.unsqueeze(2).to_broadcast([P, NT, n])

                link(dve.tensor_copy(iog[:, :, :], iota_row[:, 0:EPG].unsqueeze(1).to_broadcast([P, NT, EPG])))

                def first_max(src, m, n, onehot):
                    link(dve.tensor_reduce(m, src, AX, ALU.max))
                    link(dve.tensor_tensor(cand[:, :, 0:n], src, wide(m, n), ALU.is_lt))
                    link(dve.scalar_tensor_tensor(cand[:, :, 0:n], cand[:, :, 0:n], 64.0, iog[:, :, 0:n], ALU.mult, ALU.add))
                    link(dve.tensor_reduce(sel[:, :], cand[:, :, 0:n], AX, ALU.min))
                    link(dve.tensor_tensor(onehot, cand[:, :, 0:n], wide(sel[:, :], n), ALU.is_equal))

                first_max(lg, mg[:, :], G, og[:, :, :])
                dve.tensor_tensor(ex[:, :, :], lg, wide(mg[:, :], G), ALU.subtract).then_inc(sem("gmax_ready"), 1)
                dve.wait_ge(sem("gexp_ready"), 1)
                link(dve.tensor_reduce(ptop[:, :], ex[:, :, :], AX, ALU.add))
                link(dve.reciprocal(ptop[:, :], ptop[:, :]))
                og4 = og[:, :, :].unsqueeze(3).to_broadcast([P, NT, G, EPG])
                for t in range(NT):
                    dve.tensor_tensor(lprod[:, t], lx[:, t], og4[:, t], ALU.mult).then_inc(sem("lprod_ready"), 1)
                dve.wait_ge(sem("lprod_ready"), NT)
                link(dve.tensor_tensor(le[:, :, :], lprod[:, :, 0, :], lprod[:, :, 1, :], ALU.add))
                link(dve.tensor_tensor(le[:, :, :], le[:, :, :], lprod[:, :, 2, :], ALU.add))
                dve.tensor_tensor(le[:, :, :], le[:, :, :], lprod[:, :, 3, :], ALU.add).then_inc(sem("logit_read"), 1)
                dve.wait_ge(sem("logit_read"), 1)
                first_max(le[:, :, :], m12[:, 0, :], EPG, oh[0][:, :, :])
                link(dve.scalar_tensor_tensor(le[:, :, :], oh[0][:, :, :], -BIG, le[:, :, :], ALU.mult, ALU.add))
                first_max(le[:, :, :], m12[:, 1, :], EPG, oh[1][:, :, :])
                dve.tensor_tensor(gatew[:, 1, :], m12[:, 1, :], m12[:, 0, :], ALU.subtract).then_inc(sem("ediff_ready"), 1)
                for k in range(2):
                    for t in range(NT):
                        ins = dve.tensor_tensor(oe[k][:, t], oh[k][:, t].unsqueeze(1).to_broadcast([P, G, EPG]), og4[:, t], ALU.mult)
                        ins.then_inc(sem("oeh_ready"), 1)
                dve.wait_ge(sem("oeh_ready"), 2 * NT)
                oef = [oe[k][:, :, :, :].rearrange("p t g e -> p t (g e)") for k in range(2)]
                link(dve.tensor_tensor(oe_b[:, :, :], oef[0], oef[1], ALU.add))
                link(dve.memset(cum_b[:, 0, :], 0.0))
                for t in range(NT):
                    link(dve.tensor_tensor(cum_b[:, t + 1, :], cum_b[:, t, :], oe_b[:, t, :], ALU.add))
                dve.memset(cmp7[:, :], 0.0).then_inc(sem("oe_ready"), 1)
                dve.wait_ge(sem("gexp_ready"), 2)
                link(dve.tensor_scalar(gatew[:, 0, :], gatew[:, 1, :], 1.0, None, ALU.add))
                link(dve.reciprocal(gatew[:, 0, :], gatew[:, 0, :]))
                link(dve.tensor_tensor(gatew[:, 0, :], gatew[:, 0, :], ptop[:, :], ALU.mult))
                link(dve.tensor_tensor(gatew[:, 1, :], gatew[:, 1, :], gatew[:, 0, :], ALU.mult))
                dve.wait_ge(sem("rank_done"), 1)
                link(dve.tensor_copy(rank_e[:, :, :].rearrange("p t e -> p (t e)"), ps[:, 0, 0:NT * NE]))
                link(dve.tensor_copy(cnt[:, :], ps[:, 1, 0:NE]))
                link(dve.tensor_scalar(novf[:, :], cnt[:, :], float(P), None, ALU.is_gt))
                for j in range(2, 8):
                    link(dve.scalar_tensor_tensor(novf[:, :], cnt[:, :], float(P * j), novf[:, :], ALU.is_gt, ALU.add))
                link(dve.tensor_tensor_scan(incl[:, :], ones[:, 0:NE], novf[:, :], 0.0, ALU.mult, ALU.add))
                link(dve.tensor_tensor(ostart[:, :], incl[:, :], novf[:, :], ALU.subtract))
                for k in range(2):
                    for dst, src in ((rk, rank_e[:, :, :]),
                                     (osk, ostart[:, :].unsqueeze(1).to_broadcast([P, NT, NE])),
                                     (eid, iota_row[:, 0:NE].unsqueeze(1).to_broadcast([P, NT, NE]))):
                        link(dve.tensor_tensor(prod[:, :, :], oef[k], src, ALU.mult))
                        link(dve.tensor_reduce(dst[:, k, :], prod[:, :, :], AX, ALU.add))
                link(dve.tensor_scalar(ob[:, :, :], rk[:, :, :], float(P), None, ALU.is_ge))
                link(dve.tensor_copy(obc[:, :, :], ob[:, :, :]))
                for j in range(2, 8):
                    link(dve.scalar_tensor_tensor(ob[:, :, :], rk[:, :, :], float(P * j), ob[:, :, :], ALU.is_ge, ALU.add))
                link(dve.scalar_tensor_tensor(rk[:, :, :], ob[:, :, :], -float(P), rk[:, :, :], ALU.mult, ALU.add))
                link(dve.scalar_tensor_tensor(blk_k[:, :, :], ob[:, :, :], float(NE - 1), osk[:, :, :], ALU.add, ALU.add))
                link(dve.tensor_tensor(blk_k[:, :, :], blk_k[:, :, :], eid[:, :, :], ALU.subtract))
                link(dve.tensor_tensor(blk_k[:, :, :], blk_k[:, :, :], obc[:, :, :], ALU.mult))
                link(dve.tensor_tensor(blk_k[:, :, :], blk_k[:, :, :], eid[:, :, :], ALU.add))
                for k in range(2):
                    link(dve.tensor_scalar(val[:, k, :], iota_row[:, 0:NT], float(P), float(k * T + 1), ALU.mult, ALU.add))
                link(dve.tensor_scalar(val[:, :, :], val[:, :, :], iota_col[:, :], None, ALU.add))
                for i in range(2 * NT):
                    k, t = divmod(i, NT)
                    if i >= 2:
                        dve.wait_ge(sem("sel_used"), i - 1)
                    link(dve.tensor_scalar(sel_a[i % 2][:, :], iota_row[:, :], rk[:, k, t:t + 1], None, ALU.is_equal))
                    dve.tensor_scalar(sel_b[i % 2][:, :], iota_row[:, 0:NBLK], blk_k[:, k, t:t + 1], val[:, k, t:t + 1],
                                      ALU.is_equal, ALU.mult).then_inc(sem("sel_ready"), 1)
                dve.wait_ge(sem("sel_used"), 2 * NT)
                link(dve.tensor_scalar(tab0[:, :], ps[:, 2, 0:NBLK], 0.0, FAR, ALU.is_equal, ALU.mult))
                link(dve.scalar_tensor_tensor(tabf[:, :], ps[:, 2, 0:NBLK], -1.0, tab0[:, :], ALU.add, ALU.add))
                link(dve.tensor_copy(yidx[:, :], tabf[:, :]))
                link(dve.tensor_scalar(tab0[:, :], tabf[:, :], float(T), -float(T), ALU.is_ge, ALU.mult))
                link(dve.tensor_tensor(tabf[:, :], tabf[:, :], tab0[:, :], ALU.add))
                link(dve.tensor_copy(xidx[:, :], tabf[:, :]))
                link(dve.tensor_copy(ovf_n[0:1, 0:1], incl[0:1, NE - 1:NE]))
                link(dve.tensor_tensor(ovc[0:1, :, :], incl[0:1, :].unsqueeze(1).to_broadcast([1, 16, NE]),
                                       iota_row[0:1, 0:16].unsqueeze(2).to_broadcast([1, 16, NE]), ALU.is_le))
                link(dve.tensor_reduce(ovf[0:1, :], ovc[0:1, :, :], AX, ALU.add))
                link(dve.tensor_scalar(ovf[0:1, :], ovf[0:1, :], float(NE - 1), None, ALU.min))
                dve.tensor_copy(ovf_e[0:1, :], ovf[0:1, :]).then_inc(sem("tab_read"), 1)
            if "E" in on:
                def low(g, e, q, slot):
                    dve.wait_ge(sem("hi_gu"), 2 * e + g + 1)
                    dve.tensor_tensor(we_lo[slot][:, :], raw_e[g][q][:, :], we_hi[slot][:, :].bitcast(F32), ALU.subtract).then_inc(sem("lo_gu"), 1)

                def rows_low(e, q):
                    dve.wait_ge(sem("xst_hi_ready"), e + 1)
                    dve.tensor_tensor(xst_lo[q][:, :, :], ps[:, 0:2, :].rearrange("p b (k c) -> p (b k) c", c=P),
                                      xst_hi[q][:, :, :].bitcast(F32), ALU.subtract).then_inc(sem("xst_ready"), 1)

                def hidden(e):
                    dve.wait_ge(sem("sg_ready"), e + 1)
                    wait(dve, "hid_tr", e)
                    dve.tensor_tensor(hid[:, :], ps[:, 3, 0:DE], sg[:, :], ALU.mult).then_inc(sem("hid_ready"), 1)

                def hidden_low(e):
                    dve.wait_ge(sem("hidt_hi_ready"), e + 1)
                    dve.tensor_tensor(hidt_lo[:, :, :].rearrange("p a b -> p (a b)"), ps[:, 4, 0:2 * P],
                                      hidt_hi[:, :, :].rearrange("p a b -> p (a b)").bitcast(F32), ALU.subtract).then_inc(sem("hidt_ready"), 1)

                def right_half(e, q, used, sent):
                    dve.wait_ge(sem("group_used"), used)
                    wait(dve, f"y_sent{q}", sent)
                    dve.tensor_copy(y[q][:, HALF:D], ps[:, 6, :]).then_inc(sem("y_right"), 1)

                def expert(e, j, left):
                    hidden(e)
                    if left(2):
                        rows_low(e + 2, j % 2)
                    hidden_low(e)
                    if left(2):
                        low(0, e + 2, j % 2, place(0, j + 2) % 4)
                    right_half(e, j % 2, 3 * e + 4 if not (isinstance(e, int) and e == NE - 1) else 3 * NE, 8 * (e - j % 2))
                    if left(2):
                        low(1, e + 2, j % 2, place(1, j + 2) % 4)

                low(0, 0, 0, 0)
                low(1, 0, 0, 1)
                low(0, 1, 1, 2)
                rows_low(0, 0)
                rows_low(1, 1)
                low(1, 1, 1, 0)
                experts(dve, expert)
                n_ovf = dve.value_load(ovf_n[0:1, 0:1], min_val=0, max_val=NOVF)
                with dve.If(n_ovf > 0):
                    with dve.Fori(0, n_ovf) as b:
                        for g in range(2):
                            low(g, b + NE, 0, g)
                        rows_low(b + NE, 0)
                        hidden(b + NE)
                        hidden_low(b + NE)
                        right_half(b + NE, 0, b * 3 + 3 * NE + 3, b * 16 + 16 * (NE // 2))
            if "C" in on:
                dve.wait_ge(sem("gfin_full"), 16)
                for t in range(NT):
                    dve.wait_ge(sem(f"yin_full{t % 2}"), 32 * (t // 2 + 1))
                    if t >= 2:
                        dve.wait_ge(sem("res_ready"), t - 1)
                    link(dve.scalar_tensor_tensor(acc[t % 2][:, :], yin[t % 2][:, 0, :], gatew[:, 0, t:t + 1], x2[:, t, :], ALU.mult, ALU.add))
                    dve.scalar_tensor_tensor(acc[t % 2][:, :], yin[t % 2][:, 1, :], gatew[:, 1, t:t + 1], acc[t % 2][:, :],
                                             ALU.mult, ALU.add).then_inc(sem("acc_ready"), 1)
                    dve.wait_ge(sem("std3_ready"), t + 1)
                    link(dve.reciprocal(rstd[:, 16 + t:17 + t], std[:, 16 + t:17 + t]))
                    if t >= 2:
                        dve.wait_ge(sem(f"res_stored{t % 2}"), 16 * (t // 2))
                    dve.scalar_tensor_tensor(res[t % 2][:, :], acc[t % 2][:, :], rstd[:, 16 + t:17 + t], g_fin[:, :],
                                             ALU.mult, ALU.mult).then_inc(sem("res_ready"), 1)

        @block.gpsimd
        def _(pool):
            pool.iota(iota_row[:, :], [[1, P]], base=0, channel_multiplier=0,
                      allow_small_or_imprecise_dtypes=True).then_inc(sem("iota_ready"), 1)
            pool.iota(iota_col[:, :], [[0, 1]], base=0, channel_multiplier=1,
                      allow_small_or_imprecise_dtypes=True).then_inc(sem("iota_ready"), 1)
            if "Z" in on:
                split_units(pool, 0, NZ)
            if "A" in on:
                def head_split(h):
                    pool.wait_ge(sem(f"hraw_full{h % 2}"), 80 * (h // 2 + 1))
                    if h >= 2:
                        pool.wait_ge(sem("job_done"), 5 * (h - 1))
                    pool.tensor_copy(h_hi[h % 2][:, :], h_raw[h % 2][:, :]).then_inc(sem("hw_hi"), 1)
                    pool.wait_ge(sem("hw_hi"), h + 1)
                    pool.tensor_tensor(h_lo[h % 2][:, :], h_raw[h % 2][:, :], h_hi[h % 2][:, :].bitcast(F32),
                                       ALU.subtract).then_inc(sem("hw_split"), 1)

                head_split(0)
                for h in range(HEADS):
                    for j in range(2):
                        pool.wait_ge(sem("q_hi_ready"), 2 * h + j + 1)
                        pool.tensor_tensor(q_lo[h % 2][:, j * HALF:(j + 1) * HALF], q_tmp[j][:, :],
                                           q_hi[h % 2][:, j * HALF:(j + 1) * HALF].bitcast(F32), ALU.subtract).then_inc(sem("q_lo_ready"), 1)
                    if h + 1 < HEADS:
                        head_split(h + 1)
            if "U" in on:
                split_units(pool, NZ, NZ + NU)
            if "M" in on:
                split_units(pool, NZ + NU, NZ + NU + NM)
            if "E" in on:
                x_copies, y_copies = pool.alloc_register("x_copies"), pool.alloc_register("y_copies")
                pool.reg_mov(x_copies, 0)
                pool.reg_mov(y_copies, 0)
                last_token, last_row = pool.to_reg(T - 1), pool.to_reg(2 * T - 1)

                def gather(blk, j):
                    pool.tensor_copy(xcol[j][:, :], xidx[:, blk]).then_inc(sem("xcol_ready"), 1)
                    pool.reg_add(x_copies, x_copies, 1)
                    pool.wait_ge(sem("tab_read"), 1)
                    pool.wait_ge(sem("xcol_ready"), x_copies)
                    pool.indirect_dma_start(xs[j][:, :], None, h2_dram, bass.IndirectOffsetOnAxis(xcol[j][:, :], 0),
                                            bounds_check=last_token, oob_is_err=False).then_inc(sem(f"xs_full{j}"), 16)

                def scatter(blk, j, sent):
                    wait(pool, f"y_sent{j}", sent)
                    pool.tensor_copy(ycol[j][:, :], yidx[:, blk]).then_inc(sem("ycol_ready"), 1)
                    pool.reg_add(y_copies, y_copies, 1)
                    pool.wait_ge(sem("tab_read"), 1)
                    pool.wait_ge(sem("ycol_ready"), y_copies)
                    pool.indirect_dma_start(y_dram, bass.IndirectOffsetOnAxis(ycol[j][:, :], 0), y[j][:, :], None,
                                            bounds_check=last_row, oob_is_err=False).then_inc(sem(f"y_sent{j}"), 16)

                def down_low(e, q, slot):
                    pool.wait_ge(sem("hi_dn"), e + 1)
                    pool.tensor_tensor(we_lo[slot][:, :], raw_e[2][q][:, :], we_hi[slot][:, :].bitcast(F32), ALU.subtract).then_inc(sem("lo_dn"), 1)

                def expert(e, j, left):
                    if left(4):
                        pool.wait_ge(sem("xs_tr"), e + 1)
                        gather(slice(e + 4, e + 5) if isinstance(e, int) else bass.ds(e + 4, 1), j)
                    if left(1):
                        down_low(e + 1, (j + 1) % 2, place(2, j + 1) % 4)
                    pool.wait_ge(sem("y_left"), e + 1)
                    pool.wait_ge(sem("y_right"), e + 1)
                    scatter(slice(e, e + 1) if isinstance(e, int) else bass.ds(e, 1), j % 2, 8 * (e - j % 2))

                pool.wait_ge(sem("out_done"), NT)
                pool.wait_ge(sem("x2_ready"), NT)
                for j in range(4):
                    pool.memset(xs[j][:, :], 0.0).then_inc(sem("xs_clear"), 1)
                pool.wait_ge(sem("xs_clear"), 4)
                for i in range(2):
                    pool.wait_ge(sem(f"h2_stored{i}"), 16 * NT // 2)
                down_low(0, 0, place(2, 0) % 4)
                pool.wait_ge(sem("tab_read"), 1)
                for j in range(4):
                    gather(slice(j, j + 1), j)
                experts(pool, expert)
                n_ovf = pool.value_load(ovf_n[0:1, 0:1], min_val=0, max_val=NOVF)
                with pool.If(n_ovf > 0):
                    with pool.Fori(0, n_ovf) as b:
                        pool.wait_ge(sem("xs_tr"), b + NE)
                        gather(bass.ds(b + NE, 1), 0)
                        down_low(b + NE, 0, 2)
                        pool.wait_ge(sem("y_left"), b + NE + 1)
                        pool.wait_ge(sem("y_right"), b + NE + 1)
                        scatter(bass.ds(b + NE, 1), 0, b * 16 + 16 * (NE // 2))
                    pool.wait_ge(sem("y_sent0"), n_ovf * 16 + 16 * (NE // 2))
                pool.wait_ge(sem("y_sent0"), 16 * (NE // 2))
                pool.wait_ge(sem("y_sent1"), 16 * (NE // 2))
                pool.memset(junk3[:, 0:1], 0.0).then_inc(sem("y_stored_all"), 1)


_INS = ["x", "positions", "g_attn_norm", "w_in", "g_cq", "w_uq", "g_ckv", "w_uk", "w_uv", "w_o_attn", "sgu_gain",
        "sgu_bias", "w_spatial", "b_spatial", "w_o_sgu", "w_out", "g_ffn_norm", "w_router_group", "b_router_group",
        "w_router_expert", "b_router_expert", "w_exp_gate", "w_exp_up", "w_exp_down", "g_final"]


def kernel(**inputs):
    import numpy as _np
    import concourse.bacc as _bacc
    from concourse import mybir as _mybir
    from concourse.bass_utils import run_bass_kernel_spmd as _run

    nc = _bacc.Bacc("TRN2", target_bir_lowering=False, num_devices=1)
    arrays, args = {}, {}
    for name in _INS:
        arr = _np.ascontiguousarray(inputs[name])
        arrays[f"in_{name}_dram"] = arr
        args[name] = nc.dram_tensor(f"in_{name}_dram", arr.shape, _mybir.dt.from_np(arr.dtype), kind="ExternalInput").ap()
    c = rope_constants()
    arrays["rope_constants_dram"] = c
    args["rope_constants"] = nc.dram_tensor("rope_constants_dram", c.shape, _mybir.dt.float32, kind="ExternalInput").ap()
    out = nc.dram_tensor("out_0_dram", (1, T, D), _mybir.dt.float32, kind="ExternalOutput").ap()
    build(nc, args, out)
    r = _run(nc, [arrays], core_ids=[0])
    return r.results[0]["out_0_dram"]
```

```python
from contextlib import ExitStack

import numpy as np

import concourse.bass as bass
from concourse import mybir

F32 = mybir.dt.float32
F32R = mybir.dt.float32r
BF16 = mybir.dt.bfloat16
I32 = mybir.dt.int32
U32 = mybir.dt.uint32
ALU = mybir.AluOpType
ACT = mybir.ActivationFunctionType
AX = mybir.AxisListType.X

P = 128
D = 1024
T = 1024
NT = T // P
KD = D // P
HALF = 512
EPS = 1e-6
HEADS, NOPE, ROPE, VH = 8, 64, 32, 64
QR, KVR = 256, 128
SCALE = (NOPE + ROPE) ** -0.5
THETA = 10000.0
SGU = 512
KS = SGU // P
CHUNK = 64
G, EPG = 4, 8
NE = G * EPG
DE = 256
NOVF = 15
NBLK = 48
NR = G + NE
C_UV, C_GATE = QR + KVR + ROPE, QR + KVR + ROPE + 2 * SGU
BIG = 1.0e30
FAR = 8192.0
PI_IN = 3.1415925
TWO_PI = 2 * np.pi
C1 = 6.28125
C2 = float(np.float32(np.floor((TWO_PI - C1) * 2 ** 21) / 2 ** 21))
C3 = float(TWO_PI - C1 - C2)
MAGIC = 1.5 * 2 ** 23
KB = 1024
NQ = 64


def rope_constants():
    f = (np.float32(THETA) ** (-np.arange(0, ROPE, 2, dtype=np.float32) / np.float32(ROPE))).astype(np.float32)
    turn = np.concatenate([-f, f])
    c = np.zeros((P, 8), np.float32)
    c[:64, 1], c[:64, 2] = 0.25, np.pi / 2
    c[64:96, 0], c[64:96, 1], c[64:96, 2] = np.concatenate([f, f]), 0.25, np.pi / 2
    c[96:, 0] = turn
    c[:64, 3] = np.concatenate([turn, turn])
    c[64:, 3], c[64:, 4], c[64:, 5] = np.concatenate([f] * 4), 0.25, np.pi / 2
    return c


def chunks_through(s):
    return sum((i % NT) // 4 + 1 for i in range(s + 1))


def build(nc, a, out, stop_after=None):
    base = 16512

    with ExitStack() as ctx:
        def at(name, kb, shape, dt):
            return nc.alloc_sbuf_tensor_at(name, shape, dt, offset=base + int(kb * KB))

        sems = {}

        def sem(name):
            if name not in sems:
                sems[name] = ctx.enter_context(nc.semaphore(name))
            return sems[name]

        ident = at("ident", 0, [P, P], F32)
        iota_row = at("iota_row", 0.5, [P, P], F32)
        ones = at("ones", 1, [P, P], F32)
        mask_l = at("mask_l", 1.5, [P, P], F32R)
        mask_r = at("mask_r", 2, [P, CHUNK], F32R)
        before = at("before", 2.25, [P, P], BF16)
        ones_b = at("ones_b", 2.5, [P, P], BF16)
        iota_col = at("iota_col", 2.75, [P, 1], F32)
        epst = at("epst", 2.78125, [P, 1], F32)
        cst = at("cst", 2.8125, [P, 8], F32)
        gcol = at("gcol", 2.875, [P, 3], F32)
        ssq = at("ssq", 3, [P, 3 * NT], F32)
        std = at("std", 3.125, [P, 3 * NT], F32)
        rstd = at("rstd", 3.25, [P, 3 * NT], F32)
        negm = at("negm", 3.5, [P, NQ], F32)
        lsum = at("lsum", 3.75, [P, NQ], F32)
        rl = at("rl", 4, [P, NQ], F32)
        bnst = at("bnst", 4.25, [P, NT, 6], F32)
        bnag = at("bnag", 4.5, [P, NT, 2], F32)
        gatew = at("gatew", 4.75, [P, 2, NT], F32)
        yidx = at("yidx", 5, [P, NBLK], U32)
        xidx = at("xidx", 5.25, [P, NBLK], U32)
        xcol = [at(f"xcol{i}", 5.75 + i / 32, [P, 1], U32) for i in range(4)]
        ycol = [at(f"ycol{i}", 5.875 + i / 32, [P, 1], U32) for i in range(2)]
        ovf_e = at("ovf_e", 5.5, [1, 16], I32)
        ovf_n = at("ovf_n", 5.625, [1, 8], I32)

        raw = [at(f"raw{i}", 8 + 4 * i, [P, KD, P], F32) for i in range(3)]
        w_hi = [at(f"w_hi{i}", 20 + 8 * i, [P, KD, P], F32R) for i in range(3)]
        w_lo = [at(f"w_lo{i}", 24 + 8 * i, [P, KD, P], F32R) for i in range(3)]
        ht_hi = at("ht_hi", 44, [P, KD, T], F32R)
        ht_lo = at("ht_lo", 76, [P, KD, T], F32R)
        xin = [at(f"xin{i}", 108 + 4 * i, [P, D], F32) for i in range(4)]
        hrow = [at(f"hrow{i}", 124 + 4 * i, [P, D], F32) for i in range(2)]
        g_attn = at("g_attn", 176, [P, D], F32)
        junk = at("junk", 180, [P, D], F32)
        pos_i = at("pos_i", 200, [P, T], I32)
        ang = at("ang", 160, [P, T], F32)
        turns = at("turns", 164, [P, T], F32)
        tab_q = at("tab_q", 132, [P, T], F32)
        tab_k = at("tab_k", 168, [P, T], F32)
        c_raw = at("c_raw", 136, [P, 3, T], F32)
        c_sq = at("c_sq", 148, [P, 3, T], F32)
        c_rs = at("c_rs", 160, [P, 4, HALF], F32)
        kr1 = at("kr1", 192, [P, T], F32)
        kr2 = at("kr2", 196, [P, T], F32)
        c_hi = at("c_hi", 108, [P, 3, T], F32R)
        c_lo = at("c_lo", 120, [P, 3, T], F32R)
        h_raw = at("h_raw", 200, [P, 384], F32)
        h_hi = [at(f"h_hi{i}", 201.5 + 3 * i, [P, 384], F32R) for i in range(2)]
        h_lo = [at(f"h_lo{i}", 203 + 3 * i, [P, 384], F32R) for i in range(2)]
        pt_hi = [at(f"pt_hi{i}", (20, 24, 36, 40)[i], [P, 4, P], F32R) for i in range(4)]
        pt_lo = [at(f"pt_lo{i}", (22, 26, 38, 42)[i], [P, 4, P], F32R) for i in range(4)]
        q_tmp = at("q_tmp", 6, [P, HALF], F32)
        rl_diag = [at(f"rl_diag{i}", 5 + i / 2, [P, P], F32) for i in range(2)]
        q_hi = [at(f"q_hi{i}", 136 + 8 * i, [P, T], F32R) for i in range(2)]
        q_lo = [at(f"q_lo{i}", 140 + 8 * i, [P, T], F32R) for i in range(2)]
        v_hi = [at(f"v_hi{i}", 152 + 4 * i, [P, NT, VH], F32R) for i in range(2)]
        v_lo = [at(f"v_lo{i}", 154 + 4 * i, [P, NT, VH], F32R) for i in range(2)]
        o_t = at("o_t", 160, [P, KS, T], F32)
        k_hi = [at(f"k_hi{i}", 176 + 8 * i, [P, T], F32R) for i in range(2)]
        k_lo = [at(f"k_lo{i}", 180 + 8 * i, [P, T], F32R) for i in range(2)]
        prob = [at(f"prob{i}", 192 + 4 * i, [P, T], F32) for i in range(2)]
        ot_hi = at("ot_hi", 108, [P, KS, T], F32R)
        ot_lo = at("ot_lo", 124, [P, KS, T], F32R)
        st_hi = at("st_hi", 140, [P, NT, KS, P], F32R)
        st_lo = at("st_lo", 156, [P, NT, KS, P], F32R)
        st_f = at("st_f", 156, [P, NT, KS, P], F32)
        v_t = at("v_t", 172, [P, KS, T], F32)
        u_t = at("u_t", 188, [P, KS, T], F32)
        sp_raw = at("sp_raw", 172, [P, 8, P], F32)
        sp_hi = at("sp_hi", 176, [P, 8, P], F32R)
        sp_lo = at("sp_lo", 180, [P, 8, P], F32R)
        sp_b = at("sp_b", 184, [P, KS, P], F32)
        ln_g = at("ln_g", 204, [P, SGU], F32)
        ln_b = at("ln_b", 6, [P, SGU], F32)
        mix = at("mix", 172, [P, KD, T], F32)
        sig_b = [at("sig_b0", 204, [P, HALF], F32), at("sig_b1", 6, [P, HALF], F32)]
        wo_hi = at("wo_hi", 44, [P, KD, D], F32R)
        wo_lo = at("wo_lo", 76, [P, KD, D], F32R)
        mt_hi = [at(f"mt_hi{i}", 108 + 8 * i, [P, KD, P], F32R) for i in range(2)]
        mt_lo = [at(f"mt_lo{i}", 112 + 8 * i, [P, KD, P], F32R) for i in range(2)]
        xre = [at(f"xre{i}", 124 + 4 * i, [P, D], F32) for i in range(2)]
        x2 = at("x2", 132, [P, NT, D], F32)
        h2 = [at(f"h2{i}", 164 + 4 * i, [P, D], F32) for i in range(2)]
        h2t = [at(f"h2t{i}", 20 + 4 * i, [P, KD, P], F32) for i in range(2)]
        g_ffn = at("g_ffn", 28, [P, D], F32)
        w_rt = at("w_rt", 32, [P, KD, NR], F32)
        b_rt = at("b_rt", 33.25, [P, NR], F32)
        junk2 = at("junk2", 34, [P, D], F32)
        r_at = [172.0]

        def scratch(name, shape, dt=F32):
            n = int(np.prod(shape[1:])) * (2 if dt is BF16 else 4)
            t = at(name, r_at[0], shape, dt)
            r_at[0] += -(-n // 32) * 32 / KB
            return t

        logit = at("logit", 38.5, [P, NT, NR], F32)
        iog = scratch("iog", [P, NT, EPG])
        mg = scratch("mg", [P, NT])
        cand = scratch("cand", [P, NT, EPG])
        sel = scratch("sel", [P, NT])
        og = scratch("og", [P, NT, G])
        ex = scratch("ex", [P, NT, G])
        ptop = scratch("ptop", [P, NT])
        lprod = scratch("lprod", [P, NT, G, EPG])
        le = scratch("le", [P, NT, EPG])
        m12 = scratch("m12", [P, 2, NT])
        oh = [scratch(f"oh{k}", [P, NT, EPG]) for k in range(2)]
        oe = [scratch(f"oe{k}", [P, NT, G, EPG]) for k in range(2)]
        oe_b = scratch("oe_b", [P, NT, NE], BF16)
        cum_b = scratch("cum_b", [P, NT + 1, NE], BF16)
        cum = scratch("cum", [P, NT, NE])
        rank_e = scratch("rank_e", [P, NT, NE])
        prod = scratch("prod", [P, NT, NE])
        cnt = scratch("cnt", [P, NE])
        cmp7 = scratch("cmp7", [P, NE])
        novf = scratch("novf", [P, NE])
        incl = scratch("incl", [P, NE])
        ostart = scratch("ostart", [P, NE])
        rk = scratch("rk", [P, 2, NT])
        eid = scratch("eid", [P, 2, NT])
        osk = scratch("osk", [P, 2, NT])
        ob = scratch("ob", [P, 2, NT])
        obc = scratch("obc", [P, 2, NT])
        blk_k = scratch("blk_k", [P, 2, NT])
        val = scratch("val", [P, 2, NT])
        sel_a = [scratch(f"sel_a{i}", [P, P], F32R) for i in range(2)]
        sel_b = [scratch(f"sel_b{i}", [P, NBLK], F32R) for i in range(2)]
        tabf = scratch("tabf", [P, NBLK])
        tab0 = scratch("tab0", [P, NBLK])
        ovc = scratch("ovc", [1, 16, NE])
        ovf = scratch("ovf", [1, 16])
        assert r_at[0] < 188, r_at
        raw_e = [[at(f"raw_e{g}{q}", 8 + 8 * (3 * q + g), [P, 2048], F32) for q in range(2)] for g in range(3)]
        we_hi = [at(f"we_hi{i}", 56 + 16 * i, [P, 2048], F32R) for i in range(4)]
        we_lo = [at(f"we_lo{i}", 64 + 16 * i, [P, 2048], F32R) for i in range(4)]
        xs = [at(f"xs{i}", (128, 188, 192, 196)[i], [P, D], F32) for i in range(4)]
        xst_hi = [at(f"xst_hi{i}", (120, 180)[i], [P, KD, P], F32R) for i in range(2)]
        xst_lo = [at(f"xst_lo{i}", (124, 184)[i], [P, KD, P], F32R) for i in range(2)]
        sg = at("sg", 200, [P, DE], F32)
        hid = at("hid", 201, [P, DE], F32)
        hidt_hi = at("hidt_hi", 202, [P, 2, P], F32R)
        hidt_lo = at("hidt_lo", 203, [P, 2, P], F32R)
        y = [at(f"y{i}", 164 + 4 * i, [P, D], F32) for i in range(2)]
        yin = [at(f"yin{i}", 8 + 8 * i, [P, 2, D], F32) for i in range(NT)]
        g_fin = at("g_fin", 72, [P, D], F32)
        acc = [at(f"acc{i}", 80 + 4 * i, [P, D], F32) for i in range(2)]
        res = [at(f"res{i}", 88 + 4 * i, [P, D], F32) for i in range(NT)]
        junk3 = at("junk3", 120, [P, D], F32)

        ps = ctx.enter_context(nc.psum_tensor("ps", [P, 8, HALF], F32))

        h2_dram = nc.dram_tensor("h2_dram", [T, D], F32, kind="Internal").ap()
        y_dram = nc.dram_tensor("y_dram", [2 * T, D], F32, kind="Internal").ap()

        ctx.enter_context(nc.allow_non_contiguous_dma(reason="small columns and weight slices"))
        block = ctx.enter_context(nc.Block())

        w_in = a["w_in"][0].rearrange("(k p) n -> p k n", p=P)
        w_oa = a["w_o_attn"][0].rearrange("(k p) n -> p k n", p=P)
        w_os = a["w_o_sgu"][0].rearrange("(k p) n -> p k n", p=P)
        w_out = a["w_out"][0].rearrange("(k p) n -> p k n", p=P)
        w_uq = a["w_uq"][0].rearrange("(k p) n -> p k n", p=P)
        x_d = a["x"][0].rearrange("(t p) d -> t p d", p=P)
        out_d = out[0].rearrange("(t p) d -> t p d", p=P)
        wg_d = a["w_exp_gate"][0].rearrange("e (p k) f -> e p (k f)", p=P)
        wu_d = a["w_exp_up"][0].rearrange("e (p k) f -> e p (k f)", p=P)
        wd_d = a["w_exp_down"][0].rearrange("e (p j) d -> e p (j d)", p=P)

        NZ, NU, NM = 4, 8, 3 * KD

        def unit_loads(n):
            r = raw[n % 3]
            if n == 0:
                return [(r[:, :, :], w_in[:, :, QR:QR + KVR])]
            if n == 1:
                c = QR + KVR
                hr = ROPE // 2
                return ([(r[:, :, q * 32:q * 32 + hr], w_in[:, :, c + hr:c + ROPE]) for q in range(2)]
                        + [(r[:, :, q * 32 + hr:q * 32 + 32], w_in[:, :, c:c + hr]) for q in range(2)]
                        + [(r[:, :, q * 32:q * 32 + 32], w_in[:, :, c:c + ROPE]) for q in (2, 3)])
            if n < NZ:
                return [(r[:, :, :], w_in[:, :, (n - 2) * P:(n - 1) * P])]
            if n < NZ + NU:
                c = C_UV + (n - NZ + KS) % NU * P
                return [(r[:, :, :], w_in[:, :, c:c + P])]
            f, kind = divmod(n - NZ - NU, 3)
            if kind < 2:
                c = C_GATE + kind * D + f * P
                return [(r[:, :, :], w_in[:, :, c:c + P])]
            return [(r[:, 0:KS, :], w_oa[:, :, f * P:(f + 1) * P]),
                    (r[:, KS:, :], w_os[:, :, f * P:(f + 1) * P])]

        raw_count = [0, 0, 0]
        raw_value = {}
        for n in range(NZ + NU + NM):
            raw_count[n % 3] += 16 * len(unit_loads(n))
            raw_value[n] = raw_count[n % 3]

        def unit_used(eng, n):
            if n < NZ:
                eng.wait_ge(sem("z_done"), 2 * n + 2)
            elif n < NZ + NU:
                eng.wait_ge(sem("uv_done"), 2 * (n - NZ) + 2)
            else:
                eng.wait_ge(sem("unit_done"), n - NZ - NU + 1)

        def load_units(sp, lo, hi):
            for n in range(lo, hi):
                if n >= 3:
                    sp.wait_ge(sem("w_split"), n - 2)
                for dst, src in unit_loads(n):
                    sp.dma_start(dst, src).then_inc(sem(f"raw_full{n % 3}"), 16)

        def split_units(pool, lo, hi):
            for n in range(lo, hi):
                pool.wait_ge(sem(f"raw_full{n % 3}"), raw_value[n])
                if n >= 3:
                    unit_used(pool, n - 3)
                pool.tensor_copy(w_hi[n % 3][:, :, :], raw[n % 3][:, :, :]).then_inc(sem("w_hi_done"), 1)
                pool.wait_ge(sem("w_hi_done"), n + 1)
                pool.tensor_tensor(w_lo[n % 3][:, :, :], raw[n % 3][:, :, :],
                                   w_hi[n % 3][:, :, :].bitcast(F32), ALU.subtract).then_inc(sem("w_split"), 1)

        def mm3(pe, dst, st, mv, first, last):
            pe.matmul(dst, st[0], mv[0], start=first, stop=False)
            pe.matmul(dst, st[0], mv[1], start=False, stop=False)
            return pe.matmul(dst, st[1], mv[0], start=False, stop=last)

        def place(g, e):
            return (3 * e - 1, 3 * e + 1, 3 * e + 3)[g] if not (isinstance(e, int) and e == 0 and g == 0) else 0

        def wait(eng, name, value):
            if not (isinstance(value, int) and value <= 0):
                eng.wait_ge(sem(name), value)

        def experts(eng, body):
            for j in range(4):
                body(j, j, lambda n: True)
            with eng.Fori(1, NE // 4 - 1) as it:
                for j in range(4):
                    body(it * 4 + j, j, lambda n: True)
            for j in range(4):
                e = NE - 4 + j
                body(e, j, lambda n, e=e: e + n < NE)

        def fourth(e, j):
            return e // 4 if isinstance(e, int) else (e - j) // 4

        def v_tiles_after(jj):
            return {8: (0,), 9: (1, 2), 10: (3,), 11: (4, 5), 12: (6,), 13: (7,)}.get(jj, ())

        stages = ["X", "Z", "A", "O", "U", "L", "M", "W", "R", "E", "C"]
        on = stages if stop_after is None else stages[:stages.index(stop_after) + 1]

        @block.sync
        def _(sp):
            sp.dma_start(cst[:, :], a["rope_constants"]).then_inc(sem("cst_full"), 16)
            sp.dma_start(pos_i[:, :], a["positions"].to_broadcast([P, T])).then_inc(sem("pos_full"), 16)
            sp.dma_start(g_attn[:, :], a["g_attn_norm"].to_broadcast([P, D])).then_inc(sem("g_full"), 16)
            for t in range(NT):
                if t >= 4:
                    sp.wait_ge(sem("hrow_ready"), t - 3)
                sp.dma_start(xin[t % 4][:, :], x_d[t]).then_inc(sem(f"x_full{t % 4}"), 16)
                if t == 3:
                    load_units(sp, 0, 3)
            sp.dma_start(gcol[:, 0:1], a["g_ckv"].rearrange("a p -> p a")).then_inc(sem("gcol_full"), 16)
            sp.dma_start(gcol[:, 1:3], a["g_cq"].rearrange("a (k p) -> p (a k)", p=P)).then_inc(sem("gcol_full"), 16)
            if "Z" in on:
                load_units(sp, 3, NZ)
            if "A" in on:
                sp.wait_ge(sem("ang_ready"), 2)
                for h in range(HEADS):
                    if h >= 1:
                        sp.wait_ge(sem("hw_split"), h)
                    f = sem("hraw_full")
                    q = h_raw[:, 0:256].rearrange("p (k c) -> p k c", k=2)
                    c = h * (NOPE + ROPE)
                    sp.dma_start(q[:, :, 0:96], w_uq[:, :, c:c + 96]).then_inc(f, 16)
                    sp.dma_start(q[:, :, 96:112], w_uq[:, :, c + 80:c + 96]).then_inc(f, 16)
                    sp.dma_start(q[:, :, 112:128], w_uq[:, :, c + 64:c + 80]).then_inc(f, 16)
                    sp.dma_start(h_raw[:, 256:320], a["w_uk"][0][:, h * 64:h * 64 + 64]).then_inc(f, 16)
                    sp.dma_start(h_raw[:, 320:384], a["w_uv"][0][:, h * 64:h * 64 + 64]).then_inc(f, 16)
                    if h == 1 and "U" in on:
                        load_units(sp, NZ, NZ + 3)
            if "U" in on:
                sp.wait_ge(sem("job_done"), 5 * HEADS)
                sp.dma_start(ln_g[:, :], a["sgu_gain"].to_broadcast([P, SGU])).then_inc(sem("ln_full"), 16)
                sp.wait_ge(sem("q_lo_ready"), 2 * HEADS)
                sp.dma_start(ln_b[:, :], a["sgu_bias"].to_broadcast([P, SGU])).then_inc(sem("ln_full"), 16)
                load_units(sp, NZ + 3, NZ + NU)
            if "M" in on:
                load_units(sp, NZ + NU, NZ + NU + 1)
                sp.wait_ge(sem("v_tr"), NT)
                sp.dma_start(sp_raw[:, :, :], a["w_spatial"][0].rearrange("g i j -> i g j")).then_inc(sem("spraw_full"), 16)
                bs = a["b_spatial"].rearrange("a (q h) i -> a h q i", h=2)
                for hh in range(2):
                    sp.dma_start(sp_b[64 * hh:64 * hh + 64, :, :],
                                 bs[:, hh].to_broadcast([64, KS, P])).then_inc(sem("spb_full"), 16)
                load_units(sp, NZ + NU + 1, NZ + NU + NM)
            if "W" in on:
                nu = NZ + NU + NM
                sp.wait_ge(sem("w_split"), nu)
                for k in range(KD):
                    if k >= 3:
                        sp.wait_ge(sem("wo_split"), k - 2)
                    sp.dma_start(raw[k % 3][:, :, :].rearrange("p a b -> p (a b)"),
                                 w_out[:, k, :]).then_inc(sem(f"wo_full{k % 3}"), 16)
                sp.wait_ge(sem("unit_done"), NM)
                sp.dma_start(g_ffn[:, :], a["g_ffn_norm"].to_broadcast([P, D])).then_inc(sem("rt_full"), 16)
                sp.dma_start(w_rt[:, :, 0:G], a["w_router_group"][0].rearrange("(k p) g -> p k g", p=P)).then_inc(sem("rt_full"), 16)
                for g in range(G):
                    sp.dma_start(w_rt[:, :, G + g * EPG:G + (g + 1) * EPG],
                                 a["w_router_expert"][0, g].rearrange("(k p) e -> p k e", p=P)).then_inc(sem("rt_full"), 16)
                sp.dma_start(b_rt[:, 0:G], a["b_router_group"].to_broadcast([P, G])).then_inc(sem("rt_full"), 16)
                sp.dma_start(b_rt[:, G:NR], a["b_router_expert"].rearrange("a g e -> a (g e)").to_broadcast([P, NE])).then_inc(sem("rt_full"), 16)
                for t in range(NT):
                    if t >= 2:
                        sp.wait_ge(sem("x2_ready"), t - 1)
                    sp.dma_start(xre[t % 2][:, :], x_d[t]).then_inc(sem(f"xre_full{t % 2}"), 16)
                    if t >= 1:
                        sp.wait_ge(sem("h2_ready"), t)
                        sp.dma_start(h2_dram[(t - 1) * P:t * P, :], h2[(t - 1) % 2][:, :]).then_inc(sem(f"h2_stored{(t - 1) % 2}"), 16)
                sp.wait_ge(sem("h2_ready"), NT)
                sp.dma_start(h2_dram[(NT - 1) * P:NT * P, :], h2[(NT - 1) % 2][:, :]).then_inc(sem(f"h2_stored{(NT - 1) % 2}"), 16)
            if "E" in on:
                sp.wait_ge(sem("out_done"), NT)
                sp.wait_ge(sem("rt_done"), NT)
                sp.wait_ge(sem("logit_ready"), NT)
                sp.wait_ge(sem("logit_read"), 1)

                def load_expert(e, q, free_gu, free_dn, src):
                    for g, w_d in enumerate((wg_d, wu_d, wd_d)):
                        if g < 2:
                            wait(sp, "lo_gu", free_gu + g)
                        else:
                            wait(sp, "lo_dn", free_dn)
                        sp.dma_start(raw_e[g][q][:, :], w_d[bass.ds(src, 1)].rearrange("e p n -> (e p) n")).then_inc(
                            sem(f"raw_e_full{g}{q}"), 16)

                experts(sp, lambda e, j, left: load_expert(e, j % 2, 2 * e - 3, e - 1, e))
                sp.wait_ge(sem("tab_read"), 1)
                n_ovf = sp.value_load(ovf_n[0:1, 0:1], min_val=0, max_val=NOVF)
                with sp.If(n_ovf > 0):
                    with sp.Fori(0, n_ovf) as b:
                        e = sp.value_load(ovf_e[0:1, bass.ds(b, 1)], min_val=0, max_val=NE - 1)
                        load_expert(b + NE, 0, 2 * b + 2 * NE - 1, b + NE, e)
            if "C" in on:
                sp.wait_ge(sem("y_stored_all"), 1)
                sp.dma_start(g_fin[:, :], a["g_final"].rearrange("(a d) -> a d", a=1).to_broadcast([P, D])).then_inc(sem("gfin_full"), 16)
                for t in range(NT):
                    if t >= 4:
                        sp.wait_ge(sem("acc_ready"), t - 3)
                    for k in range(2):
                        r0 = k * T + t * P
                        sp.dma_start(yin[t][:, k, :], y_dram[r0:r0 + P, :]).then_inc(sem(f"yin_full{t % 4}"), 16)
                for t in range(NT):
                    sp.wait_ge(sem("res_ready"), t + 1)
                    sp.dma_start(out_d[t], res[t][:, :]).then_inc(sem("res_stored"), 16)
                sp.wait_ge(sem("res_stored"), 16 * NT)

        @block.tensor
        def _(pe):
            for t in range(NT):
                pe.wait_ge(sem("hrow_ready"), t + 1)
                if t == 0:
                    pe.wait_ge(sem("const_ready"), 1)
                if t >= 2:
                    pe.wait_ge(sem("ht_lo_ready"), t - 1)
                b = 2 * (t % 2)
                for k in range(KD):
                    mm = pe.transpose(ps[:, b + k // 4, (k % 4) * P:(k % 4) * P + P],
                                      hrow[t % 2][:, k * P:(k + 1) * P], ident[:, :])
                mm.then_inc(sem("x_tr"), 1)
            if "Z" in on:
                for u in range(NZ):
                    pe.wait_ge(sem("w_split"), u + 1)
                    for c in range(2):
                        pe.wait_ge(sem("ht_lo_ready"), 4 * (c + 1) if u == 0 else NT)
                        dst = ps[:, (2 * u + c + 4) % 8, :]
                        for k in range(KD):
                            mm = mm3(pe, dst, (w_hi[u % 3][:, k, :], w_lo[u % 3][:, k, :]),
                                     (ht_hi[:, k, c * HALF:(c + 1) * HALF], ht_lo[:, k, c * HALF:(c + 1) * HALF]),
                                     k == 0, k == KD - 1)
                        mm.then_inc(sem("z_done"), 1)
                pe.wait_ge(sem("c_sq_ready"), 2)
                for c in range(2):
                    pe.matmul(ps[:, 4 + c, :], ones[:, :], c_sq[:, 0, c * HALF:(c + 1) * HALF],
                              start=True, stop=True).then_inc(sem("ms_done"), 1)
                pe.wait_ge(sem("c_sq_ready"), 6)
                pe.wait_ge(sem("kr_read"), 2)
                for c in range(2):
                    pe.matmul(ps[:, 6 + c, :], ones[:, :], c_sq[:, 1, c * HALF:(c + 1) * HALF], start=True, stop=False)
                    pe.matmul(ps[:, 6 + c, :], ones[:, :], c_sq[:, 2, c * HALF:(c + 1) * HALF],
                              start=False, stop=True).then_inc(sem("ms_done"), 1)
            if "A" in on:
                def job(h, j):
                    hh, hl = h_hi[h % 2], h_lo[h % 2]
                    if j == 0:
                        pe.wait_ge(sem("hw_split"), h + 1)
                    if j in (1, 3):
                        pe.wait_ge(sem("q_tmp_ready"), 2 * h + j // 2 + 1)
                    elif h or j:
                        pe.wait_ge(sem("kv_lo_ready"), 3 * h + j // 2)
                    cs = slice((j // 2) * HALF, (j // 2 + 1) * HALF)
                    if j in (0, 2):
                        for k in range(2):
                            mm = mm3(pe, ps[:, 7, :], (hh[:, k * P:(k + 1) * P], hl[:, k * P:(k + 1) * P]),
                                     (c_hi[:, 1 + k, cs], c_lo[:, 1 + k, cs]), k == 0, k == 1)
                    elif j < 4:
                        mm = mm3(pe, ps[:, 7, :], (hh[:, 256:384], hl[:, 256:384]),
                                 (c_hi[:, 0, cs], c_lo[:, 0, cs]), True, True)
                    else:
                        for t in range(NT):
                            ts = slice(t * P, (t + 1) * P)
                            mm = mm3(pe, ps[:, 7, t * VH:(t + 1) * VH], (c_hi[:, 0, ts], c_lo[:, 0, ts]),
                                     (hh[:, 320:384], hl[:, 320:384]), True, True)
                    mm.then_inc(sem("job_done"), 1)

                def scores(s):
                    h, i = divmod(s, NT)
                    pe.wait_ge(sem("q_lo_ready"), 2 * h + 1 + i // 4)
                    pe.wait_ge(sem("kv_lo_ready"), 3 * h + 1 + i // 4)
                    if s >= 2:
                        pe.wait_ge(sem("exp_done"), s - 1)
                    qs = slice(i * P, (i + 1) * P)
                    n = (i + 1) * P
                    for c in range(i // 4 + 1):
                        m = min(n - c * HALF, HALF)
                        dst = ps[:, 2 * (s % 2) + c, :]
                        last = c == i // 4
                        mm = mm3(pe, dst[:, 0:m], (q_hi[h % 2][:, qs], q_lo[h % 2][:, qs]),
                                 (k_hi[h % 2][:, c * HALF:c * HALF + m], k_lo[h % 2][:, c * HALF:c * HALF + m]),
                                 True, not last)
                        if last:
                            mm = pe.matmul(dst[:, m - CHUNK:m], mask_l[:, :], mask_r[:, :], start=False, stop=True)
                    mm.then_inc(sem("s_done"), 1)

                def prob_transposes(s):
                    i = s % NT
                    c0 = chunks_through(s - 1) if s else 0
                    pe.wait_ge(sem("diag_ready"), s + 1)
                    for c in range(i // 4 + 1):
                        if c0 + c >= 2:
                            pe.wait_ge(sem("pt_lo_ready"), c0 + c - 1)
                        for j in range(4 * c, min(4 * c + 4, i + 1)):
                            mm = pe.matmul(ps[:, 4 + (c0 + c) % 2, (j % 4) * P:(j % 4) * P + P],
                                           prob[s % 2][:, j * P:(j + 1) * P], rl_diag[s % 2][:, :], start=True, stop=True)
                        mm.then_inc(sem("pt_done"), 1)

                def values(s):
                    h, i = divmod(s, NT)
                    c0 = chunks_through(s - 1) if s else 0
                    pe.wait_ge(sem("kv_lo_ready"), 3 * h + 3)
                    pe.wait_ge(sem("pt_lo_ready"), chunks_through(s))
                    if s and s % 4 == 0:
                        pe.wait_ge(sem("o_ready"), s // 4)
                    dst = ps[0:VH, 6, (i % 4) * P:(i % 4 + 1) * P]
                    for j in range(i + 1):
                        c = (c0 + j // 4) % 4
                        mm = mm3(pe, dst, (v_hi[h % 2][:, j, :], v_lo[h % 2][:, j, :]),
                                 (pt_hi[c][:, j % 4, :], pt_lo[c][:, j % 4, :]), j == 0, j == i)
                    mm.then_inc(sem("pv_done"), 1)

                pe.wait_ge(sem("c_lo_ready"), 6)
                pe.wait_ge(sem("c_std_ready"), 4)
                for j in range(5):
                    job(0, j)
                scores(0)
                scores(1)
                for s in range(NQ):
                    prob_transposes(s)
                    if s + 2 < NQ:
                        scores(s + 2)
                    if s:
                        values(s - 1)
                    h, i = divmod(s, NT)
                    if i < 5 and h + 1 < HEADS:
                        job(h + 1, i)
                values(NQ - 1)
            if "U" in on:
                def v_rows(t):
                    pe.wait_ge(sem("gelu_ready"), NU)
                    if t >= 2:
                        pe.wait_ge(sem("ln_read"), t - 1)
                    else:
                        pe.wait_ge(sem("pt_lo_ready"), chunks_through(NQ - 1))
                    for j in range(KS):
                        mm = pe.transpose(ps[:, 4 + t % 2, j * P:(j + 1) * P], v_t[:, j, t * P:(t + 1) * P], ident[:, :])
                    mm.then_inc(sem("v_tr"), 1)

                pe.wait_ge(sem("exp_done"), NQ)
                for n in range(NZ, NZ + NU):
                    pe.wait_ge(sem("w_split"), n + 1)
                    for c in range(2):
                        jj = 2 * (n - NZ) + c
                        if jj >= 4:
                            pe.wait_ge(sem("gelu_ready"), jj - 3)
                        cs = slice(c * HALF, (c + 1) * HALF)
                        for k in range(KD):
                            mm = mm3(pe, ps[:, jj % 4, :], (w_hi[n % 3][:, k, :], w_lo[n % 3][:, k, :]),
                                     (ht_hi[:, k, cs], ht_lo[:, k, cs]), k == 0, k == KD - 1)
                        mm.then_inc(sem("uv_done"), 1)
                        for t in v_tiles_after(jj):
                            v_rows(t)
            if "M" in on:
                def spatial(t):
                    pe.wait_ge(sem("sp_lo_ready"), 1)
                    pe.wait_ge(sem("vn_lo_ready"), t + 1)
                    if t >= 2:
                        pe.wait_ge(sem("s_read"), 2 * (t - 1))
                    for pr in range(KS):
                        gs = slice(2 * pr, 2 * pr + 2)
                        mm = mm3(pe, ps[:, 4 + 2 * (t % 2) + pr // 2, (pr % 2) * 256:(pr % 2) * 256 + 256],
                                 (st_hi[:, t, pr, :], st_lo[:, t, pr, :]),
                                 (sp_hi[:, gs, :].rearrange("p a b -> p (a b)"), sp_lo[:, gs, :].rearrange("p a b -> p (a b)")),
                                 True, True)
                    mm.then_inc(sem("sp_done"), 1)

                pe.wait_ge(sem("sp_masked"), 1)
                pe.wait_ge(sem("o_ready"), NQ // 4)
                for g in range(8):
                    mm = pe.transpose(ps[:, 6 + g // 4, (g % 4) * P:(g % 4) * P + P], sp_raw[:, g, :], ident[:, :])
                mm.then_inc(sem("sp_tr"), 1)
                for f in range(KD):
                    for kind in range(2):
                        n = NZ + NU + 3 * f + kind
                        pe.wait_ge(sem("w_split"), n + 1)
                        if f:
                            pe.wait_ge(sem("sig_a_ready" if kind == 0 else "sig_b_ready"), 2 * f)
                        else:
                            pe.wait_ge(sem("gelu_ready"), 2 * NU)
                        wh, wl = w_hi[n % 3], w_lo[n % 3]
                        for c in range(2):
                            cs = slice(c * HALF, (c + 1) * HALF)
                            for k in range(KD):
                                mm = mm3(pe, ps[:, 2 * kind + c, :], (wh[:, k, :], wl[:, k, :]),
                                         (ht_hi[:, k, cs], ht_lo[:, k, cs]), k == 0, k == KD - 1)
                            if c:
                                mm.then_inc(sem("unit_done"), 1)
                            if f == 0:
                                for t in range(4 * kind + 2 * c, 4 * kind + 2 * c + 2):
                                    spatial(t)
                    n = NZ + NU + 3 * f + 2
                    pe.wait_ge(sem("w_split"), n + 1)
                    if f:
                        pe.wait_ge(sem("mix_ready"), 2 * f)
                    else:
                        pe.wait_ge(sem("s_read"), 2 * NT)
                        pe.wait_ge(sem("ot_lo_ready"), KS)
                    wh, wl = w_hi[n % 3], w_lo[n % 3]
                    for c in range(2):
                        cs = slice(c * HALF, (c + 1) * HALF)
                        for k in range(KS):
                            mm3(pe, ps[:, 4 + c, :], (wh[:, k, :], wl[:, k, :]),
                                (ot_hi[:, k, cs], ot_lo[:, k, cs]), k == 0, k == KS - 1)
                    pe.wait_ge(sem("s_lo_ready"), NT)
                    for c in range(2):
                        for k in range(KS):
                            mm = mm3(pe, ps[:, 6 + c, :].rearrange("p (t q) -> p t q", q=P), (wh[:, KS + k, :], wl[:, KS + k, :]),
                                     (st_hi[:, 4 * c:4 * c + 4, k, :], st_lo[:, 4 * c:4 * c + 4, k, :]), k == 0, k == KS - 1)
                    mm.then_inc(sem("unit_done"), 1)
            if "W" in on:
                pe.wait_ge(sem("mix_ready"), 2 * KD)

                def router(t):
                    pe.wait_ge(sem("h2_ready"), t + 1)
                    if t >= 1:
                        pe.wait_ge(sem("h2t_ready"), t)
                    for k in range(KD):
                        mm = pe.transpose(ps[:, 4 + k // 4, (k % 4) * P:(k % 4) * P + P],
                                          h2[t % 2][:, k * P:(k + 1) * P], ident[:, :])
                    mm.then_inc(sem("h2_tr"), 1)
                    pe.wait_ge(sem("h2t_ready"), t + 1)
                    pe.wait_ge(sem("rt_full"), 16 * 8)
                    if t >= 1:
                        pe.wait_ge(sem("logit_ready"), t)
                    for k in range(KD):
                        mm = pe.matmul(ps[:, 6, 0:NR], h2t[t % 2][:, k, :], w_rt[:, k, :], start=(k == 0), stop=(k == KD - 1))
                    mm.then_inc(sem("rt_done"), 1)

                for t in range(NT):
                    pe.wait_ge(sem("mt_lo_ready"), t + 1)
                    if t >= 2:
                        pe.wait_ge(sem("x2_ready"), t - 1)
                    for k in range(KD):
                        if t == 0:
                            pe.wait_ge(sem("wo_split"), k + 1)
                        for c in range(2):
                            cs = slice(c * HALF, (c + 1) * HALF)
                            mm = mm3(pe, ps[:, 2 * (t % 2) + c, :], (mt_hi[t % 2][:, k, :], mt_lo[t % 2][:, k, :]),
                                     (wo_hi[:, k, cs], wo_lo[:, k, cs]), k == 0, k == KD - 1)
                    mm.then_inc(sem("out_done"), 1)
                    if t >= 1:
                        router(t - 1)
                router(NT - 1)
            if "R" in on:
                pe.wait_ge(sem("oe_ready"), 1)
                pe.matmul(ps[:, 0, 0:NT * NE], before[:, :], oe_b[:, :, :].rearrange("p t e -> p (t e)"), start=True, stop=False)
                pe.matmul(ps[:, 0, 0:NT * NE], ones_b[:, :], cum_b[:, 0:NT, :].rearrange("p t e -> p (t e)"),
                          start=False, stop=True)
                pe.matmul(ps[:, 1, 0:NE], ones_b[:, :], cum_b[:, NT, :], start=True, stop=True).then_inc(sem("rank_done"), 1)
                for i in range(2 * NT):
                    pe.wait_ge(sem("sel_ready"), i + 1)
                    pe.matmul(ps[:, 2, 0:NBLK], sel_a[i % 2][:, :], sel_b[i % 2][:, :], start=(i == 0),
                              stop=(i == 2 * NT - 1)).then_inc(sem("sel_used"), 1)
            if "E" in on:
                def rows_in(e, j, full=None):
                    pe.wait_ge(sem(f"xs_full{j % 4}"), 16 * (fourth(e, j) + 1) if full is None else full)
                    wait(pe, "xst_ready", e)
                    v = xs[j % 4][:, :].rearrange("s (p k) -> s k p", k=KD)
                    for k in range(KD):
                        mm = pe.transpose(ps[:, k // 4, (k % 4) * P:(k % 4) * P + P], v[:, k, :], ident[:, :])
                    mm.then_inc(sem("xs_tr"), 1)

                def columns(e, j, g, slot):
                    pe.wait_ge(sem("xst_ready"), e + 1)
                    pe.wait_ge(sem("lo_gu"), 2 * e + g + 1)
                    q = j % 2
                    for k in range(KD):
                        ws = slice(k * DE, (k + 1) * DE)
                        mm = mm3(pe, ps[:, 2 + g, 0:DE], (xst_hi[q][:, k, :], xst_lo[q][:, k, :]),
                                 (we_hi[slot][:, ws], we_lo[slot][:, ws]), k == 0, k == KD - 1)
                    mm.then_inc(sem("group_used"), 1)

                def hidden_in(e):
                    pe.wait_ge(sem("hid_ready"), e + 1)
                    v = hid[:, :].rearrange("s (p q) -> s q p", q=2)
                    for q in range(2):
                        mm = pe.transpose(ps[:, 4, q * P:(q + 1) * P], v[:, q, :], ident[:, :])
                    mm.then_inc(sem("hid_tr"), 1)

                def down(e, slot):
                    pe.wait_ge(sem("hidt_ready"), e + 1)
                    pe.wait_ge(sem("lo_dn"), e + 1)
                    wait(pe, "y_left", e)
                    wait(pe, "y_right", e)
                    for c in range(2):
                        for q in range(2):
                            ws = slice(q * D + c * HALF, q * D + (c + 1) * HALF)
                            mm = mm3(pe, ps[:, 5 + c, :], (hidt_hi[:, q, :], hidt_lo[:, q, :]),
                                     (we_hi[slot][:, ws], we_lo[slot][:, ws]), q == 0, q == 1)
                    mm.then_inc(sem("group_used"), 1)

                def expert(e, j, left):
                    columns(e, j, 1, place(1, j) % 4)
                    if left(2):
                        rows_in(e + 2, j + 2, None if isinstance(e, int) else 16 * ((e - j) // 4 + (j + 2) // 4 + 1))
                    hidden_in(e)
                    if left(1):
                        columns(e + 1, j + 1, 0, place(0, j + 1) % 4)
                    down(e, place(2, j) % 4)

                pe.wait_ge(sem("tab_read"), 1)
                rows_in(0, 0)
                rows_in(1, 1)
                columns(0, 0, 0, 0)
                experts(pe, expert)
                n_ovf = pe.value_load(ovf_n[0:1, 0:1], min_val=0, max_val=NOVF)
                with pe.If(n_ovf > 0):
                    rows_in(NE, 0)
                    with pe.Fori(0, n_ovf) as b:
                        for g in range(2):
                            columns(b + NE, 0, g, g + 1)
                        rows_in(b + NE + 1, 0, 16 * (b + NE // 4 + 2))
                        hidden_in(b + NE)
                        down(b + NE, 3)

        @block.scalar
        def _(act):
            act.wait_ge(sem("const_ready"), 1)

            def ht_high(t):
                act.wait_ge(sem("x_tr"), t + 1)
                b = 2 * (t % 2)
                act.activation(ht_hi[:, :, t * P:(t + 1) * P],
                               ps[:, b:b + 2, :].rearrange("p b (k c) -> p (b k) c", c=P), ACT.Copy).then_inc(sem("ht_hi_ready"), 1)

            for t in range(NT):
                act.wait_ge(sem(f"x_full{t % 4}"), 16 * (t // 4 + 1))
                if t:
                    act.wait_ge(sem("ssq_ready"), t)
                act.activation(junk[:, :], xin[t % 4][:, :], ACT.Square, accum_out=ssq[:, t:t + 1]).then_inc(sem("ssq_ready"), 1)
                act.wait_ge(sem("ssq_ready"), t + 1)
                act.activation(std[:, t:t + 1], ssq[:, t:t + 1], ACT.Sqrt, scale=1.0 / D, bias=epst[:, :]).then_inc(sem("std_ready"), 1)
                if t:
                    ht_high(t - 1)
            ht_high(NT - 1)
            if "Z" in on:
                for j in range(2):
                    act.wait_ge(sem("ang_ready"), j + 1)
                    act.activation((tab_q if j == 0 else tab_k)[:, :], ang[:, :], ACT.Sin).then_inc(sem("sin_ready"), 1)
                for i, u in enumerate((0, 2, 3)):
                    for c in range(2):
                        cs = slice(c * HALF, (c + 1) * HALF)
                        act.wait_ge(sem("z_done"), 2 * u + c + 1)
                        src = ps[:, (2 * u + c + 4) % 8, :]
                        act.activation(c_raw[:, i, cs], src, ACT.Copy).then_inc(sem("c_raw_ready"), 1)
                        act.activation(c_sq[:, i, cs], src, ACT.Square).then_inc(sem("c_sq_ready"), 1)
                for i in range(4):
                    act.wait_ge(sem("ms_done"), i + 1)
                    act.activation(c_rs[:, i, :], ps[:, 4 + i, :], ACT.Sqrt, scale=1.0 / (KVR if i < 2 else QR),
                                   bias=epst[:, :]).then_inc(sem("c_std_ready"), 1)
                for i in range(6):
                    cs = slice((i % 2) * HALF, (i % 2 + 1) * HALF)
                    act.wait_ge(sem("cn_ready"), i + 1)
                    act.activation(c_hi[:, i // 2, cs], c_raw[:, i // 2, cs], ACT.Copy).then_inc(sem("c_hi_ready"), 1)
            if "A" in on:
                def job_high(h, j):
                    act.wait_ge(sem("job_done"), 5 * h + j + 1)
                    cs = slice((j // 2) * HALF, (j // 2 + 1) * HALF)
                    if j in (0, 2):
                        act.wait_ge(sem("q_tmp_ready"), 2 * h + j // 2 + 1)
                        act.activation(q_hi[h % 2][:, cs], q_tmp[:, :], ACT.Copy).then_inc(sem("q_hi_ready"), 1)
                    elif j < 4:
                        act.activation(k_hi[h % 2][0:64, cs], ps[0:64, 7, :], ACT.Copy).then_inc(sem("kv_hi_ready"), 1)
                    else:
                        act.activation(v_hi[h % 2][:, :, :].rearrange("p t c -> p (t c)"), ps[:, 7, :], ACT.Copy).then_inc(sem("kv_hi_ready"), 1)

                def outputs(g):
                    h, c = divmod(g, 2)
                    r = (h % 2) * VH
                    act.wait_ge(sem("pv_done"), 4 * g + 4)
                    act.activation(o_t[r:r + VH, h // 2, c * HALF:(c + 1) * HALF], ps[0:VH, 6, :], ACT.Copy).then_inc(sem("o_ready"), 1)

                def exponent(s):
                    n = (s % NT + 1) * P
                    act.wait_ge(sem("max_ready"), s + 1)
                    if s >= 2:
                        act.wait_ge(sem("pt_done"), chunks_through(s - 2))
                    b = 2 * (s % 2)
                    act.activation(prob[s % 2][:, 0:n], ps[:, b:b + 2, :].rearrange("p b c -> p (b c)")[:, 0:n], ACT.Exp,
                                   bias=negm[:, s:s + 1], accum_out=lsum[:, s:s + 1]).then_inc(sem("exp_done"), 1)

                for j in range(5):
                    job_high(0, j)
                exponent(0)
                for s in range(NQ):
                    h, i = divmod(s, NT)
                    if s + 1 < NQ:
                        exponent(s + 1)
                    c0 = chunks_through(s - 1) if s else 0
                    for c in range(i // 4 + 1):
                        w = min(4, i + 1 - 4 * c)
                        cc = c0 + c
                        act.wait_ge(sem("pt_done"), cc + 1)
                        if cc >= 4:
                            used = next(x for x in range(s + 1) if chunks_through(x) > cc - 4)
                            act.wait_ge(sem("pv_done"), used + 1)
                        act.activation(pt_hi[cc % 4][:, 0:w, :].rearrange("p a b -> p (a b)"), ps[:, 4 + cc % 2, 0:w * P],
                                       ACT.Copy).then_inc(sem("pt_hi_ready"), 1)
                    if s % 4 == 0 and s:
                        outputs(s // 4 - 1)
                    if i < 5 and h + 1 < HEADS:
                        job_high(h + 1, i)
                outputs(NQ // 4 - 1)
            if "O" in on:
                act.wait_ge(sem("o_ready"), NQ // 4)
                for k in range(KS):
                    act.activation(ot_hi[:, k, :], o_t[:, k, :], ACT.Copy).then_inc(sem("ot_hi_ready"), 1)
            if "U" in on:
                act.wait_ge(sem("ot_lo_ready"), KS)
                for jj in range(2 * NU):
                    f, c = divmod(jj, 2)
                    act.wait_ge(sem("uv_done"), jj + 1)
                    dst = (v_t if f < KS else u_t)[:, f % KS, c * HALF:(c + 1) * HALF]
                    act.activation(dst, ps[:, jj % 4, :], ACT.Gelu_apprx_tanh).then_inc(sem("gelu_ready"), 1)
                    for t in v_tiles_after(jj):
                        act.wait_ge(sem("bn_ready"), t + 1)
                        act.activation(std[:, NT + t:NT + t + 1], bnag[:, t, 1:2], ACT.Sqrt, bias=epst[:, :]).then_inc(sem("ln_std_ready"), 1)
                        act.wait_ge(sem("ln_ready"), t + 1)
                        act.activation(st_hi[:, t, :, :], st_f[:, t, :, :], ACT.Copy).then_inc(sem("vn_hi_ready"), 1)
            if "M" in on:
                def s_high(t):
                    act.wait_ge(sem("s_ready"), t + 1)
                    act.activation(st_hi[:, t, :, :], st_f[:, t, :, :], ACT.Copy).then_inc(sem("s_hi_ready"), 1)

                act.wait_ge(sem("sp_tr"), 1)
                act.activation(sp_hi[:, :, :], ps[:, 6:8, :].rearrange("p b (g c) -> p (b g) c", c=P), ACT.Copy).then_inc(sem("sp_hi_ready"), 1)
                s_high(0)
                s_high(1)
                for f in range(KD):
                    for kind in range(2):
                        act.wait_ge(sem("unit_done"), 3 * f + kind + 1)
                        for c in range(2):
                            cs = slice(c * HALF, (c + 1) * HALF)
                            if kind == 1 and f:
                                act.wait_ge(sem("mix_ready"), 2 * f + c - 1)
                            dst = mix[:, f, cs] if kind == 0 else sig_b[c][:, :]
                            act.activation(dst, ps[:, 2 * kind + c, :],
                                           ACT.Sigmoid).then_inc(sem("sig_a_ready" if kind == 0 else "sig_b_ready"), 1)
                        if f == 0:
                            for t in (2, 3, 4, 5) if kind == 0 else (6, 7):
                                s_high(t)
            if "W" in on:
                for k in range(KD):
                    act.wait_ge(sem(f"wo_full{k % 3}"), 16 * (k // 3 + 1))
                    if k == 0:
                        act.wait_ge(sem("unit_done"), NM)
                    act.activation(wo_hi[:, k, :], raw[k % 3][:, :, :].rearrange("p a b -> p (a b)"), ACT.Copy).then_inc(sem("wo_hi_ready"), 1)
                    if k < 2:
                        act.wait_ge(sem("mix_ready"), 2 * KD)
                        act.activation(mt_hi[k][:, :, :], mix[:, :, k * P:(k + 1) * P], ACT.Copy).then_inc(sem("mt_hi_ready"), 1)

                def logits_in(t):
                    act.wait_ge(sem("h2_tr"), t + 1)
                    if t >= 2:
                        act.wait_ge(sem("rt_done"), t - 1)
                    act.activation(h2t[t % 2][:, :, :], ps[:, 4:6, :].rearrange("p b (k c) -> p (b k) c", c=P), ACT.Copy).then_inc(sem("h2t_ready"), 1)

                for t in range(NT):
                    act.wait_ge(sem("x2_ready"), t + 1)
                    if t:
                        act.wait_ge(sem("ssq2_ready"), t)
                    act.activation(junk2[:, :], x2[:, t, :], ACT.Square, accum_out=ssq[:, 8 + t:9 + t]).then_inc(sem("ssq2_ready"), 1)
                    act.wait_ge(sem("ssq2_ready"), t + 1)
                    act.activation(std[:, 8 + t:9 + t], ssq[:, 8 + t:9 + t], ACT.Sqrt, scale=1.0 / D, bias=epst[:, :]).then_inc(sem("std2_ready"), 1)
                    if t + 2 < NT:
                        act.wait_ge(sem("out_done"), t + 1)
                        act.activation(mt_hi[t % 2][:, :, :], mix[:, :, (t + 2) * P:(t + 3) * P], ACT.Copy).then_inc(sem("mt_hi_ready"), 1)
                    logits_in(t)
            if "R" in on:
                act.wait_ge(sem("gmax_ready"), 1)
                act.activation(ex[:, :, :], ex[:, :, :], ACT.Exp).then_inc(sem("gexp_ready"), 1)
                act.wait_ge(sem("ediff_ready"), 1)
                act.activation(gatew[:, 1, :], gatew[:, 1, :], ACT.Exp).then_inc(sem("gexp_ready"), 1)
            if "E" in on:
                def high(g, e, q, full, used, slot):
                    act.wait_ge(sem(f"raw_e_full{g}{q}"), full)
                    wait(act, "group_used", used)
                    act.activation(we_hi[slot][:, :], raw_e[g][q][:, :], ACT.Copy).then_inc(sem("hi_gu" if g < 2 else "hi_dn"), 1)

                def split(g, e, j):
                    full = 16 * (e // 2 + 1) if isinstance(e, int) else 8 * (e - j % 2) + 16
                    high(g, e, j % 2, full, place(g, e) - 3, place(g, j) % 4)

                def rows_high(e, q):
                    act.wait_ge(sem("xs_tr"), e + 1)
                    act.activation(xst_hi[q][:, :, :], ps[:, 0:2, :].rearrange("p b (k c) -> p (b k) c", c=P), ACT.Copy).then_inc(sem("xst_hi_ready"), 1)

                def silu(e, used):
                    act.wait_ge(sem("group_used"), used)
                    wait(act, "hid_ready", e)
                    act.activation(sg[:, :], ps[:, 2, 0:DE], ACT.Silu).then_inc(sem("sg_ready"), 1)

                def hidden_high(e):
                    act.wait_ge(sem("hid_tr"), e + 1)
                    act.activation(hidt_hi[:, :, :].rearrange("p a b -> p (a b)"), ps[:, 4, 0:2 * P], ACT.Copy).then_inc(sem("hidt_hi_ready"), 1)

                def left_half(e, q, used, sent):
                    act.wait_ge(sem("group_used"), used)
                    wait(act, f"y_sent{q}", sent)
                    act.activation(y[q][:, 0:HALF], ps[:, 5, :], ACT.Copy).then_inc(sem("y_left"), 1)

                def expert(e, j, left):
                    silu(e, 3 * e + 2)
                    if left(2):
                        rows_high(e + 2, j % 2)
                    hidden_high(e)
                    if left(2):
                        split(0, e + 2, j + 2)
                    if left(1):
                        split(2, e + 1, j + 1)
                    left_half(e, j % 2, 3 * e + 4 if not (isinstance(e, int) and e == NE - 1) else 3 * NE, 8 * (e - j % 2))
                    if left(2):
                        split(1, e + 2, j + 2)

                act.wait_ge(sem("out_done"), NT)
                act.wait_ge(sem("rt_done"), NT)
                split(0, 0, 0)
                split(1, 0, 0)
                split(0, 1, 1)
                split(2, 0, 0)
                act.wait_ge(sem("tab_read"), 1)
                rows_high(0, 0)
                rows_high(1, 1)
                split(1, 1, 1)
                experts(act, expert)
                n_ovf = act.value_load(ovf_n[0:1, 0:1], min_val=0, max_val=NOVF)
                with act.If(n_ovf > 0):
                    rows_high(NE, 0)
                    with act.Fori(0, n_ovf) as b:
                        for g in range(3):
                            high(g, b + NE, 0, b * 16 + 16 * (NE // 2 + 1), b * 3 + 3 * NE + g - 2, g + 1)
                        silu(b + NE, b * 3 + 3 * NE + 2)
                        rows_high(b + NE + 1, 0)
                        hidden_high(b + NE)
                        left_half(b + NE, 0, b * 3 + 3 * NE + 3, b * 16 + 16 * (NE // 2))
            if "C" in on:
                for t in range(NT):
                    act.wait_ge(sem("acc_ready"), t + 1)
                    if t:
                        act.wait_ge(sem("ssq3_ready"), t)
                    act.activation(junk3[:, :], acc[t % 2][:, :], ACT.Square, accum_out=ssq[:, 16 + t:17 + t]).then_inc(sem("ssq3_ready"), 1)
                    act.wait_ge(sem("ssq3_ready"), t + 1)
                    act.activation(std[:, 16 + t:17 + t], ssq[:, 16 + t:17 + t], ACT.Sqrt, scale=1.0 / D, bias=epst[:, :]).then_inc(sem("std3_ready"), 1)

        @block.vector
        def _(dve):
            steps = [0]

            def link(ins):
                steps[0] += 1
                ins.then_inc(sem("dve_step"), 1)
                dve.wait_ge(sem("dve_step"), steps[0])

            dve.wait_ge(sem("iota_ready"), 2)
            link(dve.tensor_scalar(ident[:, :], iota_row[:, :], iota_col[:, :], None, ALU.is_equal))
            link(dve.tensor_scalar(before[:, :], iota_row[:, :], iota_col[:, :], None, ALU.is_gt))
            link(dve.memset(ones[:, :], 1.0))
            link(dve.memset(ones_b[:, :], 1.0))
            link(dve.memset(epst[:, :], EPS))
            link(dve.memset(mask_l[:, :].bitcast(F32), 0.0))
            link(dve.memset(mask_l[0:1, 0:CHUNK].bitcast(F32), -BIG))
            dve.memset(mask_r[:, :].bitcast(F32), 1.0).then_inc(sem("const_ready"), 1)

            def rope_angles(j):
                fr, ph = cst[:, 3 * j:3 * j + 1], cst[:, 3 * j + 2:3 * j + 3]
                if j:
                    dve.wait_ge(sem("sin_ready"), j)
                link(dve.tensor_copy(turns[:, :], pos_i[:, :]))
                link(dve.tensor_scalar(ang[:, :], turns[:, :], fr, None, ALU.mult))
                link(dve.tensor_scalar(turns[:, :], ang[:, :], 1.0 / TWO_PI, cst[:, 3 * j + 1:3 * j + 2], ALU.mult, ALU.add))
                link(dve.tensor_scalar(turns[:, :], turns[:, :], MAGIC, MAGIC, ALU.add, ALU.subtract))
                for c in (C1, C2, C3):
                    link(dve.scalar_tensor_tensor(ang[:, :], turns[:, :], -c, ang[:, :], ALU.mult, ALU.add))
                link(dve.tensor_scalar(ang[:, :], ang[:, :], ph, PI_IN, ALU.add, ALU.min))
                dve.tensor_scalar(ang[:, :], ang[:, :], -PI_IN, None, ALU.max).then_inc(sem("ang_ready"), 1)

            def ht_low(t):
                dve.wait_ge(sem("ht_hi_ready"), t + 1)
                b = 2 * (t % 2)
                ts = slice(t * P, (t + 1) * P)
                dve.tensor_tensor(ht_lo[:, :, ts], ps[:, b:b + 2, :].rearrange("p b (k c) -> p (b k) c", c=P),
                                  ht_hi[:, :, ts].bitcast(F32), ALU.subtract).then_inc(sem("ht_lo_ready"), 1)

            dve.wait_ge(sem("g_full"), 16)
            for t in range(NT):
                dve.wait_ge(sem("std_ready"), t + 1)
                link(dve.reciprocal(rstd[:, t:t + 1], std[:, t:t + 1]))
                if t >= 2:
                    dve.wait_ge(sem("x_tr"), t - 1)
                dve.scalar_tensor_tensor(hrow[t % 2][:, :], xin[t % 4][:, :], rstd[:, t:t + 1], g_attn[:, :],
                                         ALU.mult, ALU.mult).then_inc(sem("hrow_ready"), 1)
                if t:
                    ht_low(t - 1)
            ht_low(NT - 1)
            if "Z" in on:
                dve.wait_ge(sem("cst_full"), 16)
                dve.wait_ge(sem("pos_full"), 16)
                rope_angles(0)
                rope_angles(1)
                dve.wait_ge(sem("sin_ready"), 2)
                link(dve.tensor_scalar(tab_q[:, :], tab_q[:, :], SCALE, None, ALU.mult))
                for c in range(2):
                    cs = slice(c * HALF, (c + 1) * HALF)
                    dve.wait_ge(sem("z_done"), 3 + c)
                    dve.tensor_tensor(kr1[64:128, cs], ps[64:128, 6 + c, :], tab_k[64:128, cs], ALU.mult).then_inc(sem("kr_half"), 1)
                    dve.tensor_tensor(kr2[64:128, cs], ps[0:64, 6 + c, :], tab_k[0:64, cs], ALU.mult).then_inc(sem("kr_read"), 1)
                dve.wait_ge(sem("kr_half"), 2)
                dve.wait_ge(sem("kr_read"), 2)
                link(dve.tensor_tensor(kr1[64:128, :], kr1[64:128, :], kr2[64:128, :], ALU.add))
                for i in range(2):
                    link(dve.tensor_copy(k_hi[i][64:128, :], kr1[64:128, :]))
                    link(dve.tensor_tensor(k_lo[i][64:128, :], kr1[64:128, :], k_hi[i][64:128, :].bitcast(F32), ALU.subtract))
                dve.wait_ge(sem("gcol_full"), 32)
                dve.wait_ge(sem("c_raw_ready"), 6)
                for i in range(4):
                    dve.wait_ge(sem("c_std_ready"), i + 1)
                    link(dve.reciprocal(c_rs[:, i, :], c_rs[:, i, :]))
                for i in range(6):
                    cs = slice((i % 2) * HALF, (i % 2 + 1) * HALF)
                    u = i // 2
                    dve.scalar_tensor_tensor(c_raw[:, u, cs], c_raw[:, u, cs], gcol[:, u:u + 1],
                                             c_rs[:, (0 if u == 0 else 2) + i % 2, :], ALU.mult, ALU.mult).then_inc(sem("cn_ready"), 1)
                for i in range(6):
                    cs = slice((i % 2) * HALF, (i % 2 + 1) * HALF)
                    u = i // 2
                    dve.wait_ge(sem("c_hi_ready"), i + 1)
                    dve.tensor_tensor(c_lo[:, u, cs], c_raw[:, u, cs], c_hi[:, u, cs].bitcast(F32), ALU.subtract).then_inc(sem("c_lo_ready"), 1)
            if "A" in on:
                def job_read(h, j):
                    dve.wait_ge(sem("job_done"), 5 * h + j + 1)
                    cs = slice((j // 2) * HALF, (j // 2 + 1) * HALF)
                    if j in (0, 2):
                        if h or j:
                            dve.wait_ge(sem("q_lo_ready"), 2 * h + j // 2)
                        dve.tensor_tensor(q_tmp[:, :], ps[:, 7, :], tab_q[:, cs], ALU.mult).then_inc(sem("q_tmp_ready"), 1)
                    elif j < 4:
                        dve.wait_ge(sem("kv_hi_ready"), 3 * h + j // 2 + 1)
                        dve.tensor_tensor(k_lo[h % 2][0:64, cs], ps[0:64, 7, :], k_hi[h % 2][0:64, cs].bitcast(F32), ALU.subtract).then_inc(sem("kv_lo_ready"), 1)
                    else:
                        dve.wait_ge(sem("kv_hi_ready"), 3 * h + 3)
                        dve.tensor_tensor(v_lo[h % 2][:, :, :].rearrange("p t c -> p (t c)"), ps[:, 7, :],
                                          v_hi[h % 2][:, :, :].rearrange("p t c -> p (t c)").bitcast(F32), ALU.subtract).then_inc(sem("kv_lo_ready"), 1)

                def row_max(s):
                    n = (s % NT + 1) * P
                    dve.wait_ge(sem("s_done"), s + 1)
                    b = 2 * (s % 2)
                    dve.tensor_reduce(negm[:, s:s + 1], ps[:, b:b + 2, :].rearrange("p b c -> p (b c)")[:, 0:n], AX, ALU.max,
                                      negate=True).then_inc(sem("max_ready"), 1)

                def diagonal(s):
                    dve.wait_ge(sem("exp_done"), s + 1)
                    dve.reciprocal(rl[:, s:s + 1], lsum[:, s:s + 1]).then_inc(sem("rl_ready"), 1)
                    dve.wait_ge(sem("rl_ready"), s + 1)
                    if s >= 2:
                        dve.wait_ge(sem("pt_done"), chunks_through(s - 2))
                    dve.tensor_scalar(rl_diag[s % 2][:, :], ident[:, :], rl[:, s:s + 1], None, ALU.mult).then_inc(sem("diag_ready"), 1)

                for j in range(5):
                    job_read(0, j)
                row_max(0)
                row_max(1)
                diagonal(0)
                for s in range(NQ):
                    h, i = divmod(s, NT)
                    if s + 1 < NQ:
                        diagonal(s + 1)
                    c0 = chunks_through(s - 1) if s else 0
                    for c in range(i // 4 + 1):
                        w = min(4, i + 1 - 4 * c)
                        cc = c0 + c
                        dve.wait_ge(sem("pt_hi_ready"), cc + 1)
                        dve.tensor_tensor(pt_lo[cc % 4][:, 0:w, :].rearrange("p a b -> p (a b)"), ps[:, 4 + cc % 2, 0:w * P],
                                          pt_hi[cc % 4][:, 0:w, :].rearrange("p a b -> p (a b)").bitcast(F32), ALU.subtract).then_inc(sem("pt_lo_ready"), 1)
                    if s + 2 < NQ:
                        row_max(s + 2)
                    if i < 5 and h + 1 < HEADS:
                        job_read(h + 1, i)
            if "O" in on:
                for k in range(KS):
                    dve.wait_ge(sem("ot_hi_ready"), k + 1)
                    dve.tensor_tensor(ot_lo[:, k, :], o_t[:, k, :], ot_hi[:, k, :].bitcast(F32), ALU.subtract).then_inc(sem("ot_lo_ready"), 1)
            if "U" in on:
                def vn_low(t):
                    dve.wait_ge(sem("vn_hi_ready"), t + 1)
                    dve.tensor_tensor(st_lo[:, t, :, :], st_f[:, t, :, :], st_hi[:, t, :, :].bitcast(F32),
                                      ALU.subtract).then_inc(sem("vn_lo_ready"), 1)

                dve.wait_ge(sem("ln_full"), 32)
                for t in range(NT):
                    bank = ps[:, 4 + t % 2, :]
                    normed = st_f[:, t, :, :].rearrange("p k c -> p (k c)")
                    dve.wait_ge(sem("v_tr"), t + 1)
                    link(dve.bn_stats(bnst[:, t, :], bank))
                    dve.bn_aggr(bnag[:, t, :], bnst[:, t, :]).then_inc(sem("bn_ready"), 1)
                    if t:
                        vn_low(t - 1)
                    dve.wait_ge(sem("ln_std_ready"), t + 1)
                    link(dve.reciprocal(rstd[:, NT + t:NT + t + 1], std[:, NT + t:NT + t + 1]))
                    dve.scalar_tensor_tensor(normed, bank, bnag[:, t, 0:1], ln_g[:, :], ALU.subtract, ALU.mult).then_inc(sem("ln_read"), 1)
                    dve.wait_ge(sem("ln_read"), t + 1)
                    dve.scalar_tensor_tensor(normed, normed, rstd[:, NT + t:NT + t + 1], ln_b[:, :], ALU.mult, ALU.add).then_inc(sem("ln_ready"), 1)
                vn_low(NT - 1)
            if "M" in on:
                dve.wait_ge(sem("spraw_full"), 16)
                dve.memset(sp_raw[0:CHUNK, :, CHUNK:P], 0.0).then_inc(sem("sp_masked"), 1)
                dve.wait_ge(sem("sp_hi_ready"), 1)
                dve.tensor_tensor(sp_lo[:, :, :], ps[:, 6:8, :].rearrange("p b (g c) -> p (b g) c", c=P),
                                  sp_hi[:, :, :].bitcast(F32), ALU.subtract).then_inc(sem("sp_lo_ready"), 1)
                dve.wait_ge(sem("spb_full"), 32)

                def gate_u(t):
                    dve.wait_ge(sem("sp_done"), t + 1)
                    s_f = st_f[:, t, :, :]
                    b = 4 + 2 * (t % 2)
                    src = ps[:, b:b + 2, :].rearrange("p b (q h i) -> p (b q) h i", q=2, h=2)
                    for hh in range(2):
                        r = slice(64 * hh, 64 * hh + 64)
                        dve.tensor_tensor(s_f[r, :, :], src[r, :, hh, :], sp_b[r, :, :], ALU.add).then_inc(sem("s_read"), 1)
                    dve.wait_ge(sem("s_read"), 2 * t + 2)
                    dve.tensor_tensor(s_f, s_f, u_t[:, :, t * P:(t + 1) * P], ALU.mult).then_inc(sem("s_ready"), 1)

                def gate_low(t):
                    dve.wait_ge(sem("s_hi_ready"), t + 1)
                    dve.tensor_tensor(st_lo[:, t, :, :], st_f[:, t, :, :], st_hi[:, t, :, :].bitcast(F32),
                                      ALU.subtract).then_inc(sem("s_lo_ready"), 1)

                dve.wait_ge(sem("gelu_ready"), 2 * NU)
                for t in range(NT):
                    gate_u(t)
                    gate_low(t)
                for f in range(KD):
                    for c in range(2):
                        n = 2 * f + c
                        cs = slice(c * HALF, (c + 1) * HALF)
                        dve.wait_ge(sem("unit_done"), 3 * f + 3)
                        dve.wait_ge(sem("sig_a_ready"), n + 1)
                        dve.tensor_tensor(mix[:, f, cs], ps[:, 4 + c, :], mix[:, f, cs], ALU.mult).then_inc(sem("mix_a_ready"), 1)
                        dve.wait_ge(sem("sig_b_ready"), n + 1)
                        link(dve.tensor_tensor(sig_b[c][:, :], ps[:, 6 + c, :], sig_b[c][:, :], ALU.mult))
                        dve.wait_ge(sem("mix_a_ready"), n + 1)
                        dve.tensor_tensor(mix[:, f, cs], mix[:, f, cs], sig_b[c][:, :], ALU.add).then_inc(sem("mix_ready"), 1)
            if "W" in on:
                def mt_low(t):
                    dve.wait_ge(sem("mt_hi_ready"), t + 1)
                    dve.tensor_tensor(mt_lo[t % 2][:, :, :], mix[:, :, t * P:(t + 1) * P], mt_hi[t % 2][:, :, :].bitcast(F32),
                                      ALU.subtract).then_inc(sem("mt_lo_ready"), 1)

                for k in range(KD):
                    dve.wait_ge(sem("wo_hi_ready"), k + 1)
                    dve.tensor_tensor(wo_lo[:, k, :], raw[k % 3][:, :, :].rearrange("p a b -> p (a b)"),
                                      wo_hi[:, k, :].bitcast(F32), ALU.subtract).then_inc(sem("wo_split"), 1)
                    if k < 2:
                        mt_low(k)
                dve.wait_ge(sem("rt_full"), 128)

                def logits(t):
                    dve.wait_ge(sem("rt_done"), t + 1)
                    dve.tensor_tensor(logit[:, t, :], ps[:, 6, 0:NR], b_rt[:, :], ALU.add).then_inc(sem("logit_ready"), 1)

                for t in range(NT):
                    dve.wait_ge(sem("out_done"), t + 1)
                    dve.wait_ge(sem(f"xre_full{t % 2}"), 16 * (t // 2 + 1))
                    dve.tensor_tensor(x2[:, t, :], ps[:, 2 * (t % 2):2 * (t % 2) + 2, :].rearrange("p b c -> p (b c)"),
                                      xre[t % 2][:, :], ALU.add).then_inc(sem("x2_ready"), 1)
                    dve.wait_ge(sem("std2_ready"), t + 1)
                    link(dve.reciprocal(rstd[:, 8 + t:9 + t], std[:, 8 + t:9 + t]))
                    if t >= 2:
                        dve.wait_ge(sem("h2_tr"), t - 1)
                        dve.wait_ge(sem(f"h2_stored{t % 2}"), 16 * (t // 2))
                    dve.scalar_tensor_tensor(h2[t % 2][:, :], x2[:, t, :], rstd[:, 8 + t:9 + t], g_ffn[:, :],
                                             ALU.mult, ALU.mult).then_inc(sem("h2_ready"), 1)
                    if t + 2 < NT:
                        mt_low(t + 2)
                    if t:
                        logits(t - 1)
                logits(NT - 1)
            if "R" in on:
                lg = logit[:, :, 0:G]
                lx = logit[:, :, G:NR].rearrange("p t (g e) -> p t g e", g=G)
                dve.wait_ge(sem("logit_ready"), NT)

                def wide(ap, n):
                    return ap.unsqueeze(2).to_broadcast([P, NT, n])

                link(dve.tensor_copy(iog[:, :, :], iota_row[:, 0:EPG].unsqueeze(1).to_broadcast([P, NT, EPG])))

                def first_max(src, m, n, onehot):
                    link(dve.tensor_reduce(m, src, AX, ALU.max))
                    link(dve.tensor_tensor(cand[:, :, 0:n], src, wide(m, n), ALU.is_lt))
                    link(dve.scalar_tensor_tensor(cand[:, :, 0:n], cand[:, :, 0:n], 64.0, iog[:, :, 0:n], ALU.mult, ALU.add))
                    link(dve.tensor_reduce(sel[:, :], cand[:, :, 0:n], AX, ALU.min))
                    link(dve.tensor_tensor(onehot, cand[:, :, 0:n], wide(sel[:, :], n), ALU.is_equal))

                first_max(lg, mg[:, :], G, og[:, :, :])
                dve.tensor_tensor(ex[:, :, :], lg, wide(mg[:, :], G), ALU.subtract).then_inc(sem("gmax_ready"), 1)
                dve.wait_ge(sem("gexp_ready"), 1)
                link(dve.tensor_reduce(ptop[:, :], ex[:, :, :], AX, ALU.add))
                link(dve.reciprocal(ptop[:, :], ptop[:, :]))
                og4 = og[:, :, :].unsqueeze(3).to_broadcast([P, NT, G, EPG])
                for t in range(NT):
                    dve.tensor_tensor(lprod[:, t], lx[:, t], og4[:, t], ALU.mult).then_inc(sem("lprod_ready"), 1)
                dve.wait_ge(sem("lprod_ready"), NT)
                link(dve.tensor_tensor(le[:, :, :], lprod[:, :, 0, :], lprod[:, :, 1, :], ALU.add))
                link(dve.tensor_tensor(le[:, :, :], le[:, :, :], lprod[:, :, 2, :], ALU.add))
                dve.tensor_tensor(le[:, :, :], le[:, :, :], lprod[:, :, 3, :], ALU.add).then_inc(sem("logit_read"), 1)
                dve.wait_ge(sem("logit_read"), 1)
                first_max(le[:, :, :], m12[:, 0, :], EPG, oh[0][:, :, :])
                link(dve.scalar_tensor_tensor(le[:, :, :], oh[0][:, :, :], -BIG, le[:, :, :], ALU.mult, ALU.add))
                first_max(le[:, :, :], m12[:, 1, :], EPG, oh[1][:, :, :])
                dve.tensor_tensor(gatew[:, 1, :], m12[:, 1, :], m12[:, 0, :], ALU.subtract).then_inc(sem("ediff_ready"), 1)
                for k in range(2):
                    for t in range(NT):
                        ins = dve.tensor_tensor(oe[k][:, t], oh[k][:, t].unsqueeze(1).to_broadcast([P, G, EPG]), og4[:, t], ALU.mult)
                        ins.then_inc(sem("oeh_ready"), 1)
                dve.wait_ge(sem("oeh_ready"), 2 * NT)
                oef = [oe[k][:, :, :, :].rearrange("p t g e -> p t (g e)") for k in range(2)]
                link(dve.tensor_tensor(oe_b[:, :, :], oef[0], oef[1], ALU.add))
                link(dve.memset(cum_b[:, 0, :], 0.0))
                for t in range(NT):
                    link(dve.tensor_tensor(cum_b[:, t + 1, :], cum_b[:, t, :], oe_b[:, t, :], ALU.add))
                dve.memset(cmp7[:, :], 0.0).then_inc(sem("oe_ready"), 1)
                dve.wait_ge(sem("gexp_ready"), 2)
                link(dve.tensor_scalar(gatew[:, 0, :], gatew[:, 1, :], 1.0, None, ALU.add))
                link(dve.reciprocal(gatew[:, 0, :], gatew[:, 0, :]))
                link(dve.tensor_tensor(gatew[:, 0, :], gatew[:, 0, :], ptop[:, :], ALU.mult))
                link(dve.tensor_tensor(gatew[:, 1, :], gatew[:, 1, :], gatew[:, 0, :], ALU.mult))
                dve.wait_ge(sem("rank_done"), 1)
                link(dve.tensor_copy(rank_e[:, :, :].rearrange("p t e -> p (t e)"), ps[:, 0, 0:NT * NE]))
                link(dve.tensor_copy(cnt[:, :], ps[:, 1, 0:NE]))
                link(dve.tensor_scalar(novf[:, :], cnt[:, :], float(P), None, ALU.is_gt))
                for j in range(2, 8):
                    link(dve.scalar_tensor_tensor(novf[:, :], cnt[:, :], float(P * j), novf[:, :], ALU.is_gt, ALU.add))
                link(dve.tensor_tensor_scan(incl[:, :], ones[:, 0:NE], novf[:, :], 0.0, ALU.mult, ALU.add))
                link(dve.tensor_tensor(ostart[:, :], incl[:, :], novf[:, :], ALU.subtract))
                for k in range(2):
                    for dst, src in ((rk, rank_e[:, :, :]),
                                     (osk, ostart[:, :].unsqueeze(1).to_broadcast([P, NT, NE])),
                                     (eid, iota_row[:, 0:NE].unsqueeze(1).to_broadcast([P, NT, NE]))):
                        link(dve.tensor_tensor(prod[:, :, :], oef[k], src, ALU.mult))
                        link(dve.tensor_reduce(dst[:, k, :], prod[:, :, :], AX, ALU.add))
                link(dve.tensor_scalar(ob[:, :, :], rk[:, :, :], float(P), None, ALU.is_ge))
                link(dve.tensor_copy(obc[:, :, :], ob[:, :, :]))
                for j in range(2, 8):
                    link(dve.scalar_tensor_tensor(ob[:, :, :], rk[:, :, :], float(P * j), ob[:, :, :], ALU.is_ge, ALU.add))
                link(dve.scalar_tensor_tensor(rk[:, :, :], ob[:, :, :], -float(P), rk[:, :, :], ALU.mult, ALU.add))
                link(dve.scalar_tensor_tensor(blk_k[:, :, :], ob[:, :, :], float(NE - 1), osk[:, :, :], ALU.add, ALU.add))
                link(dve.tensor_tensor(blk_k[:, :, :], blk_k[:, :, :], eid[:, :, :], ALU.subtract))
                link(dve.tensor_tensor(blk_k[:, :, :], blk_k[:, :, :], obc[:, :, :], ALU.mult))
                link(dve.tensor_tensor(blk_k[:, :, :], blk_k[:, :, :], eid[:, :, :], ALU.add))
                for k in range(2):
                    link(dve.tensor_scalar(val[:, k, :], iota_row[:, 0:NT], float(P), float(k * T + 1), ALU.mult, ALU.add))
                link(dve.tensor_scalar(val[:, :, :], val[:, :, :], iota_col[:, :], None, ALU.add))
                for i in range(2 * NT):
                    k, t = divmod(i, NT)
                    if i >= 2:
                        dve.wait_ge(sem("sel_used"), i - 1)
                    link(dve.tensor_scalar(sel_a[i % 2][:, :], iota_row[:, :], rk[:, k, t:t + 1], None, ALU.is_equal))
                    dve.tensor_scalar(sel_b[i % 2][:, :], iota_row[:, 0:NBLK], blk_k[:, k, t:t + 1], val[:, k, t:t + 1],
                                      ALU.is_equal, ALU.mult).then_inc(sem("sel_ready"), 1)
                dve.wait_ge(sem("sel_used"), 2 * NT)
                link(dve.tensor_scalar(tab0[:, :], ps[:, 2, 0:NBLK], 0.0, FAR, ALU.is_equal, ALU.mult))
                link(dve.scalar_tensor_tensor(tabf[:, :], ps[:, 2, 0:NBLK], -1.0, tab0[:, :], ALU.add, ALU.add))
                link(dve.tensor_copy(yidx[:, :], tabf[:, :]))
                link(dve.tensor_scalar(tab0[:, :], tabf[:, :], float(T), -float(T), ALU.is_ge, ALU.mult))
                link(dve.tensor_tensor(tabf[:, :], tabf[:, :], tab0[:, :], ALU.add))
                link(dve.tensor_copy(xidx[:, :], tabf[:, :]))
                link(dve.tensor_copy(ovf_n[0:1, 0:1], incl[0:1, NE - 1:NE]))
                link(dve.tensor_tensor(ovc[0:1, :, :], incl[0:1, :].unsqueeze(1).to_broadcast([1, 16, NE]),
                                       iota_row[0:1, 0:16].unsqueeze(2).to_broadcast([1, 16, NE]), ALU.is_le))
                link(dve.tensor_reduce(ovf[0:1, :], ovc[0:1, :, :], AX, ALU.add))
                link(dve.tensor_scalar(ovf[0:1, :], ovf[0:1, :], float(NE - 1), None, ALU.min))
                dve.tensor_copy(ovf_e[0:1, :], ovf[0:1, :]).then_inc(sem("tab_read"), 1)
            if "E" in on:
                def low(g, e, q, slot):
                    dve.wait_ge(sem("hi_gu"), 2 * e + g + 1)
                    dve.tensor_tensor(we_lo[slot][:, :], raw_e[g][q][:, :], we_hi[slot][:, :].bitcast(F32), ALU.subtract).then_inc(sem("lo_gu"), 1)

                def rows_low(e, q):
                    dve.wait_ge(sem("xst_hi_ready"), e + 1)
                    dve.tensor_tensor(xst_lo[q][:, :, :], ps[:, 0:2, :].rearrange("p b (k c) -> p (b k) c", c=P),
                                      xst_hi[q][:, :, :].bitcast(F32), ALU.subtract).then_inc(sem("xst_ready"), 1)

                def hidden(e):
                    dve.wait_ge(sem("sg_ready"), e + 1)
                    wait(dve, "hid_tr", e)
                    dve.tensor_tensor(hid[:, :], ps[:, 3, 0:DE], sg[:, :], ALU.mult).then_inc(sem("hid_ready"), 1)

                def hidden_low(e):
                    dve.wait_ge(sem("hidt_hi_ready"), e + 1)
                    dve.tensor_tensor(hidt_lo[:, :, :].rearrange("p a b -> p (a b)"), ps[:, 4, 0:2 * P],
                                      hidt_hi[:, :, :].rearrange("p a b -> p (a b)").bitcast(F32), ALU.subtract).then_inc(sem("hidt_ready"), 1)

                def right_half(e, q, used, sent):
                    dve.wait_ge(sem("group_used"), used)
                    wait(dve, f"y_sent{q}", sent)
                    dve.tensor_copy(y[q][:, HALF:D], ps[:, 6, :]).then_inc(sem("y_right"), 1)

                def expert(e, j, left):
                    hidden(e)
                    if left(2):
                        rows_low(e + 2, j % 2)
                    hidden_low(e)
                    if left(2):
                        low(0, e + 2, j % 2, place(0, j + 2) % 4)
                    right_half(e, j % 2, 3 * e + 4 if not (isinstance(e, int) and e == NE - 1) else 3 * NE, 8 * (e - j % 2))
                    if left(2):
                        low(1, e + 2, j % 2, place(1, j + 2) % 4)

                low(0, 0, 0, 0)
                low(1, 0, 0, 1)
                low(0, 1, 1, 2)
                rows_low(0, 0)
                rows_low(1, 1)
                low(1, 1, 1, 0)
                experts(dve, expert)
                n_ovf = dve.value_load(ovf_n[0:1, 0:1], min_val=0, max_val=NOVF)
                with dve.If(n_ovf > 0):
                    rows_low(NE, 0)
                    with dve.Fori(0, n_ovf) as b:
                        for g in range(2):
                            low(g, b + NE, 0, g + 1)
                        hidden(b + NE)
                        rows_low(b + NE + 1, 0)
                        hidden_low(b + NE)
                        right_half(b + NE, 0, b * 3 + 3 * NE + 3, b * 16 + 16 * (NE // 2))
            if "C" in on:
                dve.wait_ge(sem("gfin_full"), 16)
                def combine(t):
                    dve.wait_ge(sem(f"yin_full{t % 4}"), 32 * (t // 4 + 1))
                    if t >= 2:
                        dve.wait_ge(sem("res_ready"), t - 1)
                        dve.wait_ge(sem("ssq3_ready"), t - 1)
                    link(dve.scalar_tensor_tensor(acc[t % 2][:, :], yin[t][:, 0, :], gatew[:, 0, t:t + 1], x2[:, t, :], ALU.mult, ALU.add))
                    dve.scalar_tensor_tensor(acc[t % 2][:, :], yin[t][:, 1, :], gatew[:, 1, t:t + 1], acc[t % 2][:, :],
                                             ALU.mult, ALU.add).then_inc(sem("acc_ready"), 1)

                combine(0)
                for t in range(NT):
                    if t + 1 < NT:
                        combine(t + 1)
                    dve.wait_ge(sem("std3_ready"), t + 1)
                    link(dve.reciprocal(rstd[:, 16 + t:17 + t], std[:, 16 + t:17 + t]))
                    dve.scalar_tensor_tensor(res[t][:, :], acc[t % 2][:, :], rstd[:, 16 + t:17 + t], g_fin[:, :],
                                             ALU.mult, ALU.mult).then_inc(sem("res_ready"), 1)

        @block.gpsimd
        def _(pool):
            pool.iota(iota_row[:, :], [[1, P]], base=0, channel_multiplier=0,
                      allow_small_or_imprecise_dtypes=True).then_inc(sem("iota_ready"), 1)
            pool.iota(iota_col[:, :], [[0, 1]], base=0, channel_multiplier=1,
                      allow_small_or_imprecise_dtypes=True).then_inc(sem("iota_ready"), 1)
            if "Z" in on:
                split_units(pool, 0, NZ)
            if "A" in on:
                def head_split(h):
                    pool.wait_ge(sem("hraw_full"), 80 * (h + 1))
                    if h >= 2:
                        pool.wait_ge(sem("job_done"), 5 * (h - 1))
                    pool.tensor_copy(h_hi[h % 2][:, :], h_raw[:, :]).then_inc(sem("hw_hi"), 1)
                    pool.wait_ge(sem("hw_hi"), h + 1)
                    pool.tensor_tensor(h_lo[h % 2][:, :], h_raw[:, :], h_hi[h % 2][:, :].bitcast(F32),
                                       ALU.subtract).then_inc(sem("hw_split"), 1)

                head_split(0)
                for h in range(HEADS):
                    for j in range(2):
                        pool.wait_ge(sem("q_hi_ready"), 2 * h + j + 1)
                        pool.tensor_tensor(q_lo[h % 2][:, j * HALF:(j + 1) * HALF], q_tmp[:, :],
                                           q_hi[h % 2][:, j * HALF:(j + 1) * HALF].bitcast(F32), ALU.subtract).then_inc(sem("q_lo_ready"), 1)
                    if h + 1 < HEADS:
                        head_split(h + 1)
                    if h == 1 and "U" in on:
                        split_units(pool, NZ, NZ + 1)
            if "U" in on:
                pool.wait_ge(sem("pv_done"), NQ)
                split_units(pool, NZ + 1, NZ + NU)
            if "M" in on:
                split_units(pool, NZ + NU, NZ + NU + NM)
            if "E" in on:
                x_copies, y_copies = pool.alloc_register("x_copies"), pool.alloc_register("y_copies")
                pool.reg_mov(x_copies, 0)
                pool.reg_mov(y_copies, 0)
                last_token, last_row = pool.to_reg(T - 1), pool.to_reg(2 * T - 1)

                def gather(blk, j):
                    pool.tensor_copy(xcol[j][:, :], xidx[:, blk]).then_inc(sem("xcol_ready"), 1)
                    pool.reg_add(x_copies, x_copies, 1)
                    pool.wait_ge(sem("tab_read"), 1)
                    pool.wait_ge(sem("xcol_ready"), x_copies)
                    pool.indirect_dma_start(xs[j][:, :], None, h2_dram, bass.IndirectOffsetOnAxis(xcol[j][:, :], 0),
                                            bounds_check=last_token, oob_is_err=False).then_inc(sem(f"xs_full{j}"), 16)

                def scatter(blk, j, sent):
                    wait(pool, f"y_sent{j}", sent)
                    pool.tensor_copy(ycol[j][:, :], yidx[:, blk]).then_inc(sem("ycol_ready"), 1)
                    pool.reg_add(y_copies, y_copies, 1)
                    pool.wait_ge(sem("tab_read"), 1)
                    pool.wait_ge(sem("ycol_ready"), y_copies)
                    pool.indirect_dma_start(y_dram, bass.IndirectOffsetOnAxis(ycol[j][:, :], 0), y[j][:, :], None,
                                            bounds_check=last_row, oob_is_err=False).then_inc(sem(f"y_sent{j}"), 16)

                def down_low(e, q, slot):
                    pool.wait_ge(sem("hi_dn"), e + 1)
                    pool.tensor_tensor(we_lo[slot][:, :], raw_e[2][q][:, :], we_hi[slot][:, :].bitcast(F32), ALU.subtract).then_inc(sem("lo_dn"), 1)

                def expert(e, j, left):
                    if left(4):
                        pool.wait_ge(sem("xs_tr"), e + 1)
                        gather(slice(e + 4, e + 5) if isinstance(e, int) else bass.ds(e + 4, 1), j)
                    if left(1):
                        down_low(e + 1, (j + 1) % 2, place(2, j + 1) % 4)
                    pool.wait_ge(sem("y_left"), e + 1)
                    pool.wait_ge(sem("y_right"), e + 1)
                    scatter(slice(e, e + 1) if isinstance(e, int) else bass.ds(e, 1), j % 2, 8 * (e - j % 2))

                pool.wait_ge(sem("out_done"), NT)
                pool.wait_ge(sem("x2_ready"), NT)
                for j in range(4):
                    pool.memset(xs[j][:, :], 0.0).then_inc(sem("xs_clear"), 1)
                pool.wait_ge(sem("xs_clear"), 4)
                for i in range(2):
                    pool.wait_ge(sem(f"h2_stored{i}"), 16 * NT // 2)
                down_low(0, 0, place(2, 0) % 4)
                pool.wait_ge(sem("tab_read"), 1)
                for j in range(4):
                    gather(slice(j, j + 1), j)
                experts(pool, expert)
                n_ovf = pool.value_load(ovf_n[0:1, 0:1], min_val=0, max_val=NOVF)
                with pool.If(n_ovf > 0):
                    pool.wait_ge(sem("xs_tr"), NE - 3)
                    gather(slice(NE, NE + 1), 0)
                    with pool.Fori(0, n_ovf) as b:
                        down_low(b + NE, 0, 3)
                        pool.wait_ge(sem("xs_tr"), b + NE + 1)
                        gather(bass.ds(b + NE + 1, 1), 0)
                        pool.wait_ge(sem("y_left"), b + NE + 1)
                        pool.wait_ge(sem("y_right"), b + NE + 1)
                        scatter(bass.ds(b + NE, 1), 0, b * 16 + 16 * (NE // 2))
                    pool.wait_ge(sem("y_sent0"), n_ovf * 16 + 16 * (NE // 2))
                pool.wait_ge(sem("y_sent0"), 16 * (NE // 2))
                pool.wait_ge(sem("y_sent1"), 16 * (NE // 2))
                pool.memset(junk3[:, 0:1], 0.0).then_inc(sem("y_stored_all"), 1)


_INS = ["x", "positions", "g_attn_norm", "w_in", "g_cq", "w_uq", "g_ckv", "w_uk", "w_uv", "w_o_attn", "sgu_gain",
        "sgu_bias", "w_spatial", "b_spatial", "w_o_sgu", "w_out", "g_ffn_norm", "w_router_group", "b_router_group",
        "w_router_expert", "b_router_expert", "w_exp_gate", "w_exp_up", "w_exp_down", "g_final"]


def kernel(**inputs):
    import numpy as _np
    import concourse.bacc as _bacc
    from concourse import mybir as _mybir
    from concourse.bass_utils import run_bass_kernel_spmd as _run

    nc = _bacc.Bacc("TRN2", target_bir_lowering=False, num_devices=1)
    arrays, args = {}, {}
    for name in _INS:
        arr = _np.ascontiguousarray(inputs[name])
        arrays[f"in_{name}_dram"] = arr
        args[name] = nc.dram_tensor(f"in_{name}_dram", arr.shape, _mybir.dt.from_np(arr.dtype), kind="ExternalInput").ap()
    c = rope_constants()
    arrays["rope_constants_dram"] = c
    args["rope_constants"] = nc.dram_tensor("rope_constants_dram", c.shape, _mybir.dt.float32, kind="ExternalInput").ap()
    out = nc.dram_tensor("out_0_dram", (1, T, D), _mybir.dt.float32, kind="ExternalOutput").ap()
    build(nc, args, out)
    r = _run(nc, [arrays], core_ids=[0])
    return r.results[0]["out_0_dram"]
```
